# Optimizing a Trainium2 kernel written in Bass

```python
import jax, jax.numpy as jnp
from jax import lax
import numpy as np

D_MODEL = 2048
BATCH = 1
SEQ = 256
DEPTH = 2

N_MIXERS = 2
N_POOL_LAYERS = (DEPTH + 1) // 2
N_ATTN_LAYERS = DEPTH // 2
EPS = 1e-6

POOL_WINDOWS = (2, 4, 8, 16)
N_POOL_GROUPS = 4
POOL_GROUP_DIM = D_MODEL // N_POOL_GROUPS
POOL_IN = 2 * D_MODEL

N_HEADS = 16
HEAD_DIM = D_MODEL // N_HEADS
ATTN_WIDTH = N_HEADS * HEAD_DIM
ROT_DIM = HEAD_DIM // 4
IDX_HEADS = 16
IDX_DIM = 64
IDX_ROT = IDX_DIM // 4
ROPE_THETA = 500000.0
TOP_K_MAX = 256
Q_BLOCK = 128
ATTN_SPLITS = (ATTN_WIDTH, 2 * ATTN_WIDTH, 3 * ATTN_WIDTH, 4 * ATTN_WIDTH,
               4 * ATTN_WIDTH + IDX_HEADS * IDX_DIM,
               4 * ATTN_WIDTH + IDX_HEADS * IDX_DIM + IDX_DIM)
ATTN_IN = 4 * ATTN_WIDTH + IDX_HEADS * IDX_DIM + IDX_DIM + IDX_HEADS


def rms_norm(x, g):
    xf = x.astype(jnp.float32)
    y = xf * lax.rsqrt(jnp.mean(xf * xf, axis=-1, keepdims=True) + EPS)
    return (y * g.astype(jnp.float32)).astype(x.dtype)

def rope_partial(x, positions, rot_dim):
    half = rot_dim // 2
    inv_freq = ROPE_THETA ** (-jnp.arange(half, dtype=jnp.float32) * 2.0 / rot_dim)
    ang = positions.astype(jnp.float32)[..., None] * inv_freq
    cos = jnp.cos(ang)[:, :, None, :]
    sin = jnp.sin(ang)[:, :, None, :]
    xf = x.astype(jnp.float32)
    x1, x2, rest = xf[..., :half], xf[..., half:rot_dim], xf[..., rot_dim:]
    out = jnp.concatenate([x1 * cos - x2 * sin, x2 * cos + x1 * sin, rest], axis=-1)
    return out.astype(x.dtype)

def pool_branch(h, w_in, w_grp, layer_scale, w_out):
    B, L, D = h.shape
    v, gate = jnp.split(h @ w_in, 2, axis=-1)
    vf = v.astype(jnp.float32)
    cs = jnp.concatenate([jnp.zeros((B, 1, D), jnp.float32),
                          jnp.cumsum(vf, axis=1)], axis=1)
    t = jnp.arange(L, dtype=jnp.int32)
    outs = []
    for gi, w in enumerate(POOL_WINDOWS):
        sl = slice(gi * POOL_GROUP_DIM, (gi + 1) * POOL_GROUP_DIM)
        lo = jnp.maximum(t + 1 - w, 0)
        window_sum = cs[:, t + 1, sl] - cs[:, lo, sl]
        count = jnp.minimum(t + 1, w).astype(jnp.float32)[None, :, None]
        pooled = (window_sum / count - vf[:, :, sl]).astype(h.dtype)
        outs.append(jnp.einsum('bsc,cd->bsd', pooled, w_grp[gi]))
    mixed = jnp.concatenate(outs, axis=-1) * layer_scale
    return (mixed * jax.nn.silu(gate)) @ w_out

def dsa_branch(h, positions, w_in, w_out):
    B, L, _ = h.shape
    proj = h @ w_in
    q, k, v, gate, qi, ki, wi = jnp.split(proj, ATTN_SPLITS, axis=-1)
    q = rope_partial(q.reshape(B, L, N_HEADS, HEAD_DIM), positions, ROT_DIM)
    k = rope_partial(k.reshape(B, L, N_HEADS, HEAD_DIM), positions, ROT_DIM)
    v = v.reshape(B, L, N_HEADS, HEAD_DIM)
    qi = rope_partial(qi.reshape(B, L, IDX_HEADS, IDX_DIM), positions, IDX_ROT)
    ki = rope_partial(ki.reshape(B, L, 1, IDX_DIM), positions, IDX_ROT)[:, :, 0]
    ki_f = ki.astype(jnp.float32)
    top_k = min(TOP_K_MAX, L // 4)
    nb = L // Q_BLOCK
    key_idx = jnp.arange(L, dtype=jnp.int32)
    idx_scale = (IDX_HEADS ** -0.5) * (IDX_DIM ** -0.5)
    attn_scale = HEAD_DIM ** -0.5

    def to_blocks(a):
        return jnp.moveaxis(a.reshape(B, nb, Q_BLOCK, *a.shape[2:]), 1, 0)

    def block_fn(args):
        qb, qib, wb, tb = args
        s = jnp.einsum('bqhd,bsd->bqhs', qib.astype(jnp.float32), ki_f)
        score = jnp.einsum('bqhs,bqh->bqs', jax.nn.relu(s),
                           wb.astype(jnp.float32)) * idx_scale
        admissible = key_idx[None, None, :] <= tb[None, :, None]
        score = jnp.where(admissible, score, -jnp.inf)
        _, sel = lax.top_k(score, top_k)
        valid = sel <= tb[None, :, None]
        k_sel = jax.vmap(lambda kk, ii: kk[ii])(k, sel)
        v_sel = jax.vmap(lambda vv, ii: vv[ii])(v, sel)
        logits = jnp.einsum('bqhd,bqkhd->bhqk', qb, k_sel).astype(jnp.float32) * attn_scale
        logits = jnp.where(valid[:, None], logits, -jnp.inf)
        p = jax.nn.softmax(logits, axis=-1).astype(v.dtype)
        return jnp.einsum('bhqk,bqkhd->bqhd', p, v_sel)

    t_blocks = key_idx.reshape(nb, Q_BLOCK)
    outs = lax.map(block_fn, (to_blocks(q), to_blocks(qi), to_blocks(wi), t_blocks))
    o = jnp.moveaxis(outs, 0, 1).reshape(B, L, ATTN_WIDTH)
    return (o * jax.nn.silu(gate)) @ w_out

def first_inputs(seed: int = 0) -> dict:
    key = jax.random.key(seed)
    ks = jax.random.split(key, 13)
    D = D_MODEL
    x = jax.random.normal(ks[0], (BATCH, SEQ, D), jnp.float32)
    c = jax.random.normal(ks[1], (BATCH, D), jnp.float32)
    positions = jnp.broadcast_to(jnp.arange(SEQ, dtype=jnp.int32)[None, :], (BATCH, SEQ))
    norm_g = 1.0 + 0.02 * jax.random.normal(ks[2], (DEPTH, D), jnp.float32)
    mod_w = 0.5 * D ** -0.5 * jax.random.normal(ks[3], (DEPTH, D, 3 * D), jnp.float32)
    mod_b = 0.02 * jax.random.normal(ks[4], (DEPTH, 3 * D), jnp.float32)
    pool_w_in = D ** -0.5 * jax.random.normal(ks[5], (N_POOL_LAYERS, D, POOL_IN), jnp.float32)
    pool_w_grp = POOL_GROUP_DIM ** -0.5 * jax.random.normal(
        ks[6], (N_POOL_LAYERS, N_POOL_GROUPS, POOL_GROUP_DIM, POOL_GROUP_DIM), jnp.float32)
    pool_scale = 1.0 + 0.1 * jax.random.normal(ks[7], (N_POOL_LAYERS, D), jnp.float32)
    pool_w_out = D ** -0.5 * jax.random.normal(ks[8], (N_POOL_LAYERS, D, D), jnp.float32)
    attn_w_in = D ** -0.5 * jax.random.normal(ks[9], (N_ATTN_LAYERS, D, ATTN_IN), jnp.float32)
    attn_w_out = ATTN_WIDTH ** -0.5 * jax.random.normal(
        ks[10], (N_ATTN_LAYERS, ATTN_WIDTH, D), jnp.float32)
    final_g = 1.0 + 0.02 * jax.random.normal(ks[11], (D,), jnp.float32)
    return {"x": x, "c": c, "positions": positions, "norm_g": norm_g,
            "mod_w": mod_w, "mod_b": mod_b, "pool_w_in": pool_w_in,
            "pool_w_grp": pool_w_grp, "pool_scale": pool_scale,
            "pool_w_out": pool_w_out, "attn_w_in": attn_w_in,
            "attn_w_out": attn_w_out, "final_g": final_g}

def first_block(x, c, positions, norm_g, mod_w, mod_b, pool_w_in, pool_w_grp,
              pool_scale, pool_w_out, attn_w_in, attn_w_out, final_g):
    cond = jax.nn.silu(c)
    for i in range(DEPTH):
        mod = cond @ mod_w[i] + mod_b[i]
        shift, scale, gate = jnp.split(mod, 3, axis=-1)
        h = rms_norm(x, norm_g[i]) * (1.0 + scale[:, None, :]) + shift[:, None, :]
        j = i // N_MIXERS
        if i % N_MIXERS == 0:
            out = pool_branch(h, pool_w_in[j], pool_w_grp[j], pool_scale[j], pool_w_out[j])
        else:
            out = dsa_branch(h, positions, attn_w_in[j], attn_w_out[j])
        x = x + gate[:, None, :] * out
    return rms_norm(x, final_g)


DEPTH_2 = 1

M_HEADS = 4
M_HEAD_DIM = 256
M_WIDTH = M_HEADS * M_HEAD_DIM
M_CHUNK = 128
CONV_WIDTH = 4
A_HEADS = 8
A_HEAD_DIM = 128
A_WIDTH = A_HEADS * A_HEAD_DIM
MOBA_BLOCK = 256
MOBA_TOPK = 3
ROPE_THETA_2 = 10000.0
D_FF = 4 * D_MODEL
NORM_EPS = 1e-6

SPLITS = (M_WIDTH, M_WIDTH, M_WIDTH, M_WIDTH, M_HEADS, M_HEADS,
          A_WIDTH, A_WIDTH, A_WIDTH, D_MODEL, D_MODEL)
IN_COLS = 4 * M_WIDTH + 2 * M_HEADS + 3 * A_WIDTH + 2 * D_MODEL


def rmsnorm(x, w):
    xf = x.astype(jnp.float32)
    y = xf * lax.rsqrt(jnp.mean(xf * xf, axis=-1, keepdims=True) + NORM_EPS)
    return (y * w.astype(jnp.float32)).astype(x.dtype)

def split_cols(u):
    outs, start = [], 0
    for width in SPLITS:
        outs.append(u[..., start:start + width])
        start += width
    return outs

def to_heads(u, n_heads):
    B, S, C = u.shape
    return u.reshape(B, S, n_heads, C // n_heads).transpose(0, 2, 1, 3)

def causal_depthwise_conv(u, w, b):
    S = u.shape[1]
    up = jnp.pad(u, ((0, 0), (CONV_WIDTH - 1, 0), (0, 0)))
    out = b
    for j in range(CONV_WIDTH):
        out = out + w[j] * up[:, j:j + S]
    return out

def apply_rope(x, positions):
    D = x.shape[-1]
    inv_freq = 1.0 / (ROPE_THETA_2 ** (jnp.arange(0, D, 2, dtype=jnp.float32) / D))
    ang = positions.astype(jnp.float32)[..., None] * inv_freq
    ang = jnp.concatenate([ang, ang], axis=-1)[:, None]
    xf = x.astype(jnp.float32)
    x1, x2 = xf[..., :D // 2], xf[..., D // 2:]
    rot = jnp.concatenate([-x2, x1], axis=-1)
    return (xf * jnp.cos(ang) + rot * jnp.sin(ang)).astype(x.dtype)

def mlstm_chunkwise(q, k, v, i_pre, f_pre):
    B, H, S, D = q.shape
    L = M_CHUNK
    NC = S // L
    f32 = jnp.float32
    q = q.astype(f32).reshape(B, H, NC, L, D)
    k = (k.astype(f32) * (D ** -0.5)).reshape(B, H, NC, L, D)
    v = v.astype(f32).reshape(B, H, NC, L, D)
    log_f = jax.nn.log_sigmoid(f_pre.astype(f32)).reshape(B, H, NC, L)
    log_i = i_pre.astype(f32).reshape(B, H, NC, L)
    b = jnp.cumsum(log_f, axis=-1)
    F = b[..., -1]

    w = F[..., None] - b + log_i
    m_loc = jnp.max(w, axis=-1)
    e = jnp.exp(w - m_loc[..., None])
    C_loc = jnp.einsum('bhclv,bhclk->bhcvk', v * e[..., None], k)
    n_loc = jnp.einsum('bhcl,bhclk->bhck', e, k)

    def step(carry, xs):
        C, n, m = carry
        Fc, Cl, nl, ml = xs
        m_new = jnp.maximum(Fc + m, ml)
        a = jnp.exp(Fc + m - m_new)
        g = jnp.exp(ml - m_new)
        C_new = a[..., None, None] * C + g[..., None, None] * Cl
        n_new = a[..., None] * n + g[..., None] * nl
        return (C_new, n_new, m_new), (C, n, m)

    init = (jnp.zeros((B, H, D, D), f32), jnp.zeros((B, H, D), f32), jnp.zeros((B, H), f32))
    xs = (jnp.moveaxis(F, 2, 0), jnp.moveaxis(C_loc, 2, 0),
          jnp.moveaxis(n_loc, 2, 0), jnp.moveaxis(m_loc, 2, 0))
    _, (C_prev, n_prev, m_prev) = lax.scan(step, init, xs)
    C_prev = jnp.moveaxis(C_prev, 0, 2)
    n_prev = jnp.moveaxis(n_prev, 0, 2)
    m_prev = jnp.moveaxis(m_prev, 0, 2)

    a_log = b + m_prev[..., None]
    d_log = b[..., :, None] - b[..., None, :] + log_i[..., None, :]
    causal = jnp.tril(jnp.ones((L, L), dtype=bool))
    d_log = jnp.where(causal, d_log, -jnp.inf)
    m_t = jnp.maximum(a_log, jnp.max(d_log, axis=-1))
    s_ts = jnp.einsum('bhctd,bhcsd->bhcts', q, k) * jnp.exp(d_log - m_t[..., None])
    inter = jnp.exp(a_log - m_t)
    num = (inter[..., None] * jnp.einsum('bhcvk,bhctk->bhctv', C_prev, q)
           + jnp.einsum('bhcts,bhcsv->bhctv', s_ts, v))
    den = inter * jnp.einsum('bhck,bhctk->bhct', n_prev, q) + jnp.sum(s_ts, axis=-1)
    h = num / jnp.maximum(jnp.abs(den), jnp.exp(-m_t))[..., None]
    return h.reshape(B, H, S, D)

def moba_attention(q, k, v):
    B, H, S, D = q.shape
    BS = MOBA_BLOCK
    NB = -(-S // BS)
    K_SEL = min(MOBA_TOPK, NB)
    pad = NB * BS - S
    kp = jnp.pad(k, ((0, 0), (0, 0), (0, pad), (0, 0))).reshape(B, H, NB, BS, D)
    vp = jnp.pad(v, ((0, 0), (0, 0), (0, pad), (0, 0))).reshape(B, H, NB, BS, D)
    k_mean = jnp.mean(kp.astype(jnp.float32), axis=3)
    scale = D ** -0.5
    NQB = S // Q_BLOCK
    blk_ids = jnp.arange(NB)
    b_idx = jnp.arange(B)[:, None, None, None]
    h_idx = jnp.arange(H)[None, :, None, None]
    n_sel = K_SEL * BS

    def one_block(qb):
        start = qb * Q_BLOCK
        qf = lax.dynamic_slice_in_dim(q, start, Q_BLOCK, axis=2).astype(jnp.float32)
        own = start // BS
        gate = jnp.einsum('bhqd,bhnd->bhqn', qf, k_mean)
        gate = jnp.where(blk_ids < own, gate, -jnp.inf)
        _, sel = lax.top_k(gate, K_SEL)
        valid = jnp.arange(K_SEL) < own
        k_sel = kp[b_idx, h_idx, sel].astype(jnp.float32)
        v_sel = vp[b_idx, h_idx, sel].astype(jnp.float32)
        s_sel = jnp.einsum('bhqd,bhqnkd->bhqnk', qf, k_sel) * scale
        s_sel = jnp.where(valid[:, None], s_sel, -jnp.inf).reshape(B, H, Q_BLOCK, n_sel)
        k_own = lax.dynamic_index_in_dim(kp, own, axis=2, keepdims=False).astype(jnp.float32)
        v_own = lax.dynamic_index_in_dim(vp, own, axis=2, keepdims=False).astype(jnp.float32)
        s_own = jnp.einsum('bhqd,bhkd->bhqk', qf, k_own) * scale
        q_pos = start + jnp.arange(Q_BLOCK)
        k_pos = own * BS + jnp.arange(BS)
        s_own = jnp.where(k_pos[None, :] <= q_pos[:, None], s_own, -jnp.inf)
        p = jax.nn.softmax(jnp.concatenate([s_sel, s_own], axis=-1), axis=-1)
        o = (jnp.einsum('bhqm,bhqmd->bhqd', p[..., :n_sel],
                        v_sel.reshape(B, H, Q_BLOCK, n_sel, D))
             + jnp.einsum('bhqk,bhkd->bhqd', p[..., n_sel:], v_own))
        return o.astype(q.dtype)

    out = lax.map(one_block, jnp.arange(NQB))
    return jnp.moveaxis(out, 0, 2).reshape(B, H, S, D)

def second_inputs(seed: int = 0) -> dict:
    key = jax.random.key(seed)
    ks = jax.random.split(key, 16)
    f32 = jnp.float32

    def gain(k, n):
        return 1.0 + 0.05 * jax.random.normal(k, (DEPTH_2, n), f32)

    def dense(k, fan_in, fan_out):
        return jax.random.normal(k, (DEPTH_2, fan_in, fan_out), f32) * (fan_in ** -0.5)

    x = jax.random.normal(ks[0], (BATCH, SEQ, D_MODEL), f32)
    positions = jnp.broadcast_to(jnp.arange(SEQ, dtype=jnp.int32), (BATCH, SEQ))
    f_bias = (jnp.linspace(3.0, 6.0, M_HEADS, dtype=f32)[None, :]
              + 0.1 * jax.random.normal(ks[6], (DEPTH_2, M_HEADS), f32))
    return {
        'x': x,
        'positions': positions,
        'norm_mix_pre': gain(ks[1], D_MODEL),
        'w_in': dense(ks[2], D_MODEL, IN_COLS),
        'conv_w': jax.random.normal(ks[3], (DEPTH_2, CONV_WIDTH, 2 * M_WIDTH), f32) * (CONV_WIDTH ** -0.5),
        'conv_b': 0.01 * jax.random.normal(ks[4], (DEPTH_2, 2 * M_WIDTH), f32),
        'i_bias': 0.1 * jax.random.normal(ks[5], (DEPTH_2, M_HEADS), f32),
        'f_bias': f_bias,
        'mlstm_norm': gain(ks[7], M_WIDTH),
        'w_branch_m': dense(ks[8], M_WIDTH, D_MODEL),
        'w_branch_a': dense(ks[9], A_WIDTH, D_MODEL),
        'w_out': dense(ks[10], D_MODEL, D_MODEL),
        'norm_mix_post': gain(ks[11], D_MODEL),
        'norm_ffn_pre': gain(ks[12], D_MODEL),
        'w_up': dense(ks[13], D_MODEL, D_FF),
        'w_down': dense(ks[14], D_FF, D_MODEL),
        'norm_ffn_post': gain(ks[15], D_MODEL),
    }

def second_block(x, positions, norm_mix_pre, w_in, conv_w, conv_b, i_bias, f_bias, mlstm_norm,
              w_branch_m, w_branch_a, w_out, norm_mix_post, norm_ffn_pre, w_up, w_down,
              norm_ffn_post):
    dt = x.dtype
    B, S, _ = x.shape
    for l in range(DEPTH_2):
        xn = rmsnorm(x, norm_mix_pre[l])
        proj = jnp.einsum('bsd,dc->bsc', xn, w_in[l])
        mq, mk, mv, mo, mi, mf, aq, ak, av, g_m, g_a = split_cols(proj)

        qk = jax.nn.silu(causal_depthwise_conv(jnp.concatenate([mq, mk], axis=-1),
                                               conv_w[l], conv_b[l]))
        mq_h = to_heads(qk[..., :M_WIDTH], M_HEADS)
        mk_h = to_heads(qk[..., M_WIDTH:], M_HEADS)
        mv_h = to_heads(mv, M_HEADS)
        i_pre = jnp.transpose(mi + i_bias[l], (0, 2, 1))
        f_pre = jnp.transpose(mf + f_bias[l], (0, 2, 1))
        h = mlstm_chunkwise(mq_h, mk_h, mv_h, i_pre, f_pre)
        h = h * lax.rsqrt(jnp.mean(h * h, axis=-1, keepdims=True) + NORM_EPS)
        h = h.transpose(0, 2, 1, 3).reshape(B, S, M_WIDTH) * mlstm_norm[l].astype(jnp.float32)
        h_m = (h * jax.nn.sigmoid(mo.astype(jnp.float32))).astype(dt)

        aq_h = apply_rope(to_heads(aq, A_HEADS), positions)
        ak_h = apply_rope(to_heads(ak, A_HEADS), positions)
        av_h = to_heads(av, A_HEADS)
        o_a = moba_attention(aq_h, ak_h, av_h)
        h_a = o_a.transpose(0, 2, 1, 3).reshape(B, S, A_WIDTH)

        y_m = jnp.einsum('bsc,cd->bsd', h_m, w_branch_m[l])
        y_a = jnp.einsum('bsc,cd->bsd', h_a, w_branch_a[l])
        merged = jax.nn.sigmoid(g_m) * y_m + jax.nn.sigmoid(g_a) * y_a
        mix_out = jnp.einsum('bsd,de->bse', merged, w_out[l])
        x = x + rmsnorm(mix_out, norm_mix_post[l])

        hn = rmsnorm(x, norm_ffn_pre[l])
        u = jnp.square(jax.nn.relu(jnp.einsum('bsd,df->bsf', hn, w_up[l])))
        y = jnp.einsum('bsf,fd->bsd', u, w_down[l])
        x = x + rmsnorm(y, norm_ffn_post[l])
    return x


def setup_inputs(seed=0):
    out = dict(first_inputs(seed))
    for name, value in second_inputs(seed + 1).items():
        if name != "x":
            out[name + "_2"] = value
    return out


def reference(
    x, c, positions, norm_g, mod_w, mod_b, pool_w_in, pool_w_grp, pool_scale, pool_w_out,
    attn_w_in, attn_w_out, final_g, positions_2, norm_mix_pre_2, w_in_2, conv_w_2, conv_b_2,
    i_bias_2, f_bias_2, mlstm_norm_2, w_branch_m_2, w_branch_a_2, w_out_2, norm_mix_post_2,
    norm_ffn_pre_2, w_up_2, w_down_2, norm_ffn_post_2,
):
    x = first_block(
        x, c, positions, norm_g, mod_w, mod_b, pool_w_in, pool_w_grp, pool_scale, pool_w_out,
        attn_w_in, attn_w_out, final_g,
    )
    return second_block(
        x, positions_2, norm_mix_pre_2, w_in_2, conv_w_2, conv_b_2, i_bias_2, f_bias_2,
        mlstm_norm_2, w_branch_m_2, w_branch_a_2, w_out_2, norm_mix_post_2, norm_ffn_pre_2,
        w_up_2, w_down_2, norm_ffn_post_2,
    )


_drawn_inputs = setup_inputs


def setup_inputs(seed=0):
    import zlib

    import numpy as np

    out = dict(_drawn_inputs(seed))
    spreads = {}
    factors = {'norm_g': 4.995, 'conv_b_2': 8.0, 'i_bias_2': 64.0}
    for name, (base, spread) in spreads.items():
        noise = np.random.default_rng([zlib.crc32(name.encode()), seed]).standard_normal(out[name].shape)
        drawn = base * np.exp(spread * noise) if base else spread * noise
        out[name] = __import__('jax').numpy.asarray(drawn.astype(out[name].dtype))
    for name, factor in factors.items():
        out[name] = (out[name] * factor).astype(out[name].dtype)
    return out
```

```python
from contextlib import ExitStack, contextmanager

import concourse.bass as bass
import numpy as np
from concourse import mybir

F32 = mybir.dt.float32
F32R = mybir.dt.float32r
I32 = mybir.dt.int32
ALU = mybir.AluOpType
ACT = mybir.ActivationFunctionType

P = 128
S = 256
NT = S // P
D = 2048
KC = D // P
NBLK = 512
KPC = 2
CPB = KC // KPC
RAW = 8
SPL = 4
AHEAD = 3
EPS = 1e-6
HD = 128
CAUS = P + S
FAR = -3.0e38
TAKEN = -3.3e38
UNPICKED = -1.0e30
MAGIC = 12582912.0
TWO_PI = (6.28125, 0.0019350051879882812, 3.019915981956752e-07)
PI_CLAMP = 3.1415925
WINDOWS = (2, 4, 8, 16)
TOPK = 64
DSA_HEADS, MOBA_HEADS, M_HEADS, IDX_HEADS = 16, 8, 4, 16
IDX_COL = 4 * D
N_FFN = 8

C_ID, C_TRI, C_CUM, C_ONE, C_FRQ = 0, 128, 512, 640, 768
FRQ1, FRQI, FRQ2 = 16, 8, 64
C_ALL = C_FRQ + FRQ1 + FRQI + FRQ2

PHASES = {}


def _plan():
    b = a = 0
    for name, blocks, accs in (
        ("pool_v", 4, 4), ("pool_gate", 4, 4), ("group", 1, 4), ("pool_out", 4, 4), ("idx_q", 2, 2), ("idx_kw", 1, 1),
        ("qk", 8, 8), ("v", 4, 4), ("gate", 4, 4), ("attn_out", 4, 4), ("m_qk", 4, 4), ("m_v", 2, 2), ("m_o", 2, 2),
        ("m_if", 1, 1), ("a_qk", 4, 4), ("a_v", 2, 2), ("g_m", 4, 4), ("g_a", 4, 4), ("branch", 4, 8),
        ("mix_out", 4, 4), ("ffn", 32, 48),
    ):
        PHASES[name] = (b, a, blocks)
        b, a = b + blocks, a + accs
    return b


N_BLOCKS = _plan()

JOBS, SPLITS = {}, {}


def _jobs():
    n = s = 0
    for name, jobs, split in (
        ("norm0", 4, True), ("pool_v", 4, True), ("group", 4, True), ("norm1", 4, True), ("idx_q", 2, False),
        ("idx_kw", 1, False), ("qk", 8, False), ("attn", 4, True), ("norm2", 4, True), ("m_qk", 4, False),
        ("mlstm", 2, True), ("a_qk", 4, False), ("moba", 2, True), ("branch", 4, True), ("norm3", 4, True),
        ("ffn", 16, True),
    ):
        JOBS[name], SPLITS[name] = n, s
        n, s = n + jobs, s + (jobs if split else 0)


_jobs()
STAGED = {}


def _staged():
    n = 0
    for name, jobs in (("group", 4), ("idx_q", 2), ("idx_kw", 1), ("qk", 8), ("attn", 4), ("mlstm", 2), ("a_qk", 4),
                       ("moba", 2), ("branch", 4), ("ffn", 16)):
        STAGED[name] = n
        n += jobs


_staged()
COMBINED = {"pool_out": 0, "attn_out": 4, "ffn": 8}


class Chain:

    def __init__(self, eng, sem):
        self.eng, self.sem, self.n, self.off = eng, sem, 0, 0

    def __call__(self, ins):
        ins.then_inc(self.sem, 1)
        self.n += 1
        self.eng.wait_ge(self.sem, self.off + self.n)

    @contextmanager
    def loop(self, first, last, per):
        start = self.n
        with self.eng.Fori(first, last) as b:
            self.off = (b - first) * per if per else 0
            yield b
        assert self.n - start == per, f"{self.n - start} steps, not {per}"
        self.n, self.off = start + per * (last - first), 0


def build(nc, x, c, positions, norm_g, mod_w, mod_b, pool_w_in, pool_w_grp, pool_scale, pool_w_out, attn_w_in,
          attn_w_out, final_g, positions_2, norm_mix_pre_2, w_in_2, conv_w_2, conv_b_2, i_bias_2, f_bias_2,
          mlstm_norm_2, w_branch_m_2, w_branch_a_2, w_out_2, norm_mix_post_2, norm_ffn_pre_2, w_up_2, w_down_2,
          norm_ffn_post_2, consts, windows, mod_rows, resid, out):
    with ExitStack() as ctx:
        def sb(name, shape, dt=F32):
            return ctx.enter_context(nc.sbuf_tensor(name, shape, dt))

        def sem(name):
            return ctx.enter_context(nc.semaphore(name))

        raw = sb("raw", [P, RAW, KPC, NBLK])
        w_hi = sb("w_hi", [P, SPL, KPC, NBLK], F32R)
        w_lo = sb("w_lo", [P, SPL, KPC, NBLK], F32R)
        xa_hi, xa_lo = sb("xa_hi", [P, KC, S], F32R), sb("xa_lo", [P, KC, S], F32R)
        xb_hi, xb_lo = sb("xb_hi", [P, KC, S], F32R), sb("xb_lo", [P, KC, S], F32R)
        XA, XB = (xa_hi, xa_lo), (xb_hi, xb_lo)
        T = sb("T", [P, 4, 2 * D])
        stage = sb("stage", [P, NT, NBLK])
        tmp = sb("tmp", [P, 4, S])
        wide = sb("wide", [P, D])
        probs_t = sb("probs_t", [P, 2, CAUS])
        con = sb("con", [P, C_ALL])
        pick = sb("pick", [P, CAUS])
        vec1, vec2 = sb("vec1", [P, P]), sb("vec2", [P, P])
        vec3 = sb("vec3", [P, 64])
        rot = sb("rot", [P, 2, NT, FRQ1 + FRQI + FRQ2])
        posi = sb("posi", [P, 2, NT], I32)
        posf = sb("posf", [P, 2, NT])
        csil = sb("csil", [P, KC])
        scl = sb("scl", [P, 2, KC])
        idx_w = sb("idx_w", [P, NT, IDX_HEADS])
        ifb = sb("ifb", [P, 8])
        small = sb("small", [P, 12, 8])
        ms = sb("ms", [P, 8])
        rs = sb("rs", [P, 8])
        t8 = sb("t8", [P, 8])
        best = sb("best", [P, NT, 8])
        mx = sb("mx", [P, 2, NT])
        nmx = sb("nmx", [P, 2, NT])
        den = sb("den", [P, 4, NT])
        rden = sb("rden", [P, 2, NT])

        ps = ctx.enter_context(nc.psum_tensor("ps", [P, 8, 512], F32))

        ident, tri, cum = con[:, C_ID:C_ID + P], con[:, C_TRI:C_TRI + CAUS], con[:, C_CUM:C_CUM + P]
        ones, freqs = con[:, C_ONE:C_ONE + P], con[:, C_FRQ:C_ALL]

        def tok(i, cols=D, at=0):
            return T[:, i, at:at + NT * cols].rearrange("p (t n) -> p t n", t=NT)

        def feat(i, n=KC):
            return T[:, i, 0:n * S].rearrange("p (f t) -> p f t", t=S)

        T0, T1, T2, T3 = (tok(i) for i in range(4))
        qk_t = T[:, 0:2, :].rearrange("p a (f t) -> p (a f) t", t=S)
        amat = T[:, 2, 0:4 * NT * S].rearrange("p (g u t) -> p g u t", g=4, u=NT)
        mod_raw = T[:, 1:3, :].rearrange("p a (s n) -> p (a s) n", n=D)
        mod_acc = T[:, 3, :].rearrange("p (a n) -> p a n", a=2)
        qi_t = feat(3, 8)
        ki_t = T[:, 3, 2048:2048 + S]
        score = T[:, 3, 2560:2560 + CAUS]
        m_v, m_o = T1[:, :, 0:1024], T1[:, :, 1024:2048]
        m_num = T[:, 2, 0:2048].rearrange("p (h t n) -> p h t n", h=M_HEADS, t=NT)
        a_v = tok(3, 1024)
        probs = tmp[:].rearrange("p f t -> p (f t)")[:, 0:2 * CAUS].rearrange("p (b n) -> p b n", b=2)
        x_tmp = wide[:, 0:4 * S].rearrange("p (f t) -> p f t", t=S)
        stage_f = stage[:].rearrange("p t (f n) -> p (t f) n", n=S)
        tmp_t = tmp[:].rearrange("p f t -> p (f t)").rearrange("p (t n) -> p t n", t=NT)
        m_dec = T[:, 2, 2048:2048 + M_HEADS * CAUS].rearrange("p (h n) -> p h n", h=M_HEADS)
        m_diag = tmp[:].rearrange("p f t -> p (f t)").rearrange("p (t h n) -> p t h n", t=NT, h=M_HEADS)
        gate_i, gate_u, gate_f, gate_w, cum_f, m_max, m_nmax, m_floor, m_e = (
            small[:, i, :].rearrange("p (t h) -> p t h", t=NT) for i in range(9))
        C_, G0, G1, PSC, MIXP, FFNP, CVB, MLN = (vec1[:, 16 * i:16 * i + 16] for i in range(8))

        def job_bank(n):
            return n % 2 * 2 + 4 if isinstance(n, int) else 4

        landed = [sem(f"landed{i}") for i in range(RAW)]
        hi_ready, lo_ready, w_used = sem("hi_ready"), sem("lo_ready"), sem("w_used")
        acc_free = sem("acc_free")
        staged, combined = sem("staged"), sem("combined")
        tp_ready, tp_evac, xh_ready, x_ready = sem("tp_ready"), sem("tp_evac"), sem("xh_ready"), sem("x_ready")
        dve_step, act_step = sem("dve_step"), sem("act_step")
        in_landed, vec_landed, amat_landed = sem("in_landed"), sem("vec_landed"), sem("amat_landed")
        vec_tp, vec_done = sem("vec_tp"), sem("vec_done")
        csil_ready, sin_in, rot_ready = sem("csil_ready"), sem("sin_in"), sem("rot_ready")
        mod_landed = [sem(f"mod_landed{i}") for i in range(4)]
        mod_used, acc_zero, bias_landed = sem("mod_used"), sem("acc_zero"), sem("bias_landed")
        mod_sum, row_ready, row_stored = sem("mod_sum"), sem("row_ready"), sem("row_stored")
        rows_back, sq_done, ms_ready, root_ready, xn_ready = (
            sem("rows_back"), sem("sq_done"), sem("ms_ready"), sem("root_ready"), sem("xn_ready"))
        wide_landed, wide_used = sem("wide_landed"), sem("wide_used")
        res_landed, res_stored, res_done = sem("res_landed"), sem("res_stored"), sem("res_done")
        scl_ready, picked = sem("scl_ready"), sem("picked")
        sc_ready, relu_ready, sc_used = sem("sc_ready"), sem("relu_ready"), sem("sc_used")
        lg_ready, masked, exp_ready = sem("lg_ready"), sem("masked"), sem("exp_ready")
        pt_ready, pt_copied, pv_ready, o_done = sem("pt_ready"), sem("pt_copied"), sem("pv_ready"), sem("o_done")
        conv_in, conv_done = sem("conv_in"), sem("conv_done")
        g_in, g_act, g_mm, g_dve, g_sq = sem("g_in"), sem("g_act"), sem("g_mm"), sem("g_dve"), sem("g_sq")
        out_done, out_stored = sem("out_done"), sem("out_stored")

        def plain(w, col0):
            v = w.rearrange("(k p) n -> p k n", p=P)
            return lambda b, j: v[:, KPC * j:KPC * j + KPC, bass.ds(b * NBLK + col0, NBLK)]

        def narrow(w, col0, n):
            v = w.rearrange("(k p) n -> p k n", p=P)
            return lambda b, j: v[:, KPC * j:KPC * j + KPC, col0:col0 + n]

        grp = pool_w_grp[0].rearrange("g (k p) n -> p g k n", p=P)
        bm, ba = (w[0].rearrange("(k p) n -> p k n", p=P) for w in (w_branch_m_2, w_branch_a_2))
        down = w_down_2[0].rearrange("(e k p) n -> p e k n", e=N_FFN, p=P)

        def src_group(b, j):
            return grp[:, j // 2, KPC * (j % 2):KPC * (j % 2) + KPC, :]

        def src_branch(b, j):
            w, k = (bm, j) if j < 4 else (ba, j - 4)
            return w[:, KPC * k:KPC * k + KPC, bass.ds(b * NBLK, NBLK)]

        up = plain(w_up_2[0], 0)
        SOURCES = {
            "pool_v": plain(pool_w_in[0], 0), "pool_gate": plain(pool_w_in[0], D), "group": src_group,
            "pool_out": plain(pool_w_out[0], 0), "idx_q": plain(attn_w_in[0], IDX_COL),
            "idx_kw": narrow(attn_w_in[0], IDX_COL + 1024, 80), "qk": plain(attn_w_in[0], 0),
            "v": plain(attn_w_in[0], 2 * D), "gate": plain(attn_w_in[0], 3 * D), "attn_out": plain(attn_w_out[0], 0),
            "m_qk": plain(w_in_2[0], 0), "m_v": plain(w_in_2[0], 2048), "m_o": plain(w_in_2[0], 3072),
            "m_if": narrow(w_in_2[0], 4096, 8), "a_qk": plain(w_in_2[0], 4104), "a_v": plain(w_in_2[0], 6152),
            "g_m": plain(w_in_2[0], 7176), "g_a": plain(w_in_2[0], 9224), "branch": src_branch,
            "mix_out": plain(w_out_2[0], 0),
        }

        FB, FA, _ = PHASES["ffn"]

        block = ctx.enter_context(nc.Block())

        @block.sync
        def _(sp):
            def load(src, name_b, b, j, B, first=False, cols=NBLK):
                if not first:
                    sp.wait_ge(lo_ready, B * CPB + (j + 1 - RAW))
                sp.dma_start(raw[:, j, :, 0:cols], src(b, j)).then_inc(landed[j], 16)

            def load_phase(name, cols=NBLK):
                B0, _, n = PHASES[name]
                src = SOURCES[name]
                for j in range(CPB):
                    load(src, name, 0, j, B0, first=B0 == 0, cols=cols)
                if n > 1:
                    with sp.Fori(1, n) as b:
                        for j in range(CPB):
                            load(src, name, b, j, b + B0, cols=cols)

            sp.dma_start(con[:], consts).then_inc(in_landed, 16)
            for v, row, n, src in (
                (0, 0, 16, c[0]), (0, 16, 16, norm_g[0]), (0, 32, 16, norm_g[1]), (0, 48, 16, pool_scale[0]),
                (0, 64, 16, norm_mix_pre_2[0]), (0, 80, 16, norm_ffn_pre_2[0]), (0, 96, 16, conv_b_2[0]),
                (0, 112, 8, mlstm_norm_2[0]), (1, 0, 16, conv_w_2[0, 0]), (1, 16, 16, conv_w_2[0, 1]),
                (1, 32, 16, conv_w_2[0, 2]), (1, 48, 16, conv_w_2[0, 3]),
            ):
                sp.dma_start(stage[row:row + n, v, 0:P], src.rearrange("(r n) -> r n", n=P)).then_inc(vec_landed, 16)
            with nc.allow_non_contiguous_dma(reason="a position to a partition"):
                for i, pos in enumerate((positions, positions_2)):
                    sp.dma_start(posi[:, i, :], pos[0].rearrange("(t p) -> p t", p=P)).then_inc(in_landed, 16)
            for i, bias in enumerate((i_bias_2, f_bias_2)):
                sp.dma_start(ifb[:, 4 * i:4 * i + 4], bias[0:1, :].to_broadcast([P, 4])).then_inc(in_landed, 16)

            mw = mod_w.rearrange("i (k p) (u n) -> p i u k n", p=P, n=D)
            mb = mod_b.rearrange("i (u n) -> (i u) n", n=D)

            def third(u, first=False):
                sp.wait_ge(acc_zero, u + 1)
                sp.dma_start(mod_acc[0:1, bass.ds(u % 2, 1), :], mb[bass.ds(u, 1), :].unsqueeze(1)
                             ).then_inc(bias_landed, 16)
                for k in range(KC):
                    if not (first and k < 4):
                        sp.wait_ge(mod_used, u * KC + (k - 3))
                    sp.dma_start(mod_raw[:, k % 4:k % 4 + 1, :], mw[:, bass.ds(u // 3, 1), bass.ds(u % 3, 1), k, :]
                                 .rearrange("p a b n -> p (a b) n")).then_inc(mod_landed[k % 4], 16)

            third(0, first=True)
            with sp.Fori(1, 6) as u:
                third(u)
            sp.dma_start(T0[:], x[0].rearrange("(t p) n -> p t n", p=P)).then_inc(in_landed, 16)
            for i in range(2):
                for u in range(2):
                    sp.wait_ge(row_stored, 16 * 6)
                    row = 32 * i + 16 * u
                    sp.dma_start(stage[row:row + 16, 0, 128:256], mod_rows[3 * i + u].rearrange("(r n) -> r n", n=P)
                                 ).then_inc(rows_back, 16)
            sp.wait_ge(mod_used, 6 * KC)
            sp.dma_start(amat[:], windows).then_inc(amat_landed, 16)

            load_phase("pool_v")
            load_phase("pool_gate")
            for name in ("group", "pool_out", "idx_q"):
                load_phase(name)
            load_phase("idx_kw", cols=80)
            for name in ("qk", "v", "gate", "attn_out", "m_qk", "m_v", "m_o"):
                load_phase(name)
            load_phase("m_if", cols=8)
            for name in ("a_qk", "a_v", "g_m", "g_a", "branch", "mix_out"):
                load_phase(name)

            def ffn_up(e, B, first=False):
                for h in range(2):
                    for j in range(CPB):
                        load(lambda b, j: up(e * 2 + h, j), "", 0, j, B + h)

            def ffn_down(e, B):
                for h in range(2):
                    for j in range(CPB):
                        load(lambda b, j: down[:, bass.ds(e, 1), KPC * (j % 4):KPC * (j % 4) + KPC,
                                               NBLK * (2 * h + j // 4):NBLK * (2 * h + j // 4) + NBLK]
                             .rearrange("p e k n -> p (e k) n"), "", 0, j, B + h)

            ffn_up(0, FB)
            ffn_up(1, FB + 2)
            ffn_down(0, FB + 4)
            with sp.Fori(0, 3) as i:
                ffn_up(i * 2 + 2, i * 8 + (FB + 6))
                ffn_down(i * 2 + 1, i * 8 + (FB + 8))
                ffn_up(i * 2 + 3, i * 8 + (FB + 10))
                ffn_down(i * 2 + 2, i * 8 + (FB + 12))
            ffn_down(7, FB + 30)
            for t in range(NT):
                sp.wait_ge(out_done, t + 1)
                sp.dma_start(out[0, t * P:(t + 1) * P, :], T1[:, t, :]).then_inc(out_stored, 16)
            sp.wait_ge(out_stored, 16 * NT)

        @block.gpsimd
        def _(pool):
            def tokens(dram):
                return dram.rearrange("(t p) n -> p t n", p=P)

            def widen(row):
                pool.dma_start(wide[:], row.to_broadcast([P, D])).then_inc(wide_landed, 16)

            pool.wait_ge(tp_ready, JOBS["pool_v"] + 4)
            pool.dma_start(T2[:], tokens(x[0])).then_inc(res_landed, 16)
            pool.wait_ge(row_stored, 16 * 6)
            widen(mod_rows[2:3, :])
            pool.wait_ge(combined, 4)
            pool.dma_start(tokens(resid[0]), T2[:]).then_inc(res_stored, 16)
            pool.wait_ge(x_ready, SPLITS["attn"] + 4)
            widen(mod_rows[5:6, :])
            pool.wait_ge(pv_ready, DSA_HEADS)
            pool.wait_ge(res_stored, 16)
            pool.dma_start(T0[:], tokens(resid[0])).then_inc(res_landed, 16)
            pool.wait_ge(combined, 8)
            widen(final_g.rearrange("(a n) -> a n", a=1))
            pool.wait_ge(res_done, 1)
            pool.dma_start(tokens(resid[1]), T0[:]).then_inc(res_stored, 16)
            pool.wait_ge(x_ready, SPLITS["moba"] + 2)
            widen(norm_mix_post_2)
            pool.wait_ge(pv_ready, DSA_HEADS + M_HEADS + MOBA_HEADS)
            pool.wait_ge(res_stored, 32)
            pool.dma_start(T3[:], tokens(resid[1])).then_inc(res_landed, 16)
            pool.wait_ge(res_done, 2)
            widen(norm_ffn_post_2)

        @block.scalar
        def _(act):
            step = Chain(act, act_step)

            def hi(B, o):
                lap = B + o // CPB
                act.wait_ge(landed[o % RAW], lap * 16 + 16)
                if not (isinstance(B, int) and B == 0 and o < SPL):
                    act.wait_ge(w_used, lap * CPB + (o % CPB + 1 - SPL))
                nc.scalar.copy(w_hi[:, o % SPL], raw[:, o % RAW]).then_inc(hi_ready, 1)

            def evac(dst, A, done, func=ACT.Copy, cols=NBLK):
                act.wait_ge(w_used, done)
                nc.scalar.activation(dst, ps[:, bass.ds((A % 2) * 2, 2), 0:cols], func).then_inc(acc_free, 1)

            def split(n, s, X, g, src):
                act.wait_ge(tp_evac, n + 1)
                nc.scalar.copy(X[0][:, bass.ds(g * 4, 4), :], src).then_inc(xh_ready, 1)

            def blk(B, hooks=None, last=False):
                for o in range(AHEAD, CPB if last else CPB + AHEAD):
                    hi(B, o)
                    if hooks and o in hooks:
                        hooks[o]()

            def phase(name, each, job=None):
                B0, A0, n = PHASES[name]
                blk(B0)
                each(0, B0, A0)
                if n > 1:
                    with act.Fori(1, n) as b:
                        blk(b + B0, {6: lambda: job(b - 1)} if job else None)
                        each(b, b + B0, b + A0)
                if job:
                    job(n - 1)

            def splits(name, X):
                return lambda b: split(b + JOBS[name], b + SPLITS[name], X, b, tmp[:])

            def root(i, n):
                act.wait_ge(ms_ready, i + 1)
                nc.scalar.activation(rs[:, 0:n], t8[:, 0:n], ACT.Sqrt).then_inc(root_ready, 1)

            def squares(i, src, junk):
                for t in range(NT):
                    step(nc.scalar.activation(junk[:, t, :], src[:, t, :], ACT.Square, accum_out=ms[:, t:t + 1]))
                act.sem_inc(sq_done, 1)
                root(i, NT)

            def norm_splits(name, X):
                for g in range(4):
                    split(JOBS[name] + g, SPLITS[name] + g, X, g, (tmp[:], stage_f)[g % 2])

            act.wait_ge(vec_done, 1)
            nc.scalar.activation(csil[:], C_, ACT.Silu).then_inc(csil_ready, 1)
            act.wait_ge(sin_in, 1)
            nc.scalar.activation(rot[:], rot[:], ACT.Sin).then_inc(rot_ready, 1)

            def row(u):
                act.wait_ge(mod_sum, u + 1)
                if not isinstance(u, int):
                    act.wait_ge(row_stored, u * 16)
                nc.scalar.copy(wide[0:1, :].rearrange("p (b n) -> p b n", b=4), ps[0:1, 0:4, :]).then_inc(row_ready, 1)
                act.wait_ge(row_ready, u + 1)
                act.dma_start(mod_rows[bass.ds(u, 1), :], wide[0:1, :]).then_inc(row_stored, 16)

            row(0)
            with act.Fori(1, 6) as u:
                row(u)

            act.wait_ge(in_landed, 16 * 6)
            act.wait_ge(mod_used, 6 * KC)
            squares(0, T0, T1)
            norm_splits("norm0", XA)
            for o in range(AHEAD):
                hi(0, o)

            def pool_v(b, B, A):
                act.wait_ge(tp_ready, b + JOBS["pool_v"])
                act.wait_ge(x_ready, SPLITS["norm0"] + 4)
                evac(stage[:], A, B * CPB + CPB)

            phase("pool_v", pool_v, splits("pool_v", XB))
            phase("pool_gate", lambda b, B, A: evac(T1[:, :, bass.ds(b * NBLK, NBLK)], A, B * CPB + CPB, ACT.Silu))

            B0, A0, _ = PHASES["group"]
            jg, sg = JOBS["group"], SPLITS["group"]
            for o in range(AHEAD, CPB + AHEAD):
                hi(B0, o)
                if o in (4, 6, 8, 10):
                    g = (o - 4) // 2
                    act.wait_ge(tp_ready, jg + g)
                    evac(stage[:], A0 + g, B0 * CPB + 2 * g + 2)
                if o in (7, 9):
                    split(jg + (o - 7) // 2, sg + (o - 7) // 2, XA, (o - 7) // 2, tmp[:])
            for g in (2, 3):
                split(jg + g, sg + g, XA, g, tmp[:])

            def to_residual(name, job):
                def each(b, B, A):
                    act.wait_ge(tp_ready, job)
                    act.wait_ge(combined, b + COMBINED[name])
                    evac(stage[:], A, B * CPB + CPB)
                return each

            phase("pool_out", to_residual("pool_out", JOBS["group"] + 4))

            act.wait_ge(combined, 4)
            squares(1, T2, T1)
            norm_splits("norm1", XB)

            def to_stage(name, norm=None, cols=NBLK):
                def each(b, B, A):
                    act.wait_ge(tp_ready, b + JOBS[name])
                    if norm:
                        act.wait_ge(x_ready, SPLITS[norm] + 4)
                    evac(stage[:, :, 0:cols], A, B * CPB + CPB, cols=cols)
                return each

            phase("idx_q", to_stage("idx_q", "norm1"))
            phase("idx_kw", to_stage("idx_kw", cols=80))
            act.wait_ge(tp_evac, JOBS["idx_kw"] + 1)
            for h in range(IDX_HEADS):
                act.wait_ge(sc_ready, h + 1)
                if h >= 2:
                    act.wait_ge(sc_used, h - 1)
                nc.scalar.activation(probs[:, h % 2, :], ps[:, 4 + h % 4, 0:CAUS], ACT.Relu).then_inc(relu_ready, 1)
            phase("qk", to_stage("qk"))
            act.wait_ge(res_stored, 16)
            phase("v", lambda b, B, A: evac(T2[:, :, bass.ds(b * NBLK, NBLK)], A, B * CPB + CPB))
            act.wait_ge(picked, 1)
            phase("gate", lambda b, B, A: evac(T3[:, :, bass.ds(b * NBLK, NBLK)], A, B * CPB + CPB, ACT.Silu))

            def copy_probs(h, i):
                act.wait_ge(pt_ready, h + 1)
                if i >= 2 or h >= DSA_HEADS:
                    act.wait_ge(pv_ready, h - 1)
                nc.scalar.copy(probs_t[:, i % 2, :], ps[:, 6 + i % 2, 0:CAUS]).then_inc(pt_copied, 1)

            def attention(h0, e0, heads, name, g0):
                for i in range(heads + 3):
                    if i < heads:
                        act.wait_ge(masked, h0 + i + 1)
                        for t, (a, z) in enumerate(((0, P), (P, CAUS))):
                            last = nc.scalar.activation(
                                probs[:, i % 2, a:z], probs[:, i % 2, a:z], ACT.Exp, bias=nmx[:, i % 2, t:t + 1],
                                scale=HD ** -0.5, accum_out=den[:, i % 4, t:t + 1])
                        act.drain()
                        act.sem_inc(exp_ready, 1)
                    if 1 <= i <= heads:
                        copy_probs(h0 + i - 1, i - 1)
                    if i >= 6 and i % 4 == 2:
                        n = (i - 6) // 4
                        split(JOBS[name] + n, SPLITS[name] + n, XA, g0 + n, x_tmp)

            attention(0, 0, DSA_HEADS, "attn", 0)
            phase("attn_out", to_residual("attn_out", JOBS["attn"] + 4))

            act.wait_ge(combined, 8)
            squares(2, T0, T1)
            act.wait_ge(res_done, 1)
            squares(3, T0, T2)
            norm_splits("norm2", XB)

            def conv_silu(b):
                act.wait_ge(conv_in, b + 1)
                nc.scalar.activation(feat(0)[:, bass.ds(b * 4, 4), :], tmp[:], ACT.Silu).then_inc(conv_done, 1)

            act.wait_ge(res_stored, 32)
            phase("m_qk", to_stage("m_qk", "norm2"), conv_silu)
            phase("m_v", lambda b, B, A: evac(m_v[:, :, bass.ds(b * NBLK, NBLK)], A, B * CPB + CPB))
            phase("m_o", lambda b, B, A: evac(m_o[:, :, bass.ds(b * NBLK, NBLK)], A, B * CPB + CPB, ACT.Sigmoid))

            B0, A0, _ = PHASES["m_if"]
            blk(B0)
            act.wait_ge(tp_ready, JOBS["m_qk"] + 4)
            evac(stage[:, :, 0:8], A0, B0 * CPB + CPB, cols=8)

            act.wait_ge(g_in, 1)
            step(nc.scalar.activation(gate_u, gate_u, ACT.Exp))
            act.sem_inc(g_act, 1)
            act.wait_ge(g_in, 2)
            nc.scalar.activation(gate_f, gate_w, ACT.Ln).then_inc(g_act, 1)
            act.wait_ge(g_dve, 1)
            for h in range(M_HEADS):
                for t, (a, z) in enumerate(((0, P), (P, CAUS))):
                    nc.scalar.activation(m_dec[:, h, a:z], m_dec[:, h, a:z], ACT.Exp, bias=m_nmax[:, t, h:h + 1])
            nc.scalar.activation(m_floor, m_floor, ACT.Exp, scale=-1.0).then_inc(g_act, 1)
            for i in range(M_HEADS + 2):
                if 1 <= i <= M_HEADS:
                    copy_probs(DSA_HEADS + i - 1, i - 1)
                if i >= 2:
                    act.wait_ge(o_done, DSA_HEADS + i - 1)
                    for t in range(NT):
                        at = ((i - 2) * NT + t) * S
                        step(nc.scalar.activation(T[:, 3, at:at + S], m_num[:, i - 2, t, :], ACT.Square,
                                                  accum_out=ms[:, t * M_HEADS + i - 2:t * M_HEADS + i - 1]))
            act.sem_inc(sq_done, 1)
            root(4, NT * M_HEADS)
            for n in range(2):
                split(JOBS["mlstm"] + n, SPLITS["mlstm"] + n, XA, n, x_tmp)

            phase("a_qk", to_stage("a_qk"))
            phase("a_v", lambda b, B, A: evac(a_v[:, :, bass.ds(b * NBLK, NBLK)], A, B * CPB + CPB))
            attention(DSA_HEADS + M_HEADS, DSA_HEADS, MOBA_HEADS, "moba", 2)
            phase("g_m", lambda b, B, A: evac(T0[:, :, bass.ds(b * NBLK, NBLK)], A, B * CPB + CPB, ACT.Sigmoid))
            phase("g_a", lambda b, B, A: evac(T1[:, :, bass.ds(b * NBLK, NBLK)], A, B * CPB + CPB, ACT.Sigmoid))

            B0, A0, n = PHASES["branch"]

            def branch(b, first=False):
                B, A = b + B0, b * 2 + A0
                for o in range(AHEAD, CPB + AHEAD):
                    hi(B, o)
                    if o == 6:
                        if not first:
                            split(b + (JOBS["branch"] - 1), b + (SPLITS["branch"] - 1), XB, b - 1, tmp[:])
                        act.wait_ge(tp_ready, b + JOBS["branch"])
                        evac(stage[:], A, B * CPB + 4)
                act.wait_ge(x_ready, b + SPLITS["branch"])
                evac(tmp_t, A + 1, B * CPB + 8)

            branch(0, first=True)
            with act.Fori(1, n) as b:
                branch(b)
            split(JOBS["branch"] + 3, SPLITS["branch"] + 3, XB, 3, tmp[:])

            phase("mix_out", lambda b, B, A: evac(T2[:, :, bass.ds(b * NBLK, NBLK)], A, B * CPB + CPB))
            act.wait_ge(acc_free, PHASES["mix_out"][1] + 4)
            squares(5, T2, T1)
            act.wait_ge(res_done, 2)
            squares(6, T3, T1)
            norm_splits("norm3", XA)

            J, X0, C0 = JOBS["ffn"], SPLITS["ffn"], COMBINED["ffn"]

            def up(e, half, B, A, after=None):
                for h in range(2):
                    def mid():
                        split(e * 2 + (J + h - 1), e * 2 + (X0 + h - 1), XB, (2 * half + h - 1) % 4, tmp[:])
                    blk(B + h, {6: mid} if h == 1 or after == "up" else None)
                    act.wait_ge(tp_ready, e * 2 + (J + h))
                    if after == "norm":
                        act.wait_ge(x_ready, X0)
                    elif after is None:
                        act.wait_ge(combined, e * 4 + (C0 - 4))
                    evac(stage[:], A + h, (B + h) * CPB + CPB, ACT.Relu)

            def dn(e, half, B, A, last=False):
                def take(q):
                    act.wait_ge(tp_ready, (J + 2 * N_FFN) if last else e * 2 + (J + 4))
                    act.wait_ge(combined, e * 4 + (C0 + q))
                    evac(stage[:], A + q, B * CPB + 4 * (q + 1))

                def mid():
                    if not last:
                        split(e * 2 + (J + 3), e * 2 + (X0 + 3), XB, 2 * (1 - half) + 1, tmp[:])
                    take(0)

                blk(B, {6: mid, 10: lambda: take(1)})
                blk(B + 1, {6: lambda: take(2), 10: lambda: take(3)}, last=last)
                if last:
                    take(3)

            up(0, 0, FB, FA, after="norm")
            up(1, 1, FB + 2, FA + 2, after="up")
            dn(0, 0, FB + 4, FA + 4)
            with act.Fori(0, 3) as i:
                up(i * 2 + 2, 0, i * 8 + (FB + 6), i * 12 + (FA + 8))
                dn(i * 2 + 1, 1, i * 8 + (FB + 8), i * 12 + (FA + 10))
                up(i * 2 + 3, 1, i * 8 + (FB + 10), i * 12 + (FA + 14))
                dn(i * 2 + 2, 0, i * 8 + (FB + 12), i * 12 + (FA + 16))
            dn(7, 1, FB + 30, FA + 44, last=True)
            act.wait_ge(combined, COMBINED["ffn"] + 4 * N_FFN)
            squares(7, T1, T2)

        @block.vector
        def _(dve):
            step = Chain(dve, dve_step)
            tt, ts, stt = nc.vector.tensor_tensor, nc.vector.tensor_scalar, nc.vector.scalar_tensor_tensor

            def lo(B, o):
                dve.wait_ge(hi_ready, (B + o // CPB) * CPB + (o % CPB + 1))
                tt(w_lo[:, o % SPL], raw[:, o % RAW], w_hi[:, o % SPL].bitcast(F32), ALU.subtract
                   ).then_inc(lo_ready, 1)

            def blk(B, hooks=None, last=False):
                for o in range(AHEAD, CPB if last else CPB + AHEAD):
                    lo(B, o)
                    if hooks and o in hooks:
                        hooks[o]()

            def phase(name, each=None, out=None, low=None, per=0):
                B0, A0, n = PHASES[name]
                blk(B0)
                if each:
                    each(0, A0)
                if n > 1:
                    with step.loop(1, n, per) as b:
                        blk(b + B0, {5: lambda: out(b - 1), 6: lambda: low(b - 1)} if out else None)
                        if each:
                            each(b, b + A0)
                if out:
                    out(n - 1)
                    low(n - 1)

            def leave(n, dst, scale=None, shift=None, bank=None):
                dve.wait_ge(tp_ready, n + 1)
                p0 = job_bank(n) if bank is None else bank
                src = ps[:, p0:p0 + 2, :].rearrange("p b (f t) -> p (b f) t", t=S)
                if scale is None:
                    nc.vector.tensor_copy(dst, src).then_inc(tp_evac, 1)
                elif shift is None:
                    tt(dst, src, scale.unsqueeze(2).to_broadcast([P, 4, S]), ALU.mult).then_inc(tp_evac, 1)
                else:
                    step(tt(dst, src, scale.unsqueeze(2).to_broadcast([P, 4, S]), ALU.mult))
                    tt(dst, dst, shift.unsqueeze(2).to_broadcast([P, 4, S]), ALU.add).then_inc(tp_evac, 1)

            def low_part(s, X, g, src):
                dve.wait_ge(xh_ready, s + 1)
                tt(X[1][:, bass.ds(g * 4, 4), :], src, X[0][:, bass.ds(g * 4, 4), :].bitcast(F32), ALU.subtract
                   ).then_inc(x_ready, 1)
                dve.wait_ge(x_ready, s + 1)

            def outs(name, X, scale=None):
                def out(b):
                    leave(b + JOBS[name], tmp[:], None if scale is None else scale[:, bass.ds(b * 4, 4)])
                return out, lambda b: low_part(b + SPLITS[name], X, b, tmp[:])

            def rstd(i, n, width):
                dve.wait_ge(sq_done, i + 1)
                ts(t8[:, 0:n], ms[:, 0:n], 1.0 / width, EPS, ALU.mult, ALU.add).then_inc(ms_ready, 1)
                dve.wait_ge(root_ready, i + 1)
                y, q = rs[:, 0:n], small[:, 9, 0:n]
                step(nc.vector.reciprocal(y, y))
                step(tt(q, y, y, ALU.mult))
                step(tt(q, q, t8[:, 0:n], ALU.mult))
                step(ts(q, q, -0.5, 1.5, ALU.mult, ALU.add))
                step(tt(y, y, q, ALU.mult))

            def normed(dst, src):
                for t in range(NT):
                    step(ts(dst[:, t, :], src[:, t, :], rs[:, t:t + 1], None, ALU.mult))
                dve.sem_inc(xn_ready, 1)

            def norm_jobs(name, X, scale, shift=None):
                bufs = (tmp[:], stage_f)
                for g in range(5):
                    if g < 4:
                        leave(JOBS[name] + g, bufs[g % 2], scale[:, 4 * g:4 * g + 4],
                              None if shift is None else shift[:, 4 * g:4 * g + 4])
                    if g:
                        low_part(SPLITS[name] + g - 1, X, g - 1, bufs[(g - 1) % 2])

            def rotate(src, heads, width, half, i, at):
                v = src.rearrange("p t (h d) -> p t h d", h=heads)
                n = NT * heads * half
                ta, tb = (tmp[:].rearrange("p f t -> p (f t)")[:, k * 512:k * 512 + n]
                          .rearrange("p (t h d) -> p t h d", t=NT, h=heads) for k in range(2))
                for t in range(NT):
                    x1, x2 = v[:, t, :, 0:half], v[:, t, :, half:2 * half]
                    cosb, sinb = (rot[:, k, t:t + 1, at:at + half].to_broadcast([P, heads, half]) for k in range(2))
                    a, b = ta[:, t], tb[:, t]
                    step(tt(a, x1, cosb, ALU.mult))
                    step(tt(b, x2, sinb, ALU.mult))
                    step(tt(a, a, b, ALU.subtract))
                    step(tt(b, x1, sinb, ALU.mult))
                    step(tt(x2, x2, cosb, ALU.mult))
                    step(tt(x2, x2, b, ALU.add))
                    step(nc.vector.tensor_copy(x1, a))

            dve.wait_ge(in_landed, 16 * 5)
            step(nc.vector.tensor_copy(posf[:], posi[:]))
            cos, sin = rot[:, 0], rot[:, 1]
            ang, turns = (tmp[:].rearrange("p f t -> p (f t)")[:, k * 512:k * 512 + NT * 88]
                          .rearrange("p (t f) -> p t f", t=NT) for k in range(2))
            for t in range(NT):
                step(ts(ang[:, t, 0:24], freqs[:, 0:24], posf[:, 0, t:t + 1], None, ALU.mult))
                step(ts(ang[:, t, 24:88], freqs[:, 24:88], posf[:, 1, t:t + 1], None, ALU.mult))
            for dst, turn in ((cos, 0.25), (sin, 0.0)):
                step(ts(turns, ang, 1.0 / (2 * np.pi), turn, ALU.mult, ALU.add))
                step(ts(turns, turns, MAGIC, None, ALU.add))
                step(ts(turns, turns, MAGIC, None, ALU.subtract))
                step(stt(dst, turns, -TWO_PI[0], ang, ALU.mult, ALU.add))
                for part in TWO_PI[1:]:
                    step(stt(dst, turns, -part, dst, ALU.mult, ALU.add))
                step(ts(dst, dst, 2 * np.pi * turn, PI_CLAMP, ALU.add, ALU.min))
                step(ts(dst, dst, -PI_CLAMP, None, ALU.max))
            dve.sem_inc(sin_in, 1)

            dve.wait_ge(vec_tp, 1)
            step(nc.vector.tensor_copy(vec1[:, 0:120], ps[:, 4, 0:120]))
            step(nc.vector.tensor_copy(vec2[:, 0:64], ps[:, 5, 0:64]))
            dve.sem_inc(vec_done, 1)

            def clear(u):
                if not isinstance(u, int) or u >= 2:
                    dve.wait_ge(mod_sum, u - 1)
                zero = tri[:, P:P + 1].unsqueeze(1).to_broadcast([P, 1, D])
                nc.vector.tensor_copy(mod_acc[:, bass.ds(u % 2, 1), :], zero).then_inc(acc_zero, 1)

            def third(u):
                dve.wait_ge(bias_landed, u * 16 + 16)
                acc = mod_acc[:, bass.ds(u % 2, 1), :]
                for k in range(KC):
                    dve.wait_ge(mod_landed[k % 4], u * 64 + (k // 4 + 1) * 16)
                    stt(acc, mod_raw[:, k % 4:k % 4 + 1, :], csil[:, k:k + 1], acc, ALU.mult, ALU.add
                        ).then_inc(mod_used, 1)
                    dve.wait_ge(mod_used, u * KC + (k + 1))
                    if k == 8:
                        clear(u + 1)

            clear(0)
            dve.wait_ge(csil_ready, 1)
            third(0)
            with step.loop(1, 6, 0) as u:
                third(u)

            dve.wait_ge(vec_tp, 2)
            step(nc.vector.tensor_copy(vec3[:], ps[:, 4, 0:64]))
            for i, g in enumerate((G0, G1)):
                step(ts(scl[:, i, :], vec3[:, 32 * i + 16:32 * i + 32], 1.0, None, ALU.add))
                step(tt(scl[:, i, :], scl[:, i, :], g, ALU.mult))
            dve.sem_inc(scl_ready, 1)

            rstd(0, NT, D)
            normed(T0, T0)
            norm_jobs("norm0", XA, scl[:, 0, :], vec3[:, 0:16])
            for o in range(AHEAD):
                lo(0, o)

            phase("pool_v", None, *outs("pool_v", XB))
            phase("pool_gate")
            B0, A0, _ = PHASES["group"]
            out, low = outs("group", XA, PSC)
            for o in range(AHEAD, CPB + AHEAD):
                lo(B0, o)
                if o in (4, 6, 8, 10):
                    g = (o - 4) // 2
                    dve.wait_ge(acc_free, A0 + g + 1)
                    tt(stage[:], stage[:], T1[:, :, NBLK * g:NBLK * g + NBLK], ALU.mult).then_inc(staged, 1)
                if o in (7, 9):
                    out((o - 7) // 2)
                if o in (8, 10):
                    low((o - 8) // 2)
            for g in (2, 3):
                out(g)
                low(g)

            def add_residual(name, k, dst):
                def each(b, A):
                    dve.wait_ge(acc_free, A + 1)
                    dve.wait_ge(wide_landed, 16 * k)
                    dve.wait_ge(res_landed, 16 * k)
                    cols = bass.ds(b * NBLK, NBLK)
                    step(tt(stage[:], stage[:], wide[:, cols].unsqueeze(1).to_broadcast([P, NT, NBLK]), ALU.mult))
                    tt(dst[:, :, cols], dst[:, :, cols], stage[:], ALU.add).then_inc(combined, 1)
                return each

            phase("pool_out", add_residual("pool_out", 1, T2), per=1)

            rstd(1, NT, D)
            normed(T0, T2)
            norm_jobs("norm1", XB, scl[:, 1, :], vec3[:, 32:48])

            def index_q(b, A):
                dve.wait_ge(acc_free, A + 1)
                rotate(stage[:], 8, 64, FRQI, 0, FRQ1)
                dve.sem_inc(staged, 1)

            n0 = JOBS["idx_q"]
            phase("idx_q", index_q, lambda b: leave(b + n0, qi_t[:, bass.ds(b * 4, 4), :]), lambda b: None,
                  per=14)
            B0, A0, _ = PHASES["idx_kw"]
            blk(B0)
            dve.wait_ge(acc_free, A0 + 1)
            rotate(stage[:, :, 0:64], 1, 64, FRQI, 0, FRQ1)
            step(ts(idx_w[:], stage[:, :, 64:80], IDX_HEADS ** -0.5 * 64 ** -0.5, None, ALU.mult))
            nc.vector.tensor_copy(stage[:, :, 64:128], stage[:, :, 0:64]).then_inc(staged, 1)
            n = JOBS["idx_kw"]
            dve.wait_ge(tp_ready, n + 1)
            nc.vector.tensor_copy(ki_t, ps[:, 4 + n % 2 * 2, 0:S]).then_inc(tp_evac, 1)
            step(nc.vector.tensor_copy(score, tri))
            for h in range(IDX_HEADS):
                dve.wait_ge(relu_ready, h + 1)
                for t, (a, z) in enumerate(((0, P), (P, CAUS))):
                    step(stt(score[:, a:z], probs[:, h % 2, a:z], idx_w[:, t, h:h + 1], score[:, a:z],
                             ALU.mult, ALU.add))
                dve.sem_inc(sc_used, 1)

            def carry():
                nc.vector.tensor_copy(small[:, 10, 0:1], posf[:, 0, 0:1])

            def query_key(b, A):
                dve.wait_ge(acc_free, A + 1)
                rotate(stage[:], 4, HD, FRQ1, 0, 0)
                for t, (a, z) in enumerate(((0, P), (P, CAUS))):
                    carry()
                    step(nc.vector.max(best[:, t, :], score[:, a:z]))
                    carry()
                    step(nc.vector.match_replace(score[:, a:z], best[:, t, :], score[:, a:z], TAKEN))
                dve.sem_inc(staged, 1)

            n1 = JOBS["qk"]
            phase("qk", query_key, lambda b: leave(b + n1, qk_t[:, bass.ds(b * 4, 4), :]), lambda b: None,
                  per=18)
            step(ts(score, score, 0.5 * (TAKEN + FAR), UNPICKED, ALU.is_gt, ALU.mult))
            step(tt(pick[:], score, tri, ALU.add))
            dve.sem_inc(picked, 1)
            phase("v")
            phase("gate")

            def attention(h0, e0, heads, name, g0, mask, gate):
                for i in range(heads + 4):
                    if i < heads:
                        h, b = h0 + i, i % 2
                        dve.wait_ge(lg_ready, h + 1)
                        if i >= 2:
                            dve.wait_ge(pt_ready, h - 1)
                        for t, (a, z) in enumerate(((0, P), (P, CAUS))):
                            step(nc.vector.tensor_tensor_reduce(
                                out=probs[:, b, a:z], in0=ps[:, 4 + b, a:z], in1=mask[:, a:z], scale=1.0,
                                scalar=FAR, op0=ALU.add, op1=ALU.max, accum_out=mx[:, b, t:t + 1]))
                        ts(nmx[:, b, :], mx[:, b, :], -(HD ** -0.5), None, ALU.mult).then_inc(masked, 1)
                    if i >= 6 and i % 4 == 2:
                        n = (i - 6) // 4
                        leave(JOBS[name] + n, x_tmp, bank=2)
                    if i >= 6 and i % 4 == 3:
                        low_part(SPLITS[name] + (i - 7) // 4, XA, g0 + (i - 7) // 4, x_tmp)
                    if 2 <= i < heads + 2:
                        j = i - 2
                        b = j % 2
                        dve.wait_ge(exp_ready, e0 + j + 1)
                        step(nc.vector.reciprocal(rden[:, b, :], den[:, j % 4, :]))
                        dve.wait_ge(pv_ready, h0 + j + 1)
                        for t in range(NT):
                            dst, src = stage[:, t, j % 4 * HD:j % 4 * HD + HD], ps[:, b, t * HD:t * HD + HD]
                            if gate is None:
                                step(ts(dst, src, rden[:, b, t:t + 1], None, ALU.mult))
                            else:
                                step(stt(dst, src, rden[:, b, t:t + 1], gate[:, t, j * HD:j * HD + HD],
                                         ALU.mult, ALU.mult))
                        dve.sem_inc(o_done, 1)
                        if j % 4 == 3:
                            dve.sem_inc(staged, 1)

            dve.wait_ge(acc_free, PHASES["gate"][1] + 4)
            attention(0, 0, DSA_HEADS, "attn", 0, pick[:], T3)
            phase("attn_out", add_residual("attn_out", 2, T0), per=1)

            rstd(2, NT, D)
            dve.wait_ge(wide_landed, 48)
            for t in range(NT):
                step(stt(T0[:, t, :], T0[:, t, :], rs[:, t:t + 1], wide[:], ALU.mult, ALU.mult))
            dve.sem_inc(res_done, 1)
            rstd(3, NT, D)
            normed(T1, T0)
            norm_jobs("norm2", XB, MIXP)

            def conv(b):
                dve.wait_ge(tp_ready, b + (JOBS["m_qk"] + 1))
                p0 = job_bank(b + JOBS["m_qk"])
                u = ps[:, p0:p0 + 2, :].rearrange("p b (f t) -> p (b f) t", t=S)
                for f in range(4):
                    col = b * 4 + f
                    w = [vec2[:, bass.ds(col + 16 * k, 1)] for k in range(4)]
                    step(ts(tmp[:, f, :], u[:, f, :], w[3], CVB[:, bass.ds(col, 1)], ALU.mult, ALU.add))
                    for k in range(3):
                        lag = 3 - k
                        step(stt(tmp[:, f, lag:S], u[:, f, 0:S - lag], w[k], tmp[:, f, lag:S], ALU.mult, ALU.add))
                dve.sem_inc(tp_evac, 1)
                dve.sem_inc(conv_in, 1)

            phase("m_qk", None, conv, lambda b: dve.wait_ge(conv_done, b + 1), per=16)
            phase("m_v")
            phase("m_o")
            B0, A0, _ = PHASES["m_if"]
            blk(B0)
            dve.wait_ge(acc_free, A0 + 1)
            for k, dst in ((0, gate_i), (1, gate_f)):
                step(tt(dst, stage[:, :, 4 * k:4 * k + 4], ifb[:, 4 * k:4 * k + 4].unsqueeze(1)
                        .to_broadcast([P, NT, 4]), ALU.add))
            step(ts(gate_u, gate_f, -1.0, None, ALU.mult))
            step(tt(gate_u, gate_u, gate_f, ALU.min))
            step(ts(m_e, gate_f, 0.0, None, ALU.min))
            dve.sem_inc(g_in, 1)
            dve.wait_ge(g_act, 1)
            step(ts(gate_w, gate_u, 1.0, None, ALU.add))
            dve.sem_inc(g_in, 1)
            step(ts(cum_f, gate_w, -1.0, 1e-30, ALU.add, ALU.max))
            step(nc.vector.reciprocal(cum_f, cum_f))
            step(tt(cum_f, cum_f, gate_u, ALU.mult))
            dve.wait_ge(g_act, 2)
            step(tt(gate_f, gate_f, cum_f, ALU.mult))
            step(tt(gate_f, m_e, gate_f, ALU.subtract))
            dve.sem_inc(g_in, 1)
            dve.wait_ge(g_mm, 1)
            step(nc.vector.tensor_copy(cum_f, ps[:, 2, 0:8].rearrange("p (t h) -> p t h", t=NT)))
            step(tt(m_e, gate_i, cum_f, ALU.subtract))
            for t in range(NT):
                for h in range(M_HEADS):
                    step(ts(m_diag[:, t, h, :], ident, m_e[:, t, h:h + 1], None, ALU.mult))
            dve.sem_inc(g_in, 1)
            dve.wait_ge(g_mm, 2)
            for h in range(M_HEADS):
                for t, (a, z) in enumerate(((0, P), (P, CAUS))):
                    at = h % 2 * S
                    step(nc.vector.tensor_tensor_reduce(
                        out=m_dec[:, h, a:z], in0=ps[:, 4 + h // 2, at:at + z - a], in1=tri[:, a:z], scale=1.0,
                        scalar=0.0, op0=ALU.add, op1=ALU.max, accum_out=m_max[:, t, h:h + 1]))
            step(ts(m_nmax, m_max, -1.0, None, ALU.mult))
            step(tt(m_floor, m_max, cum_f, ALU.add))
            dve.sem_inc(g_dve, 1)
            dve.wait_ge(g_act, 3)
            for i in range(M_HEADS + 2):
                if i < M_HEADS:
                    dve.wait_ge(lg_ready, DSA_HEADS + i + 1)
                    if i >= 2:
                        dve.wait_ge(pt_ready, DSA_HEADS + i - 1)
                    for t, (a, z) in enumerate(((0, P), (P, CAUS))):
                        step(nc.vector.tensor_tensor_reduce(
                            out=probs[:, i % 2, a:z], in0=ps[:, 4 + i % 2, a:z], in1=m_dec[:, i, a:z], scale=S ** -0.5,
                            scalar=0.0, op0=ALU.mult, op1=ALU.add, accum_out=den[:, i % 2, t:t + 1]))
                    dve.sem_inc(masked, 1)
                if i >= 2:
                    j = i - 2
                    dve.wait_ge(pv_ready, DSA_HEADS + j + 1)
                    for t in range(NT):
                        step(ts(m_num[:, j, t, :], ps[:, j % 2, t * S:t * S + S], rden[:, j % 2, t:t + 1], None,
                                ALU.mult))
                    dve.sem_inc(o_done, 1)
                if i < M_HEADS:
                    step(ts(rden[:, i % 2, :], den[:, i % 2, :], -1.0, None, ALU.mult))
                    step(tt(rden[:, i % 2, :], rden[:, i % 2, :], den[:, i % 2, :], ALU.max))
                    step(tt(rden[:, i % 2, :], rden[:, i % 2, :], m_floor[:, :, i], ALU.max))
                    step(nc.vector.reciprocal(rden[:, i % 2, :], rden[:, i % 2, :]))
            rstd(4, NT * M_HEADS, S)
            for n in range(2):
                if n:
                    dve.wait_ge(tp_ready, JOBS["mlstm"] + n)
                for t in range(NT):
                    for h in range(2):
                        j = 2 * n + h
                        step(stt(stage[:, t, h * S:h * S + S], m_num[:, j, t, :],
                                 rs[:, t * M_HEADS + j:t * M_HEADS + j + 1], m_o[:, t, j * S:j * S + S],
                                 ALU.mult, ALU.mult))
                dve.sem_inc(staged, 1)
                leave(JOBS["mlstm"] + n, x_tmp, MLN[:, 4 * n:4 * n + 4], bank=2)
                low_part(SPLITS["mlstm"] + n, XA, n, x_tmp)

            def rotary_full(b, A):
                dve.wait_ge(acc_free, A + 1)
                rotate(stage[:], 4, HD, FRQ2, 1, FRQ1 + FRQI)
                dve.sem_inc(staged, 1)

            n2 = JOBS["a_qk"]
            phase("a_qk", rotary_full, lambda b: leave(b + n2, feat(2)[:, bass.ds(b * 4, 4), :]), lambda b: None,
                  per=14)
            phase("a_v")
            attention(DSA_HEADS + M_HEADS, DSA_HEADS, MOBA_HEADS, "moba", 2, tri, None)
            phase("g_m")
            phase("g_a")

            B0, A0, n = PHASES["branch"]
            out, low = outs("branch", XB)

            def branch(b, first=False):
                B, A = b + B0, b * 2 + A0
                cols = bass.ds(b * NBLK, NBLK)
                for o in range(AHEAD, CPB + AHEAD):
                    lo(B, o)
                    if o == 5 and not first:
                        out(b - 1)
                    if o == 6:
                        if not first:
                            low(b - 1)
                        dve.wait_ge(acc_free, A + 1)
                        step(tt(stage[:], stage[:], T0[:, :, cols], ALU.mult))
                dve.wait_ge(acc_free, A + 2)
                step(tt(tmp_t, tmp_t, T1[:, :, cols], ALU.mult))
                tt(stage[:], stage[:], tmp_t, ALU.add).then_inc(staged, 1)

            branch(0, first=True)
            with step.loop(1, n, 2) as b:
                branch(b)
            out(3)
            low(3)
            phase("mix_out")

            rstd(5, NT, D)
            dve.wait_ge(wide_landed, 64)
            dve.wait_ge(res_landed, 48)
            for t in range(NT):
                step(stt(T2[:, t, :], T2[:, t, :], rs[:, t:t + 1], wide[:], ALU.mult, ALU.mult))
                step(tt(T3[:, t, :], T3[:, t, :], T2[:, t, :], ALU.add))
            dve.sem_inc(res_done, 1)
            rstd(6, NT, D)
            normed(T2, T3)
            norm_jobs("norm3", XA, FFNP)
            step(nc.vector.memset(T1[:], 0.0))

            J, X0, C0, S0 = JOBS["ffn"], SPLITS["ffn"], COMBINED["ffn"], STAGED["ffn"]

            def up(e, half, B, A, after=None):
                for h in range(2):
                    hooks = None
                    if h == 1 or after == "up":
                        j, g = e * 2 + (h - 1), (2 * half + h - 1) % 4
                        hooks = {5: lambda: leave(j + J, tmp[:]), 6: lambda: low_part(j + X0, XB, g, tmp[:])}
                    blk(B + h, hooks)
                    dve.wait_ge(acc_free, A + (h + 1))
                    tt(stage[:], stage[:], stage[:], ALU.mult).then_inc(staged, 1)

            def dn(e, half, B, A, last=False):
                def add(q):
                    dve.wait_ge(acc_free, A + (q + 1))
                    y = T1[:, :, q * NBLK:q * NBLK + NBLK]
                    tt(y, y, stage[:], ALU.add).then_inc(combined, 1)

                def mid():
                    if not last:
                        low_part(e * 2 + (X0 + 3), XB, 2 * (1 - half) + 1, tmp[:])
                    add(0)

                blk(B, {5: (lambda: None) if last else (lambda: leave(e * 2 + (J + 3), tmp[:])),
                        6: mid, 10: lambda: add(1)})
                blk(B + 1, {6: lambda: add(2), 10: lambda: add(3)}, last=last)
                if last:
                    add(3)

            up(0, 0, FB, FA, after="norm")
            up(1, 1, FB + 2, FA + 2, after="up")
            dn(0, 0, FB + 4, FA + 4)
            with step.loop(0, 3, 0) as i:
                up(i * 2 + 2, 0, i * 8 + (FB + 6), i * 12 + (FA + 8))
                dn(i * 2 + 1, 1, i * 8 + (FB + 8), i * 12 + (FA + 10))
                up(i * 2 + 3, 1, i * 8 + (FB + 10), i * 12 + (FA + 14))
                dn(i * 2 + 2, 0, i * 8 + (FB + 12), i * 12 + (FA + 16))
            dn(7, 1, FB + 30, FA + 44, last=True)

            rstd(7, NT, D)
            dve.wait_ge(wide_landed, 80)
            for t in range(NT):
                step(stt(T1[:, t, :], T1[:, t, :], rs[:, t:t + 1], wide[:], ALU.mult, ALU.mult))
                tt(T1[:, t, :], T1[:, t, :], T3[:, t, :], ALU.add).then_inc(out_done, 1)

        @block.tensor
        def _(pe):
            mm = nc.tensor.matmul

            def chunk(B, j, X, k0, A, first, last, cols=NBLK):
                pe.wait_ge(lo_ready, B * CPB + (j + 1))
                bank = (A % 2) * 2
                for k in range(KPC):
                    for t in range(NT):
                        x_hi, x_lo = (v[:, k0 + k, t * P:(t + 1) * P] for v in X)
                        h, l = (w[:, j % SPL, k, 0:cols] for w in (w_hi, w_lo))
                        dst = ps[:, bank + t, 0:cols]
                        mm(dst, x_hi, h, start=first and k == 0, stop=False)
                        mm(dst, x_hi, l, start=False, stop=False)
                        ins = mm(dst, x_lo, h, start=False, stop=last and k == KPC - 1)
                ins.then_inc(w_used, 1)

            def blk(B, A, X, free, mid=None, cols=NBLK):
                if free:
                    pe.wait_ge(acc_free, A - 1)
                for j in range(CPB):
                    chunk(B, j, X, KPC * j, A, j == 0, j == CPB - 1, cols)
                    if j == 3 and mid:
                        mid()

            def phase(name, X, job=None, cols=NBLK):
                B0, A0, n = PHASES[name]
                blk(B0, A0, X, A0 >= 2, cols=cols)
                if n > 1:
                    if A0 < 2:
                        blk(1 + B0, 1 + A0, X, False, (lambda: job(0)) if job else None)
                    with pe.Fori(2 if A0 < 2 else 1, n) as b:
                        blk(b + B0, b + A0, X, True, (lambda: job(b - 1)) if job else None)
                if job:
                    job(n - 1)

            def job(n, src, ready, value, bank=None):
                pe.wait_ge(ready, value)
                if bank is not None or not isinstance(n, int):
                    pe.wait_ge(tp_evac, n)
                elif n >= 2:
                    pe.wait_ge(tp_evac, n - 1)
                p0 = job_bank(n) if bank is None else bank
                for f in range(4):
                    for t in range(NT):
                        at = f % 2 * S + t * P
                        ins = nc.tensor.transpose(ps[:, p0 + f // 2, at:at + P], src[:, t, f * P:(f + 1) * P], ident)
                ins.then_inc(tp_ready, 1)

            def stage_job(name):
                return lambda b: job(b + JOBS[name], stage, staged, b + (STAGED[name] + 1))

            def norm_jobs(name, i, src):
                for g in range(4):
                    job(JOBS[name] + g, src[:, :, g * NBLK:(g + 1) * NBLK], xn_ready, i + 1)

            pe.wait_ge(vec_landed, 16 * 12)
            pe.wait_ge(in_landed, 16 * 5)
            nc.tensor.transpose(ps[:, 4, 0:120], stage[0:120, 0, 0:P], ident[0:120, 0:120])
            nc.tensor.transpose(ps[:, 5, 0:64], stage[0:64, 1, 0:P], ident[0:64, 0:64]).then_inc(vec_tp, 1)

            def total(u):
                pe.wait_ge(mod_used, u * KC + KC)
                if not isinstance(u, int):
                    pe.wait_ge(row_ready, u)
                for q in range(4):
                    ins = mm(ps[0:1, q:q + 1, :], ones[:, 0:1],
                             mod_acc[:, bass.ds(u % 2, 1), q * NBLK:(q + 1) * NBLK], start=True, stop=True)
                ins.then_inc(mod_sum, 1)

            total(0)
            with pe.Fori(1, 6) as u:
                total(u)
            pe.wait_ge(rows_back, 64)
            pe.wait_ge(vec_done, 1)
            nc.tensor.transpose(ps[:, 4, 0:64], stage[0:64, 0, P:2 * P], ident[0:64, 0:64]).then_inc(vec_tp, 1)
            pe.wait_ge(scl_ready, 1)
            norm_jobs("norm0", 0, T0)

            def pool(b):
                n = b + JOBS["pool_v"]
                pe.wait_ge(acc_free, b + (PHASES["pool_v"][1] + 1))
                pe.wait_ge(tp_evac, n)
                p0 = job_bank(n)
                for f in range(4):
                    for u in range(NT):
                        ins = mm(ps[:, p0 + f // 2, f % 2 * S:f % 2 * S + S],
                                 stage[:, u, f * P:(f + 1) * P], amat[:, bass.ds(b, 1), u, :].rearrange("p a t -> p (a t)"),
                                 start=u == 0, stop=u == NT - 1)
                ins.then_inc(tp_ready, 1)

            pe.wait_ge(x_ready, SPLITS["norm0"] + 4)
            pe.wait_ge(row_ready, 6)
            pe.wait_ge(amat_landed, 16)
            phase("pool_v", XA, pool)
            phase("pool_gate", XA)
            B0, A0, _ = PHASES["group"]
            pe.wait_ge(x_ready, SPLITS["pool_v"] + 4)
            group_job = stage_job("group")
            for j in range(CPB):
                if j % 2 == 0:
                    pe.wait_ge(acc_free, A0 + j // 2 - 1)
                chunk(B0, j, XB, KPC * j, A0 + j // 2, j % 2 == 0, j % 2 == 1)
                if j in (5, 7):
                    group_job((j - 5) // 2)
            group_job(2)
            group_job(3)
            pe.wait_ge(x_ready, SPLITS["group"] + 4)
            phase("pool_out", XA)

            norm_jobs("norm1", 1, T0)
            pe.wait_ge(x_ready, SPLITS["norm1"] + 4)
            phase("idx_q", XB, stage_job("idx_q"))
            phase("idx_kw", XB, cols=80)
            n = JOBS["idx_kw"]
            pe.wait_ge(staged, STAGED["idx_kw"] + 1)
            pe.wait_ge(tp_evac, n - 1)
            for t in range(NT):
                ins = nc.tensor.transpose(ps[:, 4 + n % 2 * 2, t * P:(t + 1) * P], stage[:, t, 0:P], ident)
            ins.then_inc(tp_ready, 1)
            pe.wait_ge(tp_evac, n + 1)
            for h in range(IDX_HEADS):
                if h >= 4:
                    pe.wait_ge(relu_ready, h - 3)
                rows = slice(h % 2 * 64, h % 2 * 64 + 64)
                for t, (a, z) in enumerate(((0, P), (P, CAUS))):
                    ins = mm(ps[:, 4 + h % 4, a:z], qi_t[rows, h // 2, t * P:(t + 1) * P], ki_t[rows, 0:z - a],
                             start=True, stop=True)
                ins.then_inc(sc_ready, 1)
            pe.wait_ge(relu_ready, IDX_HEADS)
            phase("qk", XB, stage_job("qk"))
            phase("v", XB)
            phase("gate", XB)

            def attention(h0, e0, heads, name, q, k, v, ready, value, rows_of=1, width=HD):
                for i in range(heads + 3):
                    if i < heads:
                        h = h0 + i
                        if i >= 2:
                            pe.wait_ge(masked, h - 1)
                        for t, (a, z) in enumerate(((0, P), (P, CAUS))):
                            for r in range(rows_of):
                                ins = mm(ps[:, 4 + i % 2, a:z], q(i, r)[:, t * P:(t + 1) * P], k(i, r)[:, 0:z - a],
                                         start=r == 0, stop=r == rows_of - 1)
                        ins.then_inc(lg_ready, 1)
                    if 1 <= i <= heads:
                        h, b = h0 + i - 1, (i - 1) % 2
                        pe.wait_ge(ready, value + i)
                        if i >= 3:
                            pe.wait_ge(pt_copied, h - 1)
                        for dst, src in ((0, 0), (P, P), (2 * P, 2 * P)):
                            ins = nc.tensor.transpose(ps[:, 6 + b, dst:dst + P], probs[:, b, src:src + P], ident)
                        ins.then_inc(pt_ready, 1)
                    if name and i >= 6 and i % 4 == 2:
                        n = (i - 6) // 4
                        job(JOBS[name] + n, stage, staged, STAGED[name] + n + 1, bank=2)
                    if 2 <= i < heads + 2:
                        h, b = h0 + i - 2, (i - 2) % 2
                        pe.wait_ge(pt_copied, h + 1)
                        if i >= 4:
                            pe.wait_ge(o_done, h - 1)
                        mm(ps[:, b, 0:width], probs_t[:, b, 0:P], v(i - 2, 0), start=True, stop=True)
                        mm(ps[:, b, width:2 * width], probs_t[:, b, P:2 * P], v(i - 2, 0), start=True, stop=False)
                        mm(ps[:, b, width:2 * width], probs_t[:, b, 2 * P:CAUS], v(i - 2, 1), start=False, stop=True
                           ).then_inc(pv_ready, 1)

            pe.wait_ge(acc_free, PHASES["gate"][1] + 4)
            pe.wait_ge(tp_evac, JOBS["qk"] + 8)
            attention(0, 0, DSA_HEADS, "attn", lambda i, r: qk_t[:, i, :], lambda i, r: qk_t[:, DSA_HEADS + i, :],
                      lambda i, u: T2[:, u, i * HD:(i + 1) * HD], exp_ready, 0)
            pe.wait_ge(x_ready, SPLITS["attn"] + 4)
            phase("attn_out", XA)

            norm_jobs("norm2", 2, T1)
            pe.wait_ge(x_ready, SPLITS["norm2"] + 4)
            a0 = PHASES["m_qk"][1]
            phase("m_qk", XB, lambda b: job(b + JOBS["m_qk"], stage, acc_free, b + (a0 + 1)))
            phase("m_v", XB)
            phase("m_o", XB)
            phase("m_if", XB, cols=8)

            pe.wait_ge(g_in, 3)
            pe.wait_ge(acc_free, PHASES["m_if"][1] + 1)
            mm(ps[:, 2, 0:4], cum, gate_f[:, 0, :], start=True, stop=True)
            mm(ps[:, 2, 4:8], cum, gate_f[:, 1, :], start=True, stop=False)
            mm(ps[:, 2, 4:8], ones, gate_f[:, 0, :], start=False, stop=True).then_inc(g_mm, 1)
            pe.wait_ge(g_in, 4)
            pe.wait_ge(conv_done, 4)
            for h in range(M_HEADS):
                for t in range(NT):
                    at = h % 2 * S + t * P
                    ins = mm(ps[:, 4 + h // 2, at:at + P], ones, m_diag[:, t, h, :], start=True, stop=True)
            ins.then_inc(g_mm, 1)
            pe.wait_ge(g_dve, 1)
            mq = feat(0)
            attention(DSA_HEADS, 0, M_HEADS, None, lambda i, r: mq[:, 2 * i + r, :], lambda i, r: mq[:, 8 + 2 * i + r, :],
                      lambda i, u: m_v[:, u, i * S:(i + 1) * S], masked, DSA_HEADS, rows_of=2, width=S)
            for n in range(2):
                job(JOBS["mlstm"] + n, stage, staged, STAGED["mlstm"] + n + 1, bank=2)

            pe.wait_ge(o_done, DSA_HEADS + M_HEADS)
            pe.wait_ge(tp_evac, JOBS["mlstm"] + 2)
            phase("a_qk", XB, stage_job("a_qk"))
            phase("a_v", XB)
            pe.wait_ge(acc_free, PHASES["a_v"][1] + 2)
            pe.wait_ge(tp_evac, JOBS["a_qk"] + 4)
            aq = feat(2)
            attention(DSA_HEADS + M_HEADS, DSA_HEADS, MOBA_HEADS, "moba", lambda i, r: aq[:, i, :],
                      lambda i, r: aq[:, MOBA_HEADS + i, :], lambda i, u: a_v[:, u, i * HD:(i + 1) * HD],
                      exp_ready, DSA_HEADS)
            pe.wait_ge(o_done, DSA_HEADS + M_HEADS + MOBA_HEADS)
            pe.wait_ge(tp_evac, JOBS["moba"] + 2)
            phase("g_m", XB)
            phase("g_a", XB)

            pe.wait_ge(x_ready, SPLITS["moba"] + 2)
            B0, A0, n = PHASES["branch"]
            branch_job = stage_job("branch")

            def branch(b, first=False):
                for half in range(2):
                    A = b * 2 + (A0 + half)
                    pe.wait_ge(acc_free, A - 1)
                    for j in range(4):
                        chunk(b + B0, 4 * half + j, XA, 8 * half + KPC * j, A, j == 0, j == 3)
                    if half == 0 and not first:
                        branch_job(b - 1)

            branch(0, first=True)
            with pe.Fori(1, n) as b:
                branch(b)
            branch_job(3)
            pe.wait_ge(x_ready, SPLITS["branch"] + 4)
            phase("mix_out", XB)

            norm_jobs("norm3", 3, T2)
            pe.wait_ge(x_ready, SPLITS["norm3"] + 4)
            ffn_job = stage_job("ffn")
            X0 = SPLITS["ffn"]

            def up(e, B, A, after=None):
                for h in range(2):
                    blk(B + h, A + h, XA, True, (lambda: ffn_job(e * 2 + (h - 1))) if h == 1 or after == "up" else None)

            def dn(e, half, B, A, last=False):
                pe.wait_ge(x_ready, e * 2 + (X0 + 2))
                for q in range(4):
                    pe.wait_ge(acc_free, A + (q - 1))
                    for j in range(4):
                        chunk(B + q // 2, 4 * (q % 2) + j, XB, 8 * half + KPC * j, A + q, j == 0, j == 3)
                    if q == 0 and not last:
                        ffn_job(e * 2 + 3)

            up(0, FB, FA, after="norm")
            up(1, FB + 2, FA + 2, after="up")
            dn(0, 0, FB + 4, FA + 4)
            with pe.Fori(0, 3) as i:
                up(i * 2 + 2, i * 8 + (FB + 6), i * 12 + (FA + 8))
                dn(i * 2 + 1, 1, i * 8 + (FB + 8), i * 12 + (FA + 10))
                up(i * 2 + 3, i * 8 + (FB + 10), i * 12 + (FA + 14))
                dn(i * 2 + 2, 0, i * 8 + (FB + 12), i * 12 + (FA + 16))
            dn(7, 1, FB + 30, FA + 44, last=True)


_INS = [
    "x", "c", "positions", "norm_g", "mod_w", "mod_b", "pool_w_in", "pool_w_grp", "pool_scale", "pool_w_out",
    "attn_w_in", "attn_w_out", "final_g", "positions_2", "norm_mix_pre_2", "w_in_2", "conv_w_2", "conv_b_2",
    "i_bias_2", "f_bias_2", "mlstm_norm_2", "w_branch_m_2", "w_branch_a_2", "w_out_2", "norm_mix_post_2",
    "norm_ffn_pre_2", "w_up_2", "w_down_2", "norm_ffn_post_2",
]


def shape_constants():
    far = np.float32(FAR)
    con = np.zeros((P, C_ALL), np.float32)
    con[:, C_ID:C_ID + P] = np.eye(P)
    key, query = np.arange(P)[None, :], np.arange(P)[:, None]
    triangle = np.where(key <= query, np.float32(0), far)
    con[:, C_TRI:C_TRI + P] = triangle
    con[:, C_TRI + 2 * P:C_TRI + 3 * P] = triangle
    con[:, C_CUM:C_CUM + P] = (query <= key)
    con[:, C_ONE:C_ONE + P] = 1.0
    col = C_FRQ
    for theta, width, half in ((500000.0, 32, FRQ1), (500000.0, 16, FRQI), (10000.0, 128, FRQ2)):
        con[:, col:col + half] = theta ** (-np.arange(half) * 2.0 / width)
        col += half
    win = np.zeros((len(WINDOWS), S, S), np.float64)
    for g, w in enumerate(WINDOWS):
        for t in range(S):
            lo = max(t + 1 - w, 0)
            win[g, lo:t + 1, t] = 1.0 / (t + 1 - lo)
            win[g, t, t] -= 1.0
    win = win.astype(np.float32).reshape(len(WINDOWS), NT, P, S).transpose(2, 0, 1, 3)
    return con, np.ascontiguousarray(win)


def kernel(**inputs):
    import concourse.bacc as bacc
    from concourse.bass_utils import run_bass_kernel_spmd

    nc = bacc.Bacc("TRN2", target_bir_lowering=False, num_devices=1, dynamic_dma_scratch_size=1024)
    arrays, args = {}, {}
    for name in _INS:
        a = np.ascontiguousarray(inputs[name])
        arrays[f"in_{name}"] = a
        args[name] = nc.dram_tensor(f"in_{name}", a.shape, mybir.dt.from_np(a.dtype), kind="ExternalInput").ap()
    for name, a in zip(("consts", "windows"), shape_constants()):
        arrays[f"in_{name}"] = a
        args[name] = nc.dram_tensor(f"in_{name}", a.shape, F32, kind="ExternalInput").ap()
    args["mod_rows"] = nc.dram_tensor("mod_rows", (6, D), F32).ap()
    args["resid"] = nc.dram_tensor("resid", (2, S, D), F32).ap()
    args["out"] = nc.dram_tensor("out", (1, S, D), F32, kind="ExternalOutput").ap()
    build(nc, **args)
    r = run_bass_kernel_spmd(nc, [arrays], core_ids=[0])
    return r.results[0]["out"]
```

```python
from contextlib import ExitStack, contextmanager

import concourse.bass as bass
import numpy as np
from concourse import mybir

F32 = mybir.dt.float32
F32R = mybir.dt.float32r
I32 = mybir.dt.int32
ALU = mybir.AluOpType
ACT = mybir.ActivationFunctionType

P = 128
S = 256
NT = S // P
D = 2048
KC = D // P
NBLK = 512
KPC = 2
CPB = KC // KPC
RAW = 8
SPL = 4
AHEAD = 3
EPS = 1e-6
HD = 128
CAUS = P + S
FAR = -3.0e38
TAKEN = -3.3e38
UNPICKED = -1.0e30
MAGIC = 12582912.0
TWO_PI = (6.28125, 0.0019350051879882812, 3.019915981956752e-07)
PI_CLAMP = 3.1415925
WINDOWS = (2, 4, 8, 16)
TOPK = 64
DSA_HEADS, MOBA_HEADS, M_HEADS, IDX_HEADS = 16, 8, 4, 16
IDX_COL = 4 * D
N_FFN = 8

C_ID, C_TRI, C_CUM, C_ONE, C_FRQ = 0, 128, 512, 640, 768
FRQ1, FRQI, FRQ2 = 16, 8, 64
C_ALL = C_FRQ + FRQ1 + FRQI + FRQ2

PHASES = {}


def _plan():
    b = a = 0
    for name, blocks, accs in (
        ("pool_v", 4, 4), ("pool_gate", 4, 4), ("group", 1, 4), ("pool_out", 4, 4), ("idx_q", 2, 2), ("idx_kw", 1, 1),
        ("qk", 8, 8), ("v", 4, 4), ("gate", 4, 4), ("attn_out", 4, 4), ("m_qk", 4, 4), ("m_v", 2, 2), ("m_o", 2, 2),
        ("m_if", 1, 1), ("a_qk", 4, 4), ("a_v", 2, 2), ("g_m", 4, 4), ("g_a", 4, 4), ("branch", 4, 8),
        ("mix_out", 4, 4), ("ffn", 32, 48),
    ):
        PHASES[name] = (b, a, blocks)
        b, a = b + blocks, a + accs
    return b


N_BLOCKS = _plan()
RIDERS = {"pool_v": 2, "pool_gate": 3, "pool_out": 4, "v": 5}
RIDE = {u: 2 * KC + 2 * KC * (u - 2) for u in RIDERS.values()}

JOBS, SPLITS = {}, {}


def _jobs():
    n = s = 0
    for name, jobs, split in (
        ("norm0", 4, True), ("pool_v", 4, True), ("group", 4, True), ("norm1", 4, True), ("idx_q", 2, False),
        ("idx_kw", 1, False), ("qk", 8, False), ("attn", 4, True), ("norm2", 4, True), ("m_qk", 4, False),
        ("mlstm", 2, True), ("a_qk", 4, False), ("moba", 2, True), ("branch", 4, True), ("norm3", 4, True),
        ("ffn", 16, True),
    ):
        JOBS[name], SPLITS[name] = n, s
        n, s = n + jobs, s + (jobs if split else 0)


_jobs()
STAGED = {}


def _staged():
    n = 0
    for name, jobs in (("group", 4), ("idx_q", 2), ("idx_kw", 1), ("qk", 8), ("attn", 4), ("mlstm", 2), ("a_qk", 4),
                       ("moba", 2), ("branch", 4), ("ffn", 16)):
        STAGED[name] = n
        n += jobs


_staged()
COMBINED = {"pool_out": 0, "attn_out": 4, "ffn": 8}


class Chain:

    def __init__(self, eng, sem):
        self.eng, self.sem, self.n, self.off = eng, sem, 0, 0

    def __call__(self, ins):
        ins.then_inc(self.sem, 1)
        self.n += 1
        self.eng.wait_ge(self.sem, self.off + self.n)

    @contextmanager
    def loop(self, first, last, per):
        start = self.n
        with self.eng.Fori(first, last) as b:
            self.off = (b - first) * per if per else 0
            yield b
        assert self.n - start == per, f"{self.n - start} steps, not {per}"
        self.n, self.off = start + per * (last - first), 0


def build(nc, x, c, positions, norm_g, mod_w, mod_b, pool_w_in, pool_w_grp, pool_scale, pool_w_out, attn_w_in,
          attn_w_out, final_g, positions_2, norm_mix_pre_2, w_in_2, conv_w_2, conv_b_2, i_bias_2, f_bias_2,
          mlstm_norm_2, w_branch_m_2, w_branch_a_2, w_out_2, norm_mix_post_2, norm_ffn_pre_2, w_up_2, w_down_2,
          norm_ffn_post_2, consts, windows, gate_row, resid, out):
    with ExitStack() as ctx:
        def sb(name, shape, dt=F32):
            return ctx.enter_context(nc.sbuf_tensor(name, shape, dt))

        def sem(name):
            return ctx.enter_context(nc.semaphore(name))

        raw = sb("raw", [P, RAW, KPC, NBLK])
        w_hi = sb("w_hi", [P, SPL, KPC, NBLK], F32R)
        w_lo = sb("w_lo", [P, SPL, KPC, NBLK], F32R)
        xa_hi, xa_lo = sb("xa_hi", [P, KC, S], F32R), sb("xa_lo", [P, KC, S], F32R)
        xb_hi, xb_lo = sb("xb_hi", [P, KC, S], F32R), sb("xb_lo", [P, KC, S], F32R)
        XA, XB = (xa_hi, xa_lo), (xb_hi, xb_lo)
        T = sb("T", [P, 4, 2 * D])
        stage = sb("stage", [P, NT, NBLK])
        tmp = sb("tmp", [P, 4, S])
        wide = sb("wide", [P, D])
        probs_t = sb("probs_t", [P, 2, CAUS])
        con = sb("con", [P, C_ALL])
        pick = sb("pick", [P, CAUS])
        vec1, vec2 = sb("vec1", [P, P]), sb("vec2", [P, P])
        vec3 = sb("vec3", [P, 2 * KC])
        rot = sb("rot", [P, 2, NT, FRQ1 + FRQI + FRQ2])
        posi = sb("posi", [P, 2, NT], I32)
        posf = sb("posf", [P, 2, NT])
        csil = sb("csil", [P, KC])
        scl = sb("scl", [P, 2, KC])
        idx_w = sb("idx_w", [P, NT, IDX_HEADS])
        ifb = sb("ifb", [P, 8])
        small = sb("small", [P, 12, 8])
        ms = sb("ms", [P, 8])
        rs = sb("rs", [P, 8])
        t8 = sb("t8", [P, 8])
        best = sb("best", [P, NT, 8])
        mx = sb("mx", [P, 2, NT])
        nmx = sb("nmx", [P, 2, NT])
        den = sb("den", [P, 4, NT])
        rden = sb("rden", [P, 2, NT])

        ps = ctx.enter_context(nc.psum_tensor("ps", [P, 8, 512], F32))

        ident, tri, cum = con[:, C_ID:C_ID + P], con[:, C_TRI:C_TRI + CAUS], con[:, C_CUM:C_CUM + P]
        ones, freqs = con[:, C_ONE:C_ONE + P], con[:, C_FRQ:C_ALL]

        def tok(i, cols=D, at=0):
            return T[:, i, at:at + NT * cols].rearrange("p (t n) -> p t n", t=NT)

        def feat(i, n=KC):
            return T[:, i, 0:n * S].rearrange("p (f t) -> p f t", t=S)

        T0, T1, T2, T3 = (tok(i) for i in range(4))
        qk_t = T[:, 0:2, :].rearrange("p a (f t) -> p (a f) t", t=S)
        amat = T[:, 2, 0:4 * NT * S].rearrange("p (g u t) -> p g u t", g=4, u=NT)
        mod_raw = T[:, 1:3, :].rearrange("p a (s n) -> p (a s) n", n=D)
        sum_first = T[:, 3, :].rearrange("p (a n) -> p a n", a=2)
        mod_acc = [sum_first[:, 0], sum_first[:, 1], T[:, 0, 0:D], T[:, 0, D:2 * D], T[:, 0, 0:D], wide[:]]
        ride_raw = T[:, 3, :].rearrange("p (s n) -> p s n", s=4)
        qi_t = feat(3, 8)
        ki_t = T[:, 3, 2048:2048 + S]
        score = probs_t[:, 0, :]
        m_v, m_o = T1[:, :, 0:1024], T1[:, :, 1024:2048]
        m_num = T[:, 2, 0:2048].rearrange("p (h t n) -> p h t n", h=M_HEADS, t=NT)
        a_v = tok(3, 1024)
        probs = tmp[:].rearrange("p f t -> p (f t)")[:, 0:2 * CAUS].rearrange("p (b n) -> p b n", b=2)
        x_tmp = wide[:, 0:4 * S].rearrange("p (f t) -> p f t", t=S)
        stage_f = stage[:].rearrange("p t (f n) -> p (t f) n", n=S)
        tmp_t = tmp[:].rearrange("p f t -> p (f t)").rearrange("p (t n) -> p t n", t=NT)
        m_dec = T[:, 2, 2048:2048 + M_HEADS * CAUS].rearrange("p (h n) -> p h n", h=M_HEADS)
        m_diag = tmp[:].rearrange("p f t -> p (f t)").rearrange("p (t h n) -> p t h n", t=NT, h=M_HEADS)
        gate_i, gate_u, gate_f, gate_w, cum_f, m_max, m_nmax, m_floor, m_e = (
            small[:, i, :].rearrange("p (t h) -> p t h", t=NT) for i in range(9))
        C_, G0, G1, PSC, MIXP, FFNP, CVB, MLN = (vec1[:, 16 * i:16 * i + 16] for i in range(8))

        def job_bank(n):
            return n % 2 * 2 + 4 if isinstance(n, int) else 4

        landed = [sem(f"landed{i}") for i in range(RAW)]
        hi_ready, lo_ready, w_used = sem("hi_ready"), sem("lo_ready"), sem("w_used")
        acc_free = sem("acc_free")
        staged, combined = sem("staged"), sem("combined")
        tp_ready, tp_evac, xh_ready, x_ready = sem("tp_ready"), sem("tp_evac"), sem("xh_ready"), sem("x_ready")
        dve_step, act_step = sem("dve_step"), sem("act_step")
        in_landed, x_landed, vec_landed, amat_landed = sem("in_landed"), sem("x_landed"), sem("vec_landed"), sem("amat_landed")
        vec_tp, vec_done = sem("vec_tp"), sem("vec_done")
        csil_ready, sin_in, rot_ready = sem("csil_ready"), sem("sin_in"), sem("rot_ready")
        mod_landed = [sem(f"mod_landed{i}") for i in range(4)]
        ride_landed = [sem(f"ride_landed{i}") for i in range(4)]
        mod_used, acc_zero, bias_landed = sem("mod_used"), sem("acc_zero"), sem("bias_landed")
        mod_sum, sum_taken, row_ready, row_stored = sem("mod_sum"), sem("sum_taken"), sem("row_ready"), sem("row_stored")
        sq_done, ms_ready, root_ready, xn_ready = (
            sem("sq_done"), sem("ms_ready"), sem("root_ready"), sem("xn_ready"))
        wide_landed, wide_used = sem("wide_landed"), sem("wide_used")
        res_landed, res_stored, res_done = sem("res_landed"), sem("res_stored"), sem("res_done")
        scl_ready, picked = sem("scl_ready"), sem("picked")
        sc_ready, relu_ready, sc_used = sem("sc_ready"), sem("relu_ready"), sem("sc_used")
        lg_ready, masked, exp_ready = sem("lg_ready"), sem("masked"), sem("exp_ready")
        pt_ready, pt_copied, pv_ready, o_done = sem("pt_ready"), sem("pt_copied"), sem("pv_ready"), sem("o_done")
        conv_in, conv_done = sem("conv_in"), sem("conv_done")
        g_in, g_act, g_mm, g_dve, g_sq = sem("g_in"), sem("g_act"), sem("g_mm"), sem("g_dve"), sem("g_sq")
        out_done, out_stored = sem("out_done"), sem("out_stored")

        def plain(w, col0):
            v = w.rearrange("(k p) n -> p k n", p=P)
            return lambda b, j: v[:, KPC * j:KPC * j + KPC, bass.ds(b * NBLK + col0, NBLK)]

        def narrow(w, col0, n):
            v = w.rearrange("(k p) n -> p k n", p=P)
            return lambda b, j: v[:, KPC * j:KPC * j + KPC, col0:col0 + n]

        grp = pool_w_grp[0].rearrange("g (k p) n -> p g k n", p=P)
        bm, ba = (w[0].rearrange("(k p) n -> p k n", p=P) for w in (w_branch_m_2, w_branch_a_2))
        down = w_down_2[0].rearrange("(e k p) n -> p e k n", e=N_FFN, p=P)

        def src_group(b, j):
            return grp[:, j // 2, KPC * (j % 2):KPC * (j % 2) + KPC, :]

        def src_branch(b, j):
            w, k = (bm, j) if j < 4 else (ba, j - 4)
            return w[:, KPC * k:KPC * k + KPC, bass.ds(b * NBLK, NBLK)]

        up = plain(w_up_2[0], 0)
        SOURCES = {
            "pool_v": plain(pool_w_in[0], 0), "pool_gate": plain(pool_w_in[0], D), "group": src_group,
            "pool_out": plain(pool_w_out[0], 0), "idx_q": plain(attn_w_in[0], IDX_COL),
            "idx_kw": narrow(attn_w_in[0], IDX_COL + 1024, 80), "qk": plain(attn_w_in[0], 0),
            "v": plain(attn_w_in[0], 2 * D), "gate": plain(attn_w_in[0], 3 * D), "attn_out": plain(attn_w_out[0], 0),
            "m_qk": plain(w_in_2[0], 0), "m_v": plain(w_in_2[0], 2048), "m_o": plain(w_in_2[0], 3072),
            "m_if": narrow(w_in_2[0], 4096, 8), "a_qk": plain(w_in_2[0], 4104), "a_v": plain(w_in_2[0], 6152),
            "g_m": plain(w_in_2[0], 7176), "g_a": plain(w_in_2[0], 9224), "branch": src_branch,
            "mix_out": plain(w_out_2[0], 0),
        }

        FB, FA, _ = PHASES["ffn"]

        block = ctx.enter_context(nc.Block())

        @block.sync
        def _(sp):
            def load(src, b, j, B, first=False, cols=NBLK):
                if not first:
                    sp.wait_ge(lo_ready, B * CPB + (j + 1 - RAW))
                sp.dma_start(raw[:, j, :, 0:cols], src(b, j)).then_inc(landed[j], 16)

            def load_phase(name, cols=NBLK):
                B0, _, n = PHASES[name]
                src, u = SOURCES[name], RIDERS.get(name)
                for j in range(CPB):
                    load(src, 0, j, B0, first=B0 == 0, cols=cols)
                    if u:
                        ride(u, 0, j, first=u == 2 and j < 4)
                if n > 1:
                    with sp.Fori(1, n) as b:
                        for j in range(CPB):
                            load(src, b, j, b + B0, cols=cols)
                            if u:
                                ride(u, b, j)

            sp.dma_start(con[:], consts).then_inc(in_landed, 16)
            for v, row, n, src in (
                (0, 0, 16, c[0]), (0, 16, 16, norm_g[0]), (0, 32, 16, norm_g[1]), (0, 48, 16, pool_scale[0]),
                (0, 64, 16, norm_mix_pre_2[0]), (0, 80, 16, norm_ffn_pre_2[0]), (0, 96, 16, conv_b_2[0]),
                (0, 112, 8, mlstm_norm_2[0]), (1, 0, 16, conv_w_2[0, 0]), (1, 16, 16, conv_w_2[0, 1]),
                (1, 32, 16, conv_w_2[0, 2]), (1, 48, 16, conv_w_2[0, 3]),
            ):
                sp.dma_start(stage[row:row + n, v, 0:P], src.rearrange("(r n) -> r n", n=P)).then_inc(vec_landed, 16)
            with nc.allow_non_contiguous_dma(reason="a position to a partition"):
                for i, pos in enumerate((positions, positions_2)):
                    sp.dma_start(posi[:, i, :], pos[0].rearrange("(t p) -> p t", p=P)).then_inc(in_landed, 16)
            for i, bias in enumerate((i_bias_2, f_bias_2)):
                sp.dma_start(ifb[:, 4 * i:4 * i + 4], bias[0:1, :].to_broadcast([P, 4])).then_inc(in_landed, 16)

            sp.dma_start(T0[:], x[0].rearrange("(t p) n -> p t n", p=P)).then_inc(x_landed, 16)

            mws = [mod_w[i].rearrange("(k p) (u n) -> p u k n", p=P, n=D) for i in range(2)]
            for u in range(2):
                for k in range(KC):
                    if u or k >= 4:
                        sp.wait_ge(mod_used, u * KC + k - 3)
                    sp.dma_start(mod_raw[:, k % 4, :], mws[0][:, u, k, :]).then_inc(mod_landed[k % 4], 16)

            def ride(u, b, j, first=False):
                if not first:
                    sp.wait_ge(mod_used, b * CPB + (RIDE[u] + j - 3))
                sp.dma_start(ride_raw[:, j % 4:j % 4 + 1, :],
                             mws[u // 3][:, u % 3, bass.ds(b * 4 + j // 2, 1), j % 2 * 1024:j % 2 * 1024 + 1024]
                             ).then_inc(ride_landed[j % 4], 16)

            sp.wait_ge(xn_ready, 1)
            sp.wait_ge(scl_ready, 1)

            load_phase("pool_v")
            load_phase("pool_gate")
            for name in ("group", "pool_out", "idx_q"):
                load_phase(name)
            load_phase("idx_kw", cols=80)
            for name in ("qk", "v", "gate", "attn_out", "m_qk", "m_v", "m_o"):
                load_phase(name)
            load_phase("m_if", cols=8)
            for name in ("a_qk", "a_v", "g_m", "g_a", "branch", "mix_out"):
                load_phase(name)

            def ffn_up(e, B, first=False):
                for h in range(2):
                    for j in range(CPB):
                        load(lambda b, j: up(e * 2 + h, j), 0, j, B + h)

            def ffn_down(e, B):
                for h in range(2):
                    for j in range(CPB):
                        load(lambda b, j: down[:, bass.ds(e, 1), KPC * (j % 4):KPC * (j % 4) + KPC,
                                               NBLK * (2 * h + j // 4):NBLK * (2 * h + j // 4) + NBLK]
                             .rearrange("p e k n -> p (e k) n"), 0, j, B + h)

            ffn_up(0, FB)
            ffn_up(1, FB + 2)
            ffn_down(0, FB + 4)
            with sp.Fori(0, 3) as i:
                ffn_up(i * 2 + 2, i * 8 + (FB + 6))
                ffn_down(i * 2 + 1, i * 8 + (FB + 8))
                ffn_up(i * 2 + 3, i * 8 + (FB + 10))
                ffn_down(i * 2 + 2, i * 8 + (FB + 12))
            ffn_down(7, FB + 30)
            for t in range(NT):
                sp.wait_ge(out_done, t + 1)
                sp.dma_start(out[0, t * P:(t + 1) * P, :], T1[:, t, :]).then_inc(out_stored, 16)
            sp.wait_ge(out_stored, 16 * NT)

        @block.gpsimd
        def _(pool):
            def tokens(dram):
                return dram.rearrange("(t p) n -> p t n", p=P)

            def widen(row):
                pool.dma_start(wide[:], row.to_broadcast([P, D])).then_inc(wide_landed, 16)

            def bias(u):
                pool.wait_ge(acc_zero, u + 1)
                if u:
                    pool.wait_ge(bias_landed, 16 * u)
                pool.dma_start(mod_acc[u][0:1, :], mod_b[u // 3:u // 3 + 1, u % 3 * D:u % 3 * D + D]
                               ).then_inc(bias_landed, 16)

            for u in range(2):
                bias(u)
            pool.wait_ge(mod_used, 2 * KC)
            pool.dma_start(amat[:], windows).then_inc(amat_landed, 16)
            for u in (2, 3, 4):
                bias(u)
            pool.wait_ge(tp_ready, JOBS["pool_v"] + 4)
            pool.dma_start(T2[:], tokens(x[0])).then_inc(res_landed, 16)
            bias(5)
            pool.wait_ge(combined, 4)
            pool.dma_start(tokens(resid[0]), T2[:]).then_inc(res_stored, 16)
            pool.wait_ge(x_ready, SPLITS["attn"] + 4)
            pool.wait_ge(row_stored, 16)
            widen(gate_row)
            pool.wait_ge(pv_ready, DSA_HEADS)
            pool.wait_ge(res_stored, 16)
            pool.dma_start(T0[:], tokens(resid[0])).then_inc(res_landed, 16)
            pool.wait_ge(combined, 8)
            widen(final_g.rearrange("(a n) -> a n", a=1))
            pool.wait_ge(res_done, 1)
            pool.dma_start(tokens(resid[1]), T0[:]).then_inc(res_stored, 16)
            pool.wait_ge(x_ready, SPLITS["moba"] + 2)
            widen(norm_mix_post_2)
            pool.wait_ge(pv_ready, DSA_HEADS + M_HEADS + MOBA_HEADS)
            pool.wait_ge(res_stored, 32)
            pool.dma_start(T3[:], tokens(resid[1])).then_inc(res_landed, 16)
            pool.wait_ge(res_done, 2)
            widen(norm_ffn_post_2)

        @block.scalar
        def _(act):
            step = Chain(act, act_step)

            def hi(B, o):
                lap = B + o // CPB
                act.wait_ge(landed[o % RAW], lap * 16 + 16)
                if not (isinstance(B, int) and B == 0 and o < SPL):
                    act.wait_ge(w_used, lap * CPB + (o % CPB + 1 - SPL))
                nc.scalar.copy(w_hi[:, o % SPL], raw[:, o % RAW]).then_inc(hi_ready, 1)

            def evac(dst, A, done, func=ACT.Copy, cols=NBLK):
                act.wait_ge(w_used, done)
                nc.scalar.activation(dst, ps[:, bass.ds((A % 2) * 2, 2), 0:cols], func).then_inc(acc_free, 1)

            def split(n, s, X, g, src):
                act.wait_ge(tp_evac, n + 1)
                nc.scalar.copy(X[0][:, bass.ds(g * 4, 4), :], src).then_inc(xh_ready, 1)

            def blk(B, hooks=None, last=False):
                for o in range(AHEAD, CPB if last else CPB + AHEAD):
                    hi(B, o)
                    if hooks and o in hooks:
                        hooks[o]()

            def phase(name, each, job=None, at=6):
                B0, A0, n = PHASES[name]
                blk(B0)
                each(0, B0, A0)
                if n > 1:
                    with act.Fori(1, n) as b:
                        blk(b + B0, {at: lambda: job(b - 1)} if job else None)
                        each(b, b + B0, b + A0)
                if job:
                    job(n - 1)

            def splits(name, X):
                return lambda b: split(b + JOBS[name], b + SPLITS[name], X, b, tmp[:])

            def root(i, n):
                act.wait_ge(ms_ready, i + 1)
                nc.scalar.activation(rs[:, 0:n], t8[:, 0:n], ACT.Sqrt).then_inc(root_ready, 1)

            def squares(i, src, junk):
                for t in range(NT):
                    step(nc.scalar.activation(junk[:, t, :], src[:, t, :], ACT.Square, accum_out=ms[:, t:t + 1]))
                act.sem_inc(sq_done, 1)
                root(i, NT)

            def norm_splits(name, X):
                for g in range(4):
                    split(JOBS[name] + g, SPLITS[name] + g, X, g, (tmp[:], stage_f)[g % 2])

            act.wait_ge(vec_done, 1)
            nc.scalar.activation(csil[:], C_, ACT.Silu).then_inc(csil_ready, 1)
            act.wait_ge(sin_in, 1)
            nc.scalar.activation(rot[:], rot[:], ACT.Sin).then_inc(rot_ready, 1)

            act.wait_ge(x_landed, 16)
            act.wait_ge(mod_used, 2 * KC)
            squares(0, T0, T1)
            norm_splits("norm0", XA)
            for o in range(AHEAD):
                hi(0, o)

            def pool_v(b, B, A):
                act.wait_ge(tp_ready, b + JOBS["pool_v"])
                act.wait_ge(x_ready, SPLITS["norm0"] + 4)
                evac(stage[:], A, B * CPB + CPB)

            phase("pool_v", pool_v, splits("pool_v", XB))
            act.wait_ge(mod_sum, 3)
            nc.scalar.copy(wide[:].rearrange("p (b n) -> p b n", b=4), ps[:, 4:8, :]).then_inc(sum_taken, 1)
            phase("pool_gate", lambda b, B, A: evac(T1[:, :, bass.ds(b * NBLK, NBLK)], A, B * CPB + CPB, ACT.Silu))

            B0, A0, _ = PHASES["group"]
            jg, sg = JOBS["group"], SPLITS["group"]
            for o in range(AHEAD, CPB + AHEAD):
                hi(B0, o)
                if o in (4, 6, 8, 10):
                    g = (o - 4) // 2
                    act.wait_ge(tp_ready, jg + g)
                    evac(stage[:], A0 + g, B0 * CPB + 2 * g + 2)
                if o in (7, 9):
                    split(jg + (o - 7) // 2, sg + (o - 7) // 2, XA, (o - 7) // 2, tmp[:])
            for g in (2, 3):
                split(jg + g, sg + g, XA, g, tmp[:])

            def to_residual(name, job):
                def each(b, B, A):
                    act.wait_ge(tp_ready, job)
                    act.wait_ge(combined, b + COMBINED[name])
                    evac(stage[:], A, B * CPB + CPB)
                return each

            phase("pool_out", to_residual("pool_out", JOBS["group"] + 4))

            act.wait_ge(combined, 4)
            squares(1, T2, T1)
            norm_splits("norm1", XB)

            def to_stage(name, norm=None, cols=NBLK):
                def each(b, B, A):
                    act.wait_ge(tp_ready, b + JOBS[name])
                    if norm:
                        act.wait_ge(x_ready, SPLITS[norm] + 4)
                    evac(stage[:, :, 0:cols], A, B * CPB + CPB, cols=cols)
                return each

            phase("idx_q", to_stage("idx_q", "norm1"))
            phase("idx_kw", to_stage("idx_kw", cols=80))
            act.wait_ge(tp_evac, JOBS["idx_kw"] + 1)
            for h in range(IDX_HEADS):
                act.wait_ge(sc_ready, h + 1)
                if h >= 2:
                    act.wait_ge(sc_used, h - 1)
                nc.scalar.activation(probs[:, h % 2, :], ps[:, 4 + h % 4, 0:CAUS], ACT.Relu).then_inc(relu_ready, 1)
            phase("qk", to_stage("qk"))
            act.wait_ge(res_stored, 16)
            phase("v", lambda b, B, A: evac(T2[:, :, bass.ds(b * NBLK, NBLK)], A, B * CPB + CPB))
            act.wait_ge(picked, 1)
            act.wait_ge(mod_sum, 6)
            nc.scalar.copy(wide[0:1, :].rearrange("p (b n) -> p b n", b=4), ps[0:1, 4:8, :]).then_inc(row_ready, 1)
            act.wait_ge(row_ready, 1)
            act.dma_start(gate_row, wide[0:1, :]).then_inc(row_stored, 16)
            phase("gate", lambda b, B, A: evac(T3[:, :, bass.ds(b * NBLK, NBLK)], A, B * CPB + CPB, ACT.Silu))

            def copy_probs(h, i):
                act.wait_ge(pt_ready, h + 1)
                if i >= 2 or h >= DSA_HEADS:
                    act.wait_ge(pv_ready, h - 1)
                nc.scalar.copy(probs_t[:, i % 2, :], ps[:, 6 + i % 2, 0:CAUS]).then_inc(pt_copied, 1)

            def attention(h0, e0, heads, name, g0):
                for i in range(heads + 3):
                    if i < heads:
                        act.wait_ge(masked, h0 + i + 1)
                        for t, (a, z) in enumerate(((0, P), (P, CAUS))):
                            last = nc.scalar.activation(
                                probs[:, i % 2, a:z], probs[:, i % 2, a:z], ACT.Exp, bias=nmx[:, i % 2, t:t + 1],
                                scale=HD ** -0.5, accum_out=den[:, i % 4, t:t + 1])
                        act.drain()
                        act.sem_inc(exp_ready, 1)
                    if 1 <= i <= heads:
                        copy_probs(h0 + i - 1, i - 1)
                    if i >= 6 and i % 4 == 2:
                        n = (i - 6) // 4
                        split(JOBS[name] + n, SPLITS[name] + n, XA, g0 + n, x_tmp)

            attention(0, 0, DSA_HEADS, "attn", 0)
            phase("attn_out", to_residual("attn_out", JOBS["attn"] + 4))

            act.wait_ge(combined, 8)
            squares(2, T0, T1)
            act.wait_ge(res_done, 1)
            squares(3, T0, T2)
            norm_splits("norm2", XB)

            def conv_silu(b):
                act.wait_ge(conv_in, b + 1)
                nc.scalar.activation(feat(0)[:, bass.ds(b * 4, 4), :], tmp[:], ACT.Silu).then_inc(conv_done, 1)

            act.wait_ge(res_stored, 32)
            phase("m_qk", to_stage("m_qk", "norm2"), conv_silu, at=9)
            phase("m_v", lambda b, B, A: evac(m_v[:, :, bass.ds(b * NBLK, NBLK)], A, B * CPB + CPB))
            phase("m_o", lambda b, B, A: evac(m_o[:, :, bass.ds(b * NBLK, NBLK)], A, B * CPB + CPB, ACT.Sigmoid))

            B0, A0, _ = PHASES["m_if"]
            blk(B0)
            act.wait_ge(tp_ready, JOBS["m_qk"] + 4)
            evac(stage[:, :, 0:8], A0, B0 * CPB + CPB, cols=8)

            act.wait_ge(g_in, 1)
            step(nc.scalar.activation(gate_u, gate_u, ACT.Exp))
            act.sem_inc(g_act, 1)
            act.wait_ge(g_in, 2)
            nc.scalar.activation(gate_f, gate_w, ACT.Ln).then_inc(g_act, 1)
            act.wait_ge(g_dve, 1)
            for h in range(M_HEADS):
                for t, (a, z) in enumerate(((0, P), (P, CAUS))):
                    nc.scalar.activation(m_dec[:, h, a:z], m_dec[:, h, a:z], ACT.Exp, bias=m_nmax[:, t, h:h + 1])
            nc.scalar.activation(m_floor, m_floor, ACT.Exp, scale=-1.0).then_inc(g_act, 1)
            for i in range(M_HEADS + 2):
                if 1 <= i <= M_HEADS:
                    copy_probs(DSA_HEADS + i - 1, i - 1)
                if i >= 2:
                    act.wait_ge(o_done, DSA_HEADS + i - 1)
                    for t in range(NT):
                        at = ((i - 2) * NT + t) * S
                        step(nc.scalar.activation(T[:, 3, at:at + S], m_num[:, i - 2, t, :], ACT.Square,
                                                  accum_out=ms[:, t * M_HEADS + i - 2:t * M_HEADS + i - 1]))
            act.sem_inc(sq_done, 1)
            root(4, NT * M_HEADS)
            for n in range(2):
                split(JOBS["mlstm"] + n, SPLITS["mlstm"] + n, XA, n, x_tmp)

            phase("a_qk", to_stage("a_qk"))
            phase("a_v", lambda b, B, A: evac(a_v[:, :, bass.ds(b * NBLK, NBLK)], A, B * CPB + CPB))
            attention(DSA_HEADS + M_HEADS, DSA_HEADS, MOBA_HEADS, "moba", 2)
            phase("g_m", lambda b, B, A: evac(T0[:, :, bass.ds(b * NBLK, NBLK)], A, B * CPB + CPB, ACT.Sigmoid))
            phase("g_a", lambda b, B, A: evac(T1[:, :, bass.ds(b * NBLK, NBLK)], A, B * CPB + CPB, ACT.Sigmoid))

            B0, A0, n = PHASES["branch"]

            def branch(b, first=False):
                B, A = b + B0, b * 2 + A0
                for o in range(AHEAD, CPB + AHEAD):
                    hi(B, o)
                    if o == 6:
                        if not first:
                            split(b + (JOBS["branch"] - 1), b + (SPLITS["branch"] - 1), XB, b - 1, tmp[:])
                        act.wait_ge(tp_ready, b + JOBS["branch"])
                        evac(stage[:], A, B * CPB + 4)
                act.wait_ge(x_ready, b + SPLITS["branch"])
                evac(tmp_t, A + 1, B * CPB + 8)

            branch(0, first=True)
            with act.Fori(1, n) as b:
                branch(b)
            split(JOBS["branch"] + 3, SPLITS["branch"] + 3, XB, 3, tmp[:])

            phase("mix_out", lambda b, B, A: evac(T2[:, :, bass.ds(b * NBLK, NBLK)], A, B * CPB + CPB))
            act.wait_ge(acc_free, PHASES["mix_out"][1] + 4)
            squares(5, T2, T1)
            act.wait_ge(res_done, 2)
            squares(6, T3, T1)
            norm_splits("norm3", XA)

            J, X0, C0 = JOBS["ffn"], SPLITS["ffn"], COMBINED["ffn"]

            def up(e, half, B, A, after=None):
                for h in range(2):
                    def mid():
                        split(e * 2 + (J + h - 1), e * 2 + (X0 + h - 1), XB, (2 * half + h - 1) % 4, tmp[:])
                    blk(B + h, {6: mid} if h == 1 or after == "up" else None)
                    act.wait_ge(tp_ready, e * 2 + (J + h))
                    if after == "norm":
                        act.wait_ge(x_ready, X0)
                    elif after is None:
                        act.wait_ge(combined, e * 4 + (C0 - 4))
                    evac(stage[:], A + h, (B + h) * CPB + CPB, ACT.Relu)

            def dn(e, half, B, A, last=False):
                def take(q):
                    act.wait_ge(tp_ready, (J + 2 * N_FFN) if last else e * 2 + (J + 4))
                    act.wait_ge(combined, e * 4 + (C0 + q))
                    evac(stage[:], A + q, B * CPB + 4 * (q + 1))

                def mid():
                    if not last:
                        split(e * 2 + (J + 3), e * 2 + (X0 + 3), XB, 2 * (1 - half) + 1, tmp[:])
                    take(0)

                blk(B, {6: mid, 10: lambda: take(1)})
                blk(B + 1, {6: lambda: take(2), 10: lambda: take(3)}, last=last)
                if last:
                    take(3)

            up(0, 0, FB, FA, after="norm")
            up(1, 1, FB + 2, FA + 2, after="up")
            dn(0, 0, FB + 4, FA + 4)
            with act.Fori(0, 3) as i:
                up(i * 2 + 2, 0, i * 8 + (FB + 6), i * 12 + (FA + 8))
                dn(i * 2 + 1, 1, i * 8 + (FB + 8), i * 12 + (FA + 10))
                up(i * 2 + 3, 1, i * 8 + (FB + 10), i * 12 + (FA + 14))
                dn(i * 2 + 2, 0, i * 8 + (FB + 12), i * 12 + (FA + 16))
            dn(7, 1, FB + 30, FA + 44, last=True)
            act.wait_ge(combined, COMBINED["ffn"] + 4 * N_FFN)
            squares(7, T1, T2)

        @block.vector
        def _(dve):
            step = Chain(dve, dve_step)
            tt, ts, stt = nc.vector.tensor_tensor, nc.vector.tensor_scalar, nc.vector.scalar_tensor_tensor

            def lo(B, o):
                dve.wait_ge(hi_ready, (B + o // CPB) * CPB + (o % CPB + 1))
                tt(w_lo[:, o % SPL], raw[:, o % RAW], w_hi[:, o % SPL].bitcast(F32), ALU.subtract
                   ).then_inc(lo_ready, 1)

            def blk(B, hooks=None, last=False, ride=None, b=None, ride_to=CPB + AHEAD):
                for o in range(AHEAD, CPB if last else CPB + AHEAD):
                    lo(B, o)
                    if ride and o < ride_to:
                        rider(ride, b, o)
                    if hooks and o in hooks:
                        hooks[o]()

            def phase(name, each=None, out=None, low=None, per=0):
                B0, A0, n = PHASES[name]
                u = RIDERS.get(name)
                if u:
                    for o in range(AHEAD):
                        rider(u, 0, o)
                blk(B0, ride=u, b=0)
                if each:
                    each(0, A0)
                if n > 1:
                    hooks = lambda b: {5: lambda: out(b - 1), 6: lambda: low(b - 1)} if out else None
                    with step.loop(1, n - 1 if u else n, per) as b:
                        blk(b + B0, hooks(b), ride=u, b=b)
                        if each:
                            each(b, b + A0)
                    if u:
                        blk(n - 1 + B0, hooks(n - 1), ride=u, b=n - 1, ride_to=CPB)
                        if each:
                            each(n - 1, n - 1 + A0)
                if out:
                    out(n - 1)
                    low(n - 1)

            def leave(n, dst, scale=None, shift=None, bank=None):
                dve.wait_ge(tp_ready, n + 1)
                p0 = job_bank(n) if bank is None else bank
                src = ps[:, p0:p0 + 2, :].rearrange("p b (f t) -> p (b f) t", t=S)
                if scale is None:
                    nc.vector.tensor_copy(dst, src).then_inc(tp_evac, 1)
                elif shift is None:
                    tt(dst, src, scale.unsqueeze(2).to_broadcast([P, 4, S]), ALU.mult).then_inc(tp_evac, 1)
                else:
                    step(tt(dst, src, scale.unsqueeze(2).to_broadcast([P, 4, S]), ALU.mult))
                    tt(dst, dst, shift.unsqueeze(2).to_broadcast([P, 4, S]), ALU.add).then_inc(tp_evac, 1)

            def low_part(s, X, g, src):
                dve.wait_ge(xh_ready, s + 1)
                tt(X[1][:, bass.ds(g * 4, 4), :], src, X[0][:, bass.ds(g * 4, 4), :].bitcast(F32), ALU.subtract
                   ).then_inc(x_ready, 1)
                dve.wait_ge(x_ready, s + 1)

            def outs(name, X, scale=None):
                def out(b):
                    leave(b + JOBS[name], tmp[:], None if scale is None else scale[:, bass.ds(b * 4, 4)])
                return out, lambda b: low_part(b + SPLITS[name], X, b, tmp[:])

            def rstd(i, n, width):
                dve.wait_ge(sq_done, i + 1)
                ts(t8[:, 0:n], ms[:, 0:n], 1.0 / width, EPS, ALU.mult, ALU.add).then_inc(ms_ready, 1)
                dve.wait_ge(root_ready, i + 1)
                y, q = rs[:, 0:n], small[:, 9, 0:n]
                step(nc.vector.reciprocal(y, y))
                step(tt(q, y, y, ALU.mult))
                step(tt(q, q, t8[:, 0:n], ALU.mult))
                step(ts(q, q, -0.5, 1.5, ALU.mult, ALU.add))
                step(tt(y, y, q, ALU.mult))

            def normed(dst, src):
                for t in range(NT):
                    step(ts(dst[:, t, :], src[:, t, :], rs[:, t:t + 1], None, ALU.mult))
                dve.sem_inc(xn_ready, 1)

            def norm_jobs(name, X, scale, shift=None):
                bufs = (tmp[:], stage_f)
                for g in range(5):
                    if g < 4:
                        leave(JOBS[name] + g, bufs[g % 2], scale[:, 4 * g:4 * g + 4],
                              None if shift is None else shift[:, 4 * g:4 * g + 4])
                    if g:
                        low_part(SPLITS[name] + g - 1, X, g - 1, bufs[(g - 1) % 2])

            def rotate(src, heads, half, at):
                v = src.rearrange("p t (h d) -> p t h d", h=heads)
                n = NT * heads * half
                ta, tb = (tmp[:].rearrange("p f t -> p (f t)")[:, k * 512:k * 512 + n]
                          .rearrange("p (t h d) -> p t h d", t=NT, h=heads) for k in range(2))
                x1, x2 = v[:, :, :, 0:half], v[:, :, :, half:2 * half]
                cosb, sinb = (rot[:, k, :, at:at + half].unsqueeze(2).to_broadcast([P, NT, heads, half])
                              for k in range(2))
                step(tt(ta, x1, cosb, ALU.mult))
                step(tt(tb, x2, sinb, ALU.mult))
                step(tt(ta, ta, tb, ALU.subtract))
                step(tt(tb, x1, sinb, ALU.mult))
                step(tt(x2, x2, cosb, ALU.mult))
                step(tt(x2, x2, tb, ALU.add))
                step(nc.vector.tensor_copy(x1, ta))

            dve.wait_ge(in_landed, 16 * 5)
            step(nc.vector.tensor_copy(posf[:], posi[:]))
            cos, sin = rot[:, 0], rot[:, 1]
            ang, turns = (tmp[:].rearrange("p f t -> p (f t)")[:, k * 512:k * 512 + NT * 88]
                          .rearrange("p (t f) -> p t f", t=NT) for k in range(2))
            for t in range(NT):
                step(ts(ang[:, t, 0:24], freqs[:, 0:24], posf[:, 0, t:t + 1], None, ALU.mult))
                step(ts(ang[:, t, 24:88], freqs[:, 24:88], posf[:, 1, t:t + 1], None, ALU.mult))
            for dst, turn in ((cos, 0.25), (sin, 0.0)):
                step(ts(turns, ang, 1.0 / (2 * np.pi), turn, ALU.mult, ALU.add))
                step(ts(turns, turns, MAGIC, None, ALU.add))
                step(ts(turns, turns, MAGIC, None, ALU.subtract))
                step(stt(dst, turns, -TWO_PI[0], ang, ALU.mult, ALU.add))
                for part in TWO_PI[1:]:
                    step(stt(dst, turns, -part, dst, ALU.mult, ALU.add))
                step(ts(dst, dst, 2 * np.pi * turn, PI_CLAMP, ALU.add, ALU.min))
                step(ts(dst, dst, -PI_CLAMP, None, ALU.max))
            dve.sem_inc(sin_in, 1)

            dve.wait_ge(vec_tp, 1)
            step(nc.vector.tensor_copy(vec1[:, 0:120], ps[:, 4, 0:120]))
            step(nc.vector.tensor_copy(vec2[:, 0:64], ps[:, 5, 0:64]))
            dve.sem_inc(vec_done, 1)

            def clear(u):
                zero = tri[:, P:P + 1].to_broadcast([P, D])
                nc.vector.tensor_copy(mod_acc[u], zero).then_inc(acc_zero, 1)

            clear(0)
            clear(1)
            dve.wait_ge(csil_ready, 1)
            for u in range(2):
                dve.wait_ge(bias_landed, 16 * u + 16)
                for k in range(KC):
                    dve.wait_ge(mod_landed[k % 4], 16 * (4 * u + k // 4 + 1))
                    stt(mod_acc[u], mod_raw[:, k % 4, :], csil[:, k:k + 1], mod_acc[u], ALU.mult, ALU.add
                        ).then_inc(mod_used, 1)
                    dve.wait_ge(mod_used, u * KC + k + 1)

            def rider(u, b, o):
                if o == 0 and isinstance(b, int):
                    dve.wait_ge(bias_landed, 16 * u + 16)
                c0 = b * CPB + (o % CPB + o // CPB * CPB)
                at = o % 2 * 1024
                lap = b * 2 + (2 * KC // 16 * 4 * (u - 2) + o // 4 + 1)
                dve.wait_ge(ride_landed[o % 4], lap * 16)
                acc = mod_acc[u][:, at:at + 1024]
                stt(acc, ride_raw[:, o % 4, :], csil[:, bass.ds(b * 4 + o // 2, 1)], acc, ALU.mult, ALU.add
                    ).then_inc(mod_used, 1)
                dve.wait_ge(mod_used, c0 + (RIDE[u] + 1))

            def shift_scale(i, what, u):
                dve.wait_ge(mod_sum, u + 1)
                dst = vec3[:, 16 * i:16 * i + 16] if what == "shift" else scl[:, i, :]
                step(nc.vector.tensor_copy(dst, ps[:, 6, 0:KC]))
                if what == "scale":
                    step(ts(dst, dst, 1.0, None, ALU.add))
                    step(tt(dst, dst, (G0, G1)[i], ALU.mult))
                dve.sem_inc(sum_taken, 1)

            shift_scale(0, "shift", 0)
            shift_scale(0, "scale", 1)
            dve.sem_inc(scl_ready, 1)

            rstd(0, NT, D)
            normed(T0, T0)
            norm_jobs("norm0", XA, scl[:, 0, :], vec3[:, 0:16])
            clear(2)
            clear(3)
            for o in range(AHEAD):
                lo(0, o)

            phase("pool_v", None, *outs("pool_v", XB))
            dve.wait_ge(mod_sum, 3)
            clear(4)
            phase("pool_gate")
            shift_scale(1, "shift", 3)
            B0, A0, _ = PHASES["group"]
            out, low = outs("group", XA, PSC)
            for o in range(AHEAD, CPB + AHEAD):
                lo(B0, o)
                if o in (4, 6, 8, 10):
                    g = (o - 4) // 2
                    dve.wait_ge(acc_free, A0 + g + 1)
                    tt(stage[:], stage[:], T1[:, :, NBLK * g:NBLK * g + NBLK], ALU.mult).then_inc(staged, 1)
                if o in (7, 9):
                    out((o - 7) // 2)
                if o in (8, 10):
                    low((o - 8) // 2)
            for g in (2, 3):
                out(g)
                low(g)

            def add_residual(name, k, dst):
                def each(b, A):
                    dve.wait_ge(acc_free, A + 1)
                    if k == 1:
                        dve.wait_ge(sum_taken, 3)
                    else:
                        dve.wait_ge(wide_landed, 16)
                    dve.wait_ge(res_landed, 16 * k)
                    cols = bass.ds(b * NBLK, NBLK)
                    step(tt(stage[:], stage[:], wide[:, cols].unsqueeze(1).to_broadcast([P, NT, NBLK]), ALU.mult))
                    tt(dst[:, :, cols], dst[:, :, cols], stage[:], ALU.add).then_inc(combined, 1)
                return each

            phase("pool_out", add_residual("pool_out", 1, T2), per=1)

            shift_scale(1, "scale", 4)
            clear(5)
            rstd(1, NT, D)
            normed(T0, T2)
            norm_jobs("norm1", XB, scl[:, 1, :], vec3[:, 16:32])

            def index_q(b, A):
                dve.wait_ge(acc_free, A + 1)
                rotate(stage[:], 8, FRQI, FRQ1)
                dve.sem_inc(staged, 1)

            n0 = JOBS["idx_q"]
            phase("idx_q", index_q, lambda b: leave(b + n0, qi_t[:, bass.ds(b * 4, 4), :]), lambda b: None,
                  per=7)
            B0, A0, _ = PHASES["idx_kw"]
            blk(B0)
            dve.wait_ge(acc_free, A0 + 1)
            rotate(stage[:, :, 0:64], 1, FRQI, FRQ1)
            step(ts(idx_w[:], stage[:, :, 64:80], IDX_HEADS ** -0.5 * 64 ** -0.5, None, ALU.mult))
            nc.vector.tensor_copy(stage[:, :, 64:128], stage[:, :, 0:64]).then_inc(staged, 1)
            n = JOBS["idx_kw"]
            dve.wait_ge(tp_ready, n + 1)
            nc.vector.tensor_copy(ki_t, ps[:, 4 + n % 2 * 2, 0:S]).then_inc(tp_evac, 1)
            step(nc.vector.tensor_copy(score, tri))
            for h in range(IDX_HEADS):
                dve.wait_ge(relu_ready, h + 1)
                for t, (a, z) in enumerate(((0, P), (P, CAUS))):
                    step(stt(score[:, a:z], probs[:, h % 2, a:z], idx_w[:, t, h:h + 1], score[:, a:z],
                             ALU.mult, ALU.add))
                dve.sem_inc(sc_used, 1)

            def carry():
                nc.vector.tensor_copy(small[:, 10, 0:1], posf[:, 0, 0:1])

            def query_key(b, A):
                dve.wait_ge(acc_free, A + 1)
                rotate(stage[:], 4, FRQ1, 0)
                for t, (a, z) in enumerate(((0, P), (P, CAUS))):
                    carry()
                    step(nc.vector.max(best[:, t, :], score[:, a:z]))
                    carry()
                    step(nc.vector.match_replace(score[:, a:z], best[:, t, :], score[:, a:z], TAKEN))
                dve.sem_inc(staged, 1)

            n1 = JOBS["qk"]
            phase("qk", query_key, lambda b: leave(b + n1, qk_t[:, bass.ds(b * 4, 4), :]), lambda b: None,
                  per=11)
            step(ts(score, score, 0.5 * (TAKEN + FAR), UNPICKED, ALU.is_gt, ALU.mult))
            step(tt(pick[:], score, tri, ALU.add))
            dve.sem_inc(picked, 1)
            phase("v")
            phase("gate")

            def attention(h0, e0, heads, name, g0, mask, gate):
                for i in range(heads + 4):
                    if i < heads:
                        h, b = h0 + i, i % 2
                        dve.wait_ge(lg_ready, h + 1)
                        if i >= 2:
                            dve.wait_ge(pt_ready, h - 1)
                        for t, (a, z) in enumerate(((0, P), (P, CAUS))):
                            step(nc.vector.tensor_tensor_reduce(
                                out=probs[:, b, a:z], in0=ps[:, 4 + b, a:z], in1=mask[:, a:z], scale=1.0,
                                scalar=FAR, op0=ALU.add, op1=ALU.max, accum_out=mx[:, b, t:t + 1]))
                        ts(nmx[:, b, :], mx[:, b, :], -(HD ** -0.5), None, ALU.mult).then_inc(masked, 1)
                    if i >= 6 and i % 4 == 2:
                        n = (i - 6) // 4
                        leave(JOBS[name] + n, x_tmp, bank=2)
                    if i >= 6 and i % 4 == 3:
                        low_part(SPLITS[name] + (i - 7) // 4, XA, g0 + (i - 7) // 4, x_tmp)
                    if 2 <= i < heads + 2:
                        j = i - 2
                        b = j % 2
                        dve.wait_ge(exp_ready, e0 + j + 1)
                        step(nc.vector.reciprocal(rden[:, b, :], den[:, j % 4, :]))
                        dve.wait_ge(pv_ready, h0 + j + 1)
                        for t in range(NT):
                            dst, src = stage[:, t, j % 4 * HD:j % 4 * HD + HD], ps[:, b, t * HD:t * HD + HD]
                            if gate is None:
                                step(ts(dst, src, rden[:, b, t:t + 1], None, ALU.mult))
                            else:
                                step(stt(dst, src, rden[:, b, t:t + 1], gate[:, t, j * HD:j * HD + HD],
                                         ALU.mult, ALU.mult))
                        dve.sem_inc(o_done, 1)
                        if j % 4 == 3:
                            dve.sem_inc(staged, 1)

            dve.wait_ge(acc_free, PHASES["gate"][1] + 4)
            dve.wait_ge(row_stored, 16)
            attention(0, 0, DSA_HEADS, "attn", 0, pick[:], T3)
            phase("attn_out", add_residual("attn_out", 2, T0), per=1)

            rstd(2, NT, D)
            dve.wait_ge(wide_landed, 32)
            for t in range(NT):
                step(stt(T0[:, t, :], T0[:, t, :], rs[:, t:t + 1], wide[:], ALU.mult, ALU.mult))
            dve.sem_inc(res_done, 1)
            rstd(3, NT, D)
            normed(T1, T0)
            norm_jobs("norm2", XB, MIXP)

            def conv(b, f):
                if f == 0:
                    dve.wait_ge(tp_ready, b + (JOBS["m_qk"] + 1))
                p0 = job_bank(b + JOBS["m_qk"])
                u = ps[:, p0 + f // 2, f % 2 * S:f % 2 * S + S]
                col = b * 4 + f
                w = [vec2[:, bass.ds(col + 16 * k, 1)] for k in range(4)]
                step(ts(tmp[:, f, :], u, w[3], CVB[:, bass.ds(col, 1)], ALU.mult, ALU.add))
                for k in range(3):
                    lag = 3 - k
                    step(stt(tmp[:, f, lag:S], u[:, 0:S - lag], w[k], tmp[:, f, lag:S], ALU.mult, ALU.add))
                if f == 3:
                    dve.sem_inc(tp_evac, 1)
                    dve.sem_inc(conv_in, 1)

            B0, A0, n = PHASES["m_qk"]
            blk(B0)
            with step.loop(1, n, 16) as b:
                dve.wait_ge(conv_done, b - 1)
                blk(b + B0, {5 + f: (lambda f=f: conv(b - 1, f)) for f in range(4)})
            dve.wait_ge(conv_done, 3)
            for f in range(4):
                conv(3, f)
            phase("m_v")
            phase("m_o")
            B0, A0, _ = PHASES["m_if"]
            blk(B0)
            dve.wait_ge(acc_free, A0 + 1)
            for k, dst in ((0, gate_i), (1, gate_f)):
                step(tt(dst, stage[:, :, 4 * k:4 * k + 4], ifb[:, 4 * k:4 * k + 4].unsqueeze(1)
                        .to_broadcast([P, NT, 4]), ALU.add))
            step(ts(gate_u, gate_f, -1.0, None, ALU.mult))
            step(tt(gate_u, gate_u, gate_f, ALU.min))
            step(ts(m_e, gate_f, 0.0, None, ALU.min))
            dve.sem_inc(g_in, 1)
            dve.wait_ge(g_act, 1)
            step(ts(gate_w, gate_u, 1.0, None, ALU.add))
            dve.sem_inc(g_in, 1)
            step(ts(cum_f, gate_w, -1.0, 1e-30, ALU.add, ALU.max))
            step(nc.vector.reciprocal(cum_f, cum_f))
            step(tt(cum_f, cum_f, gate_u, ALU.mult))
            dve.wait_ge(g_act, 2)
            step(tt(gate_f, gate_f, cum_f, ALU.mult))
            step(tt(gate_f, m_e, gate_f, ALU.subtract))
            dve.sem_inc(g_in, 1)
            dve.wait_ge(g_mm, 1)
            step(nc.vector.tensor_copy(cum_f, ps[:, 2, 0:8].rearrange("p (t h) -> p t h", t=NT)))
            step(tt(m_e, gate_i, cum_f, ALU.subtract))
            for t in range(NT):
                for h in range(M_HEADS):
                    step(ts(m_diag[:, t, h, :], ident, m_e[:, t, h:h + 1], None, ALU.mult))
            dve.sem_inc(g_in, 1)
            dve.wait_ge(g_mm, 2)
            for h in range(M_HEADS):
                for t, (a, z) in enumerate(((0, P), (P, CAUS))):
                    at = h % 2 * S
                    step(nc.vector.tensor_tensor_reduce(
                        out=m_dec[:, h, a:z], in0=ps[:, 4 + h // 2, at:at + z - a], in1=tri[:, a:z], scale=1.0,
                        scalar=0.0, op0=ALU.add, op1=ALU.max, accum_out=m_max[:, t, h:h + 1]))
            step(ts(m_nmax, m_max, -1.0, None, ALU.mult))
            step(tt(m_floor, m_max, cum_f, ALU.add))
            dve.sem_inc(g_dve, 1)
            dve.wait_ge(g_act, 3)
            for i in range(M_HEADS + 2):
                if i < M_HEADS:
                    dve.wait_ge(lg_ready, DSA_HEADS + i + 1)
                    if i >= 2:
                        dve.wait_ge(pt_ready, DSA_HEADS + i - 1)
                    for t, (a, z) in enumerate(((0, P), (P, CAUS))):
                        step(nc.vector.tensor_tensor_reduce(
                            out=probs[:, i % 2, a:z], in0=ps[:, 4 + i % 2, a:z], in1=m_dec[:, i, a:z], scale=S ** -0.5,
                            scalar=0.0, op0=ALU.mult, op1=ALU.add, accum_out=den[:, i % 2, t:t + 1]))
                    dve.sem_inc(masked, 1)
                if i >= 2:
                    j = i - 2
                    dve.wait_ge(pv_ready, DSA_HEADS + j + 1)
                    for t in range(NT):
                        step(ts(m_num[:, j, t, :], ps[:, j % 2, t * S:t * S + S], rden[:, j % 2, t:t + 1], None,
                                ALU.mult))
                    dve.sem_inc(o_done, 1)
                if i < M_HEADS:
                    step(ts(rden[:, i % 2, :], den[:, i % 2, :], -1.0, None, ALU.mult))
                    step(tt(rden[:, i % 2, :], rden[:, i % 2, :], den[:, i % 2, :], ALU.max))
                    step(tt(rden[:, i % 2, :], rden[:, i % 2, :], m_floor[:, :, i], ALU.max))
                    step(nc.vector.reciprocal(rden[:, i % 2, :], rden[:, i % 2, :]))
            rstd(4, NT * M_HEADS, S)
            for n in range(2):
                if n:
                    dve.wait_ge(tp_ready, JOBS["mlstm"] + n)
                for t in range(NT):
                    for h in range(2):
                        j = 2 * n + h
                        step(stt(stage[:, t, h * S:h * S + S], m_num[:, j, t, :],
                                 rs[:, t * M_HEADS + j:t * M_HEADS + j + 1], m_o[:, t, j * S:j * S + S],
                                 ALU.mult, ALU.mult))
                dve.sem_inc(staged, 1)
                leave(JOBS["mlstm"] + n, x_tmp, MLN[:, 4 * n:4 * n + 4], bank=2)
                low_part(SPLITS["mlstm"] + n, XA, n, x_tmp)

            def rotary_full(b, A):
                dve.wait_ge(acc_free, A + 1)
                rotate(stage[:], 4, FRQ2, FRQ1 + FRQI)
                dve.sem_inc(staged, 1)

            n2 = JOBS["a_qk"]
            phase("a_qk", rotary_full, lambda b: leave(b + n2, feat(2)[:, bass.ds(b * 4, 4), :]), lambda b: None,
                  per=7)
            phase("a_v")
            attention(DSA_HEADS + M_HEADS, DSA_HEADS, MOBA_HEADS, "moba", 2, tri, None)
            phase("g_m")
            phase("g_a")

            B0, A0, n = PHASES["branch"]
            out, low = outs("branch", XB)

            def branch(b, first=False):
                B, A = b + B0, b * 2 + A0
                cols = bass.ds(b * NBLK, NBLK)
                for o in range(AHEAD, CPB + AHEAD):
                    lo(B, o)
                    if o == 5 and not first:
                        out(b - 1)
                    if o == 6:
                        if not first:
                            low(b - 1)
                        dve.wait_ge(acc_free, A + 1)
                        step(tt(stage[:], stage[:], T0[:, :, cols], ALU.mult))
                dve.wait_ge(acc_free, A + 2)
                step(tt(tmp_t, tmp_t, T1[:, :, cols], ALU.mult))
                tt(stage[:], stage[:], tmp_t, ALU.add).then_inc(staged, 1)

            branch(0, first=True)
            with step.loop(1, n, 2) as b:
                branch(b)
            out(3)
            low(3)
            phase("mix_out")

            rstd(5, NT, D)
            dve.wait_ge(wide_landed, 48)
            dve.wait_ge(res_landed, 48)
            for t in range(NT):
                step(stt(T2[:, t, :], T2[:, t, :], rs[:, t:t + 1], wide[:], ALU.mult, ALU.mult))
                step(tt(T3[:, t, :], T3[:, t, :], T2[:, t, :], ALU.add))
            dve.sem_inc(res_done, 1)
            rstd(6, NT, D)
            normed(T2, T3)
            norm_jobs("norm3", XA, FFNP)
            step(nc.vector.memset(T1[:], 0.0))

            J, X0, C0, S0 = JOBS["ffn"], SPLITS["ffn"], COMBINED["ffn"], STAGED["ffn"]

            def up(e, half, B, A, after=None):
                for h in range(2):
                    hooks = None
                    if h == 1 or after == "up":
                        j, g = e * 2 + (h - 1), (2 * half + h - 1) % 4
                        hooks = {5: lambda: leave(j + J, tmp[:]), 6: lambda: low_part(j + X0, XB, g, tmp[:])}
                    blk(B + h, hooks)
                    dve.wait_ge(acc_free, A + (h + 1))
                    tt(stage[:], stage[:], stage[:], ALU.mult).then_inc(staged, 1)

            def dn(e, half, B, A, last=False):
                def add(q):
                    dve.wait_ge(acc_free, A + (q + 1))
                    y = T1[:, :, q * NBLK:q * NBLK + NBLK]
                    tt(y, y, stage[:], ALU.add).then_inc(combined, 1)

                def mid():
                    if not last:
                        low_part(e * 2 + (X0 + 3), XB, 2 * (1 - half) + 1, tmp[:])
                    add(0)

                blk(B, {5: (lambda: None) if last else (lambda: leave(e * 2 + (J + 3), tmp[:])),
                        6: mid, 10: lambda: add(1)})
                blk(B + 1, {6: lambda: add(2), 10: lambda: add(3)}, last=last)
                if last:
                    add(3)

            up(0, 0, FB, FA, after="norm")
            up(1, 1, FB + 2, FA + 2, after="up")
            dn(0, 0, FB + 4, FA + 4)
            with step.loop(0, 3, 0) as i:
                up(i * 2 + 2, 0, i * 8 + (FB + 6), i * 12 + (FA + 8))
                dn(i * 2 + 1, 1, i * 8 + (FB + 8), i * 12 + (FA + 10))
                up(i * 2 + 3, 1, i * 8 + (FB + 10), i * 12 + (FA + 14))
                dn(i * 2 + 2, 0, i * 8 + (FB + 12), i * 12 + (FA + 16))
            dn(7, 1, FB + 30, FA + 44, last=True)

            rstd(7, NT, D)
            dve.wait_ge(wide_landed, 64)
            for t in range(NT):
                step(stt(T1[:, t, :], T1[:, t, :], rs[:, t:t + 1], wide[:], ALU.mult, ALU.mult))
                tt(T1[:, t, :], T1[:, t, :], T3[:, t, :], ALU.add).then_inc(out_done, 1)

        @block.tensor
        def _(pe):
            mm = nc.tensor.matmul

            def chunk(B, j, X, k0, A, first, last, cols=NBLK):
                pe.wait_ge(lo_ready, B * CPB + (j + 1))
                bank = (A % 2) * 2
                for k in range(KPC):
                    for t in range(NT):
                        x_hi, x_lo = (v[:, k0 + k, t * P:(t + 1) * P] for v in X)
                        h, l = (w[:, j % SPL, k, 0:cols] for w in (w_hi, w_lo))
                        dst = ps[:, bank + t, 0:cols]
                        mm(dst, x_hi, h, start=first and k == 0, stop=False)
                        mm(dst, x_hi, l, start=False, stop=False)
                        ins = mm(dst, x_lo, h, start=False, stop=last and k == KPC - 1)
                ins.then_inc(w_used, 1)

            def blk(B, A, X, free, mid=None, cols=NBLK):
                if free:
                    pe.wait_ge(acc_free, A - 1)
                for j in range(CPB):
                    chunk(B, j, X, KPC * j, A, j == 0, j == CPB - 1, cols)
                    if j == 3 and mid:
                        mid()

            def phase(name, X, job=None, cols=NBLK):
                B0, A0, n = PHASES[name]
                blk(B0, A0, X, A0 >= 2, cols=cols)
                if n > 1:
                    if A0 < 2:
                        blk(1 + B0, 1 + A0, X, False, (lambda: job(0)) if job else None)
                    with pe.Fori(2 if A0 < 2 else 1, n) as b:
                        blk(b + B0, b + A0, X, True, (lambda: job(b - 1)) if job else None)
                if job:
                    job(n - 1)

            def job(n, src, ready, value, bank=None):
                pe.wait_ge(ready, value)
                if bank is not None or not isinstance(n, int):
                    pe.wait_ge(tp_evac, n)
                elif n >= 2:
                    pe.wait_ge(tp_evac, n - 1)
                p0 = job_bank(n) if bank is None else bank
                for f in range(4):
                    for t in range(NT):
                        at = f % 2 * S + t * P
                        ins = nc.tensor.transpose(ps[:, p0 + f // 2, at:at + P], src[:, t, f * P:(f + 1) * P], ident)
                ins.then_inc(tp_ready, 1)

            def stage_job(name):
                return lambda b: job(b + JOBS[name], stage, staged, b + (STAGED[name] + 1))

            def norm_jobs(name, i, src):
                for g in range(4):
                    job(JOBS[name] + g, src[:, :, g * NBLK:(g + 1) * NBLK], xn_ready, i + 1)

            pe.wait_ge(vec_landed, 16 * 12)
            pe.wait_ge(in_landed, 16 * 5)
            nc.tensor.transpose(ps[:, 4, 0:120], stage[0:120, 0, 0:P], ident[0:120, 0:120])
            nc.tensor.transpose(ps[:, 5, 0:64], stage[0:64, 1, 0:P], ident[0:64, 0:64]).then_inc(vec_tp, 1)

            def total(u):
                pe.wait_ge(mod_used, RIDE[u] + 2 * KC if u >= 2 else KC * (u + 1))
                if u:
                    pe.wait_ge(sum_taken, u)
                for f in range(KC):
                    ins = mm(ps[:, 6, f:f + 1], mod_acc[u][:, f * P:(f + 1) * P], ones[:, 0:1], start=True, stop=True)
                ins.then_inc(mod_sum, 1)

            def total_gate(u, rows):
                pe.wait_ge(mod_used, RIDE[u] + 2 * KC)
                for q in range(4):
                    ins = mm(ps[0:rows, 4 + q, :], ones[:, 0:rows], mod_acc[u][:, q * NBLK:(q + 1) * NBLK],
                             start=True, stop=True)
                ins.then_inc(mod_sum, 1)

            total(0)
            total(1)
            pe.wait_ge(sum_taken, 2)
            norm_jobs("norm0", 0, T0)

            def pool(b):
                n = b + JOBS["pool_v"]
                pe.wait_ge(acc_free, b + (PHASES["pool_v"][1] + 1))
                pe.wait_ge(tp_evac, n)
                p0 = job_bank(n)
                for f in range(4):
                    for u in range(NT):
                        ins = mm(ps[:, p0 + f // 2, f % 2 * S:f % 2 * S + S],
                                 stage[:, u, f * P:(f + 1) * P], amat[:, bass.ds(b, 1), u, :].rearrange("p a t -> p (a t)"),
                                 start=u == 0, stop=u == NT - 1)
                ins.then_inc(tp_ready, 1)

            pe.wait_ge(x_ready, SPLITS["norm0"] + 4)
            pe.wait_ge(amat_landed, 16)
            phase("pool_v", XA, pool)
            pe.wait_ge(tp_evac, JOBS["pool_v"] + 4)
            total_gate(2, P)
            phase("pool_gate", XA)
            total(3)
            pe.wait_ge(sum_taken, 4)
            B0, A0, _ = PHASES["group"]
            pe.wait_ge(x_ready, SPLITS["pool_v"] + 4)
            group_job = stage_job("group")
            for j in range(CPB):
                if j % 2 == 0:
                    pe.wait_ge(acc_free, A0 + j // 2 - 1)
                chunk(B0, j, XB, KPC * j, A0 + j // 2, j % 2 == 0, j % 2 == 1)
                if j in (5, 7):
                    group_job((j - 5) // 2)
            group_job(2)
            group_job(3)
            pe.wait_ge(x_ready, SPLITS["group"] + 4)
            phase("pool_out", XA)

            pe.wait_ge(tp_evac, JOBS["group"] + 4)
            total(4)
            pe.wait_ge(sum_taken, 5)
            norm_jobs("norm1", 1, T0)
            pe.wait_ge(x_ready, SPLITS["norm1"] + 4)
            phase("idx_q", XB, stage_job("idx_q"))
            phase("idx_kw", XB, cols=80)
            n = JOBS["idx_kw"]
            pe.wait_ge(staged, STAGED["idx_kw"] + 1)
            pe.wait_ge(tp_evac, n - 1)
            for t in range(NT):
                ins = nc.tensor.transpose(ps[:, 4 + n % 2 * 2, t * P:(t + 1) * P], stage[:, t, 0:P], ident)
            ins.then_inc(tp_ready, 1)
            pe.wait_ge(tp_evac, n + 1)
            for h in range(IDX_HEADS):
                if h >= 4:
                    pe.wait_ge(relu_ready, h - 3)
                rows = slice(h % 2 * 64, h % 2 * 64 + 64)
                for t, (a, z) in enumerate(((0, P), (P, CAUS))):
                    ins = mm(ps[:, 4 + h % 4, a:z], qi_t[rows, h // 2, t * P:(t + 1) * P], ki_t[rows, 0:z - a],
                             start=True, stop=True)
                ins.then_inc(sc_ready, 1)
            pe.wait_ge(relu_ready, IDX_HEADS)
            phase("qk", XB, stage_job("qk"))
            phase("v", XB)
            pe.wait_ge(tp_evac, JOBS["qk"] + 8)
            total_gate(5, 1)
            phase("gate", XB)

            def attention(h0, e0, heads, name, q, k, v, ready, value, rows_of=1, width=HD):
                for i in range(heads + 3):
                    if i < heads:
                        h = h0 + i
                        if i >= 2:
                            pe.wait_ge(masked, h - 1)
                        for t, (a, z) in enumerate(((0, P), (P, CAUS))):
                            for r in range(rows_of):
                                ins = mm(ps[:, 4 + i % 2, a:z], q(i, r)[:, t * P:(t + 1) * P], k(i, r)[:, 0:z - a],
                                         start=r == 0, stop=r == rows_of - 1)
                        ins.then_inc(lg_ready, 1)
                    if 1 <= i <= heads:
                        h, b = h0 + i - 1, (i - 1) % 2
                        pe.wait_ge(ready, value + i)
                        if i >= 3:
                            pe.wait_ge(pt_copied, h - 1)
                        for dst, src in ((0, 0), (P, P), (2 * P, 2 * P)):
                            ins = nc.tensor.transpose(ps[:, 6 + b, dst:dst + P], probs[:, b, src:src + P], ident)
                        ins.then_inc(pt_ready, 1)
                    if name and i >= 6 and i % 4 == 2:
                        n = (i - 6) // 4
                        job(JOBS[name] + n, stage, staged, STAGED[name] + n + 1, bank=2)
                    if 2 <= i < heads + 2:
                        h, b = h0 + i - 2, (i - 2) % 2
                        pe.wait_ge(pt_copied, h + 1)
                        if i >= 4:
                            pe.wait_ge(o_done, h - 1)
                        mm(ps[:, b, 0:width], probs_t[:, b, 0:P], v(i - 2, 0), start=True, stop=True)
                        mm(ps[:, b, width:2 * width], probs_t[:, b, P:2 * P], v(i - 2, 0), start=True, stop=False)
                        mm(ps[:, b, width:2 * width], probs_t[:, b, 2 * P:CAUS], v(i - 2, 1), start=False, stop=True
                           ).then_inc(pv_ready, 1)

            pe.wait_ge(acc_free, PHASES["gate"][1] + 4)
            pe.wait_ge(tp_evac, JOBS["qk"] + 8)
            attention(0, 0, DSA_HEADS, "attn", lambda i, r: qk_t[:, i, :], lambda i, r: qk_t[:, DSA_HEADS + i, :],
                      lambda i, u: T2[:, u, i * HD:(i + 1) * HD], exp_ready, 0)
            pe.wait_ge(x_ready, SPLITS["attn"] + 4)
            phase("attn_out", XA)

            norm_jobs("norm2", 2, T1)
            pe.wait_ge(x_ready, SPLITS["norm2"] + 4)
            a0 = PHASES["m_qk"][1]
            phase("m_qk", XB, lambda b: job(b + JOBS["m_qk"], stage, acc_free, b + (a0 + 1)))
            phase("m_v", XB)
            phase("m_o", XB)
            phase("m_if", XB, cols=8)

            pe.wait_ge(g_in, 3)
            pe.wait_ge(acc_free, PHASES["m_if"][1] + 1)
            mm(ps[:, 2, 0:4], cum, gate_f[:, 0, :], start=True, stop=True)
            mm(ps[:, 2, 4:8], cum, gate_f[:, 1, :], start=True, stop=False)
            mm(ps[:, 2, 4:8], ones, gate_f[:, 0, :], start=False, stop=True).then_inc(g_mm, 1)
            pe.wait_ge(g_in, 4)
            pe.wait_ge(conv_done, 4)
            for h in range(M_HEADS):
                for t in range(NT):
                    at = h % 2 * S + t * P
                    ins = mm(ps[:, 4 + h // 2, at:at + P], ones, m_diag[:, t, h, :], start=True, stop=True)
            ins.then_inc(g_mm, 1)
            pe.wait_ge(g_dve, 1)
            mq = feat(0)
            attention(DSA_HEADS, 0, M_HEADS, None, lambda i, r: mq[:, 2 * i + r, :], lambda i, r: mq[:, 8 + 2 * i + r, :],
                      lambda i, u: m_v[:, u, i * S:(i + 1) * S], masked, DSA_HEADS, rows_of=2, width=S)
            for n in range(2):
                job(JOBS["mlstm"] + n, stage, staged, STAGED["mlstm"] + n + 1, bank=2)

            pe.wait_ge(o_done, DSA_HEADS + M_HEADS)
            pe.wait_ge(tp_evac, JOBS["mlstm"] + 2)
            phase("a_qk", XB, stage_job("a_qk"))
            phase("a_v", XB)
            pe.wait_ge(acc_free, PHASES["a_v"][1] + 2)
            pe.wait_ge(tp_evac, JOBS["a_qk"] + 4)
            aq = feat(2)
            attention(DSA_HEADS + M_HEADS, DSA_HEADS, MOBA_HEADS, "moba", lambda i, r: aq[:, i, :],
                      lambda i, r: aq[:, MOBA_HEADS + i, :], lambda i, u: a_v[:, u, i * HD:(i + 1) * HD],
                      exp_ready, DSA_HEADS)
            pe.wait_ge(o_done, DSA_HEADS + M_HEADS + MOBA_HEADS)
            pe.wait_ge(tp_evac, JOBS["moba"] + 2)
            phase("g_m", XB)
            phase("g_a", XB)

            pe.wait_ge(x_ready, SPLITS["moba"] + 2)
            B0, A0, n = PHASES["branch"]
            branch_job = stage_job("branch")

            def branch(b, first=False):
                for half in range(2):
                    A = b * 2 + (A0 + half)
                    pe.wait_ge(acc_free, A - 1)
                    for j in range(4):
                        chunk(b + B0, 4 * half + j, XA, 8 * half + KPC * j, A, j == 0, j == 3)
                    if half == 0 and not first:
                        branch_job(b - 1)

            branch(0, first=True)
            with pe.Fori(1, n) as b:
                branch(b)
            branch_job(3)
            pe.wait_ge(x_ready, SPLITS["branch"] + 4)
            phase("mix_out", XB)

            norm_jobs("norm3", 3, T2)
            pe.wait_ge(x_ready, SPLITS["norm3"] + 4)
            ffn_job = stage_job("ffn")
            X0 = SPLITS["ffn"]

            def up(e, B, A, after=None):
                for h in range(2):
                    blk(B + h, A + h, XA, True, (lambda: ffn_job(e * 2 + (h - 1))) if h == 1 or after == "up" else None)

            def dn(e, half, B, A, last=False):
                pe.wait_ge(x_ready, e * 2 + (X0 + 2))
                for q in range(4):
                    pe.wait_ge(acc_free, A + (q - 1))
                    for j in range(4):
                        chunk(B + q // 2, 4 * (q % 2) + j, XB, 8 * half + KPC * j, A + q, j == 0, j == 3)
                    if q == 0 and not last:
                        ffn_job(e * 2 + 3)

            up(0, FB, FA, after="norm")
            up(1, FB + 2, FA + 2, after="up")
            dn(0, 0, FB + 4, FA + 4)
            with pe.Fori(0, 3) as i:
                up(i * 2 + 2, i * 8 + (FB + 6), i * 12 + (FA + 8))
                dn(i * 2 + 1, 1, i * 8 + (FB + 8), i * 12 + (FA + 10))
                up(i * 2 + 3, i * 8 + (FB + 10), i * 12 + (FA + 14))
                dn(i * 2 + 2, 0, i * 8 + (FB + 12), i * 12 + (FA + 16))
            dn(7, 1, FB + 30, FA + 44, last=True)


_INS = [
    "x", "c", "positions", "norm_g", "mod_w", "mod_b", "pool_w_in", "pool_w_grp", "pool_scale", "pool_w_out",
    "attn_w_in", "attn_w_out", "final_g", "positions_2", "norm_mix_pre_2", "w_in_2", "conv_w_2", "conv_b_2",
    "i_bias_2", "f_bias_2", "mlstm_norm_2", "w_branch_m_2", "w_branch_a_2", "w_out_2", "norm_mix_post_2",
    "norm_ffn_pre_2", "w_up_2", "w_down_2", "norm_ffn_post_2",
]


def shape_constants():
    far = np.float32(FAR)
    con = np.zeros((P, C_ALL), np.float32)
    con[:, C_ID:C_ID + P] = np.eye(P)
    key, query = np.arange(P)[None, :], np.arange(P)[:, None]
    triangle = np.where(key <= query, np.float32(0), far)
    con[:, C_TRI:C_TRI + P] = triangle
    con[:, C_TRI + 2 * P:C_TRI + 3 * P] = triangle
    con[:, C_CUM:C_CUM + P] = (query <= key)
    con[:, C_ONE:C_ONE + P] = 1.0
    col = C_FRQ
    for theta, width, half in ((500000.0, 32, FRQ1), (500000.0, 16, FRQI), (10000.0, 128, FRQ2)):
        con[:, col:col + half] = theta ** (-np.arange(half) * 2.0 / width)
        col += half
    win = np.zeros((len(WINDOWS), S, S), np.float64)
    for g, w in enumerate(WINDOWS):
        for t in range(S):
            lo = max(t + 1 - w, 0)
            win[g, lo:t + 1, t] = 1.0 / (t + 1 - lo)
            win[g, t, t] -= 1.0
    win = win.astype(np.float32).reshape(len(WINDOWS), NT, P, S).transpose(2, 0, 1, 3)
    return con, np.ascontiguousarray(win)


def kernel(**inputs):
    import concourse.bacc as bacc
    from concourse.bass_utils import run_bass_kernel_spmd

    nc = bacc.Bacc("TRN2", target_bir_lowering=False, num_devices=1, dynamic_dma_scratch_size=1024)
    arrays, args = {}, {}
    for name in _INS:
        a = np.ascontiguousarray(inputs[name])
        arrays[f"in_{name}"] = a
        args[name] = nc.dram_tensor(f"in_{name}", a.shape, mybir.dt.from_np(a.dtype), kind="ExternalInput").ap()
    for name, a in zip(("consts", "windows"), shape_constants()):
        arrays[f"in_{name}"] = a
        args[name] = nc.dram_tensor(f"in_{name}", a.shape, F32, kind="ExternalInput").ap()
    args["gate_row"] = nc.dram_tensor("gate_row", (1, D), F32).ap()
    args["resid"] = nc.dram_tensor("resid", (2, S, D), F32).ap()
    args["out"] = nc.dram_tensor("out", (1, S, D), F32, kind="ExternalOutput").ap()
    build(nc, **args)
    r = run_bass_kernel_spmd(nc, [arrays], core_ids=[0])
    return r.results[0]["out"]
```

```python
from contextlib import ExitStack, contextmanager

import concourse.bass as bass
import numpy as np
from concourse import mybir

F32 = mybir.dt.float32
F32R = mybir.dt.float32r
I32 = mybir.dt.int32
ALU = mybir.AluOpType
ACT = mybir.ActivationFunctionType

P = 128
S = 256
NT = S // P
D = 2048
KC = D // P
NBLK = 512
KPC = 2
CPB = KC // KPC
RAW = 8
SPL = 4
AHEAD = 3
EPS = 1e-6
HD = 128
CAUS = P + S
FAR = -3.0e38
TAKEN = -3.3e38
UNPICKED = -1.0e30
MAGIC = 12582912.0
TWO_PI = (6.28125, 0.0019350051879882812, 3.019915981956752e-07)
PI_CLAMP = 3.1415925
WINDOWS = (2, 4, 8, 16)
TOPK = 64
DSA_HEADS, MOBA_HEADS, M_HEADS, IDX_HEADS = 16, 8, 4, 16
IDX_COL = 4 * D
N_FFN = 8

C_ID, C_TRI, C_CUM, C_ONE, C_FRQ = 0, 128, 512, 640, 768
FRQ1, FRQI, FRQ2 = 16, 8, 64
C_ALL = C_FRQ + FRQ1 + FRQI + FRQ2

PHASES = {}


def _plan():
    b = a = 0
    for name, blocks, accs in (
        ("pool_v", 4, 4), ("pool_gate", 4, 4), ("group", 1, 4), ("pool_out", 4, 4), ("idx_q", 2, 2), ("idx_kw", 1, 1),
        ("qk", 8, 8), ("v", 4, 4), ("gate", 4, 4), ("attn_out", 4, 4), ("m_qk", 4, 4), ("m_if", 1, 1), ("m_v", 2, 2),
        ("m_o", 2, 2), ("a_qk", 4, 4), ("a_v", 2, 2), ("g_m", 4, 4), ("g_a", 4, 4), ("branch", 4, 8),
        ("mix_out", 4, 4), ("ffn", 32, 48),
    ):
        PHASES[name] = (b, a, blocks)
        b, a = b + blocks, a + accs
    return b


N_BLOCKS = _plan()
RIDERS = {"pool_v": 2, "pool_gate": 3, "pool_out": 4, "v": 5}
RIDE = {u: 2 * KC + 2 * KC * (u - 2) for u in RIDERS.values()}

JOBS, SPLITS = {}, {}


def _jobs():
    n = s = 0
    for name, jobs, split in (
        ("norm0", 4, True), ("pool_v", 4, True), ("group", 4, True), ("norm1", 4, True), ("idx_q", 2, False),
        ("idx_kw", 2, False), ("qk", 8, False), ("attn", 4, True), ("norm2", 4, True), ("m_qk", 4, False), ("m_if", 1, False),
        ("mlstm", 2, True), ("a_qk", 4, False), ("moba", 2, True), ("branch", 4, True), ("norm3", 4, True),
        ("ffn", 16, True),
    ):
        JOBS[name], SPLITS[name] = n, s
        n, s = n + jobs, s + (jobs if split else 0)


_jobs()
STAGED = {}


def _staged():
    n = 0
    for name, jobs in (("group", 4), ("idx_q", 2), ("idx_kw", 1), ("qk", 8), ("attn", 4), ("norm2", 4), ("mlstm", 2), ("a_qk", 4),
                       ("moba", 2), ("branch", 4), ("ffn", 16)):
        STAGED[name] = n
        n += jobs


_staged()
SQ = {"norm1": 2, "norm2": 10, "mlstm": 26, "mix_out": 34, "norm3": 42, "ffn": 46}

COMBINED = {"pool_out": 0, "ffn": 4}




class Chain:

    def __init__(self, eng, sem):
        self.eng, self.sem, self.n, self.off = eng, sem, 0, 0

    def __call__(self, ins):
        ins.then_inc(self.sem, 1)
        self.n += 1
        self.eng.wait_ge(self.sem, self.off + self.n)

    @contextmanager
    def loop(self, first, last, per):
        start = self.n
        with self.eng.Fori(first, last) as b:
            self.off = (b - first) * per if per else 0
            yield b
        assert self.n - start == per, f"{self.n - start} steps, not {per}"
        self.n, self.off = start + per * (last - first), 0


def build(nc, x, c, positions, norm_g, mod_w, mod_b, pool_w_in, pool_w_grp, pool_scale, pool_w_out, attn_w_in,
          attn_w_out, final_g, positions_2, norm_mix_pre_2, w_in_2, conv_w_2, conv_b_2, i_bias_2, f_bias_2,
          mlstm_norm_2, w_branch_m_2, w_branch_a_2, w_out_2, norm_mix_post_2, norm_ffn_pre_2, w_up_2, w_down_2,
          norm_ffn_post_2, consts, windows, gate_row, resid, out):
    with ExitStack() as ctx:
        def sb(name, shape, dt=F32):
            return ctx.enter_context(nc.sbuf_tensor(name, shape, dt))

        def sem(name):
            return ctx.enter_context(nc.semaphore(name))

        raw = sb("raw", [P, RAW, KPC, NBLK])
        w_hi = sb("w_hi", [P, SPL, KPC, NBLK], F32R)
        w_lo = sb("w_lo", [P, SPL, KPC, NBLK], F32R)
        xa_hi, xa_lo = sb("xa_hi", [P, KC, S], F32R), sb("xa_lo", [P, KC, S], F32R)
        xb_hi, xb_lo = sb("xb_hi", [P, KC, S], F32R), sb("xb_lo", [P, KC, S], F32R)
        XA, XB = (xa_hi, xa_lo), (xb_hi, xb_lo)
        T = sb("T", [P, 4, 2 * D])
        stage = sb("stage", [P, NT, NBLK])
        tmp = sb("tmp", [P, 4, S])
        wide = sb("wide", [P, D])
        probs_t = sb("probs_t", [P, 2, CAUS])
        con = sb("con", [P, C_ALL])
        pick = sb("pick", [P, CAUS])
        vec1, vec2 = sb("vec1", [P, P]), sb("vec2", [P, P])
        vec3 = sb("vec3", [P, 2 * KC])
        rot = sb("rot", [P, 2, NT, FRQ1 + FRQI + FRQ2])
        posi = sb("posi", [P, 2, NT], I32)
        posf = sb("posf", [P, 2, NT])
        csil = sb("csil", [P, KC])
        scl = sb("scl", [P, 2, KC])
        idx_w = sb("idx_w", [P, NT, IDX_HEADS])
        ifb = sb("ifb", [P, 8])
        small = sb("small", [P, 12, 8])
        ms = sb("ms", [P, 8])
        ms_part = sb("ms_part", [P, 2, NT, 4])
        rs = sb("rs", [P, 8])
        t8 = sb("t8", [P, 8])
        best = sb("best", [P, NT, 8])
        mx = sb("mx", [P, 2, NT])
        nmx = sb("nmx", [P, 2, NT])
        den = sb("den", [P, 4, NT])
        rden = sb("rden", [P, 2, NT])

        ps = ctx.enter_context(nc.psum_tensor("ps", [P, 8, 512], F32))

        ident, tri, cum = con[:, C_ID:C_ID + P], con[:, C_TRI:C_TRI + CAUS], con[:, C_CUM:C_CUM + P]
        ones, freqs = con[:, C_ONE:C_ONE + P], con[:, C_FRQ:C_ALL]

        def tok(i, cols=D, at=0):
            return T[:, i, at:at + NT * cols].rearrange("p (t n) -> p t n", t=NT)

        def feat(i, n=KC):
            return T[:, i, 0:n * S].rearrange("p (f t) -> p f t", t=S)

        T0, T1, T2, T3 = (tok(i) for i in range(4))
        qk_t = T[:, 0:2, :].rearrange("p a (f t) -> p (a f) t", t=S)
        amat = T[:, 2, 0:4 * NT * S].rearrange("p (g u t) -> p g u t", g=4, u=NT)
        mod_raw = T[:, 1:3, :].rearrange("p a (s n) -> p (a s) n", n=D)
        sum_first = T[:, 3, :].rearrange("p (a n) -> p a n", a=2)
        mod_acc = [sum_first[:, 0], sum_first[:, 1], wide[:], T[:, 0, 0:D], T[:, 0, D:2 * D], wide[:]]
        ride_raw = T[:, 3, :].rearrange("p (s n) -> p s n", s=4)
        qi_t = feat(3, 8)
        ki_t = pick[:, 0:S]
        score, qi_now = probs_t[:, 0, :], probs_t[:, 1, 0:S]
        rs_diag = pick[:, 0:S].rearrange("p (t n) -> p t n", t=NT)
        final_w = T[:, 3, 0:D]
        m_v, m_o = T1[:, :, 0:1024], T1[:, :, 1024:2048]
        m_num = T[:, 2, 0:2048].rearrange("p (h t n) -> p h t n", h=M_HEADS, t=NT)
        a_v = tok(3, 1024)
        probs = tmp[:].rearrange("p f t -> p (f t)")[:, 0:2 * CAUS].rearrange("p (b n) -> p b n", b=2)
        x_tmp = wide[:, 0:4 * S].rearrange("p (f t) -> p f t", t=S)
        stage_f = stage[:].rearrange("p t (f n) -> p (t f) n", n=S)
        tmp_t = tmp[:].rearrange("p f t -> p (f t)").rearrange("p (t n) -> p t n", t=NT)
        m_dec = T[:, 2, 2048:2048 + M_HEADS * CAUS].rearrange("p (h n) -> p h n", h=M_HEADS)
        m_diag = tmp[:].rearrange("p f t -> p (f t)").rearrange("p (t h n) -> p t h n", t=NT, h=M_HEADS)
        gate_i, gate_u, gate_f, gate_w, cum_f, m_max, m_nmax, m_floor, m_e = (
            small[:, i, :].rearrange("p (t h) -> p t h", t=NT) for i in range(9))
        r_mix, r_ffn, r_out = (small[:, 11, 2 * i:2 * i + 2] for i in range(3))
        C_, G0, G1, PSC, MIXP, FFNP, CVB, MLN = (vec1[:, 16 * i:16 * i + 16] for i in range(8))

        def job_bank(n):
            return n % 2 * 2 + 4 if isinstance(n, int) else 4

        landed = [sem(f"landed{i}") for i in range(RAW)]
        hi_ready, lo_ready, w_used = sem("hi_ready"), sem("lo_ready"), sem("w_used")
        acc_free = sem("acc_free")
        staged, combined = sem("staged"), sem("combined")
        tp_ready, tp_evac, xh_ready, x_ready = sem("tp_ready"), sem("tp_evac"), sem("xh_ready"), sem("x_ready")
        dve_step, act_step = sem("dve_step"), sem("act_step")
        in_landed, x_landed, vec_landed, amat_landed = sem("in_landed"), sem("x_landed"), sem("vec_landed"), sem("amat_landed")
        vec_tp, vec_done = sem("vec_tp"), sem("vec_done")
        csil_ready, sin_in, rot_ready = sem("csil_ready"), sem("sin_in"), sem("rot_ready")
        mod_landed = [sem(f"mod_landed{i}") for i in range(4)]
        ride_landed = [sem(f"ride_landed{i}") for i in range(4)]
        mod_used, acc_zero, bias_landed = sem("mod_used"), sem("acc_zero"), sem("bias_landed")
        mod_sum, sum_taken, row_ready, row_stored = sem("mod_sum"), sem("sum_taken"), sem("row_ready"), sem("row_stored")
        sq_part, ms_ready, root_ready, xn_ready = (
            sem("sq_part"), sem("ms_ready"), sem("root_ready"), sem("xn_ready"))
        sum_ready = sem("sum_ready")
        wide_landed = sem("wide_landed")
        res_landed, res_stored, res_done = sem("res_landed"), sem("res_stored"), sem("res_done")
        scl_ready, picked, qi_ready = sem("scl_ready"), sem("picked"), sem("qi_ready")
        sc_ready, relu_ready = sem("sc_ready"), sem("relu_ready")
        lg_ready, masked, exp_ready = sem("lg_ready"), sem("masked"), sem("exp_ready")
        pt_ready, pt_copied, pv_ready, o_done = sem("pt_ready"), sem("pt_copied"), sem("pv_ready"), sem("o_done")
        conv_in, conv_done = sem("conv_in"), sem("conv_done")
        g_in, g_act, g_mm, g_dve = sem("g_in"), sem("g_act"), sem("g_mm"), sem("g_dve")
        out_done, out_stored = sem("out_done"), sem("out_stored")

        def plain(w, col0):
            v = w.rearrange("(k p) n -> p k n", p=P)
            return lambda b, j: v[:, KPC * j:KPC * j + KPC, bass.ds(b * NBLK + col0, NBLK)]

        def narrow(w, col0, n):
            v = w.rearrange("(k p) n -> p k n", p=P)
            return lambda b, j: v[:, KPC * j:KPC * j + KPC, col0:col0 + n]

        grp = pool_w_grp[0].rearrange("g (k p) n -> p g k n", p=P)
        bm, ba = (w[0].rearrange("(k p) n -> p k n", p=P) for w in (w_branch_m_2, w_branch_a_2))
        down = w_down_2[0].rearrange("(e k p) n -> p e k n", e=N_FFN, p=P)

        def src_group(b, j):
            return grp[:, j // 2, KPC * (j % 2):KPC * (j % 2) + KPC, :]

        def src_branch(b, j):
            w, k = (bm, j) if j < 4 else (ba, j - 4)
            return w[:, KPC * k:KPC * k + KPC, bass.ds(b * NBLK, NBLK)]

        up = plain(w_up_2[0], 0)
        SOURCES = {
            "pool_v": plain(pool_w_in[0], 0), "pool_gate": plain(pool_w_in[0], D), "group": src_group,
            "pool_out": plain(pool_w_out[0], 0), "idx_q": plain(attn_w_in[0], IDX_COL),
            "idx_kw": narrow(attn_w_in[0], IDX_COL + 1024, 80), "qk": plain(attn_w_in[0], 0),
            "v": plain(attn_w_in[0], 2 * D), "gate": plain(attn_w_in[0], 3 * D), "attn_out": plain(attn_w_out[0], 0),
            "m_qk": plain(w_in_2[0], 0), "m_v": plain(w_in_2[0], 2048), "m_o": plain(w_in_2[0], 3072),
            "m_if": narrow(w_in_2[0], 4096, 8), "a_qk": plain(w_in_2[0], 4104), "a_v": plain(w_in_2[0], 6152),
            "g_m": plain(w_in_2[0], 7176), "g_a": plain(w_in_2[0], 9224), "branch": src_branch,
            "mix_out": plain(w_out_2[0], 0),
        }

        FB, FA, _ = PHASES["ffn"]

        block = ctx.enter_context(nc.Block())

        @block.sync
        def _(sp):
            def load(src, b, j, B, first=False, cols=NBLK):
                if not first:
                    sp.wait_ge(lo_ready, B * CPB + (j + 1 - RAW))
                sp.dma_start(raw[:, j, :, 0:cols], src(b, j)).then_inc(landed[j], 16)

            def load_phase(name, cols=NBLK):
                B0, _, n = PHASES[name]
                src, u = SOURCES[name], RIDERS.get(name)
                for j in range(CPB):
                    load(src, 0, j, B0, first=B0 == 0, cols=cols)
                if u:
                    if name == "pool_v":
                        sp.wait_ge(scl_ready, 2)
                    if name == "v":
                        sp.wait_ge(qi_ready, 8)
                    for j in range(CPB):
                        ride(u, 0, j, first=u == 2 and j < 4)
                if n > 1:
                    with sp.Fori(1, n) as b:
                        for j in range(CPB):
                            load(src, b, j, b + B0, cols=cols)
                            if u:
                                ride(u, b, j)

            sp.dma_start(con[:], consts).then_inc(in_landed, 16)
            for v, row, n, src in (
                (0, 0, 16, c[0]), (0, 16, 16, norm_g[0]), (0, 32, 16, norm_g[1]), (0, 48, 16, pool_scale[0]),
                (0, 64, 16, norm_mix_pre_2[0]), (0, 80, 16, norm_ffn_pre_2[0]), (0, 96, 16, conv_b_2[0]),
                (0, 112, 8, mlstm_norm_2[0]), (1, 0, 16, conv_w_2[0, 0]), (1, 16, 16, conv_w_2[0, 1]),
                (1, 32, 16, conv_w_2[0, 2]), (1, 48, 16, conv_w_2[0, 3]),
            ):
                sp.dma_start(stage[row:row + n, v, 0:P], src.rearrange("(r n) -> r n", n=P)).then_inc(vec_landed, 16)
            with nc.allow_non_contiguous_dma(reason="a position to a partition"):
                for i, pos in enumerate((positions, positions_2)):
                    sp.dma_start(posi[:, i, :], pos[0].rearrange("(t p) -> p t", p=P)).then_inc(in_landed, 16)
            for i, bias in enumerate((i_bias_2, f_bias_2)):
                sp.dma_start(ifb[:, 4 * i:4 * i + 4], bias[0:1, :].to_broadcast([P, 4])).then_inc(in_landed, 16)

            sp.dma_start(T0[:], x[0].rearrange("(t p) n -> p t n", p=P)).then_inc(x_landed, 16)

            mws = [mod_w[i].rearrange("(k p) (u n) -> p u k n", p=P, n=D) for i in range(2)]
            for u in range(2):
                for k in range(KC):
                    if u or k >= 4:
                        sp.wait_ge(mod_used, u * KC + k - 3)
                    sp.dma_start(mod_raw[:, k % 4, :], mws[0][:, u, k, :]).then_inc(mod_landed[k % 4], 16)

            def ride(u, b, j, first=False):
                if not first:
                    sp.wait_ge(mod_used, b * CPB + (RIDE[u] + j - 3))
                sp.dma_start(ride_raw[:, j % 4:j % 4 + 1, :],
                             mws[u // 3][:, u % 3, bass.ds(b * 4 + j // 2, 1), j % 2 * 1024:j % 2 * 1024 + 1024]
                             ).then_inc(ride_landed[j % 4], 16)

            load_phase("pool_v")
            load_phase("pool_gate")
            for name in ("group", "pool_out", "idx_q"):
                load_phase(name)
            load_phase("idx_kw", cols=80)
            for name in ("qk", "v", "gate", "attn_out", "m_qk"):
                load_phase(name)
            load_phase("m_if", cols=8)
            for name in ("m_v", "m_o", "a_qk", "a_v", "g_m", "g_a", "branch", "mix_out"):
                load_phase(name)

            def ffn_up(e, B, first=False):
                for h in range(2):
                    for j in range(CPB):
                        load(lambda b, j: up(e * 2 + h, j), 0, j, B + h)

            def ffn_down(e, B):
                for h in range(2):
                    for j in range(CPB):
                        load(lambda b, j: down[:, bass.ds(e, 1), KPC * (j % 4):KPC * (j % 4) + KPC,
                                               NBLK * (2 * h + j // 4):NBLK * (2 * h + j // 4) + NBLK]
                             .rearrange("p e k n -> p (e k) n"), 0, j, B + h)

            ffn_up(0, FB)
            ffn_up(1, FB + 2)
            ffn_down(0, FB + 4)
            with sp.Fori(0, 3) as i:
                ffn_up(i * 2 + 2, i * 8 + (FB + 6))
                ffn_down(i * 2 + 1, i * 8 + (FB + 8))
                ffn_up(i * 2 + 3, i * 8 + (FB + 10))
                ffn_down(i * 2 + 2, i * 8 + (FB + 12))
            ffn_down(7, FB + 30)
            for i in range(2 * NT):
                t, c0 = i % 2, i // 2 * (D // 2)
                sp.wait_ge(out_done, i + 1)
                sp.dma_start(out[0, t * P:(t + 1) * P, c0:c0 + D // 2], T3[:, t, c0:c0 + D // 2]
                             ).then_inc(out_stored, 16)
            sp.wait_ge(out_stored, 16 * 2 * NT)

        @block.gpsimd
        def _(pool):
            def tokens(dram):
                return dram.rearrange("(t p) n -> p t n", p=P)

            def widen(row, dst=wide[:]):
                pool.dma_start(dst, row.to_broadcast([P, D])).then_inc(wide_landed, 16)

            def clear(u):
                nc.gpsimd.memset(mod_acc[u], 0.0).then_inc(acc_zero, 1)
                pool.wait_ge(acc_zero, u + 1)
                if u:
                    pool.wait_ge(bias_landed, 16 * u)
                pool.dma_start(mod_acc[u][0:1, :], mod_b[u // 3:u // 3 + 1, u % 3 * D:u % 3 * D + D]
                               ).then_inc(bias_landed, 16)

            for u in range(3):
                clear(u)
            pool.wait_ge(mod_used, 2 * KC)
            pool.dma_start(amat[:], windows).then_inc(amat_landed, 16)
            pool.wait_ge(tp_ready, JOBS["norm0"] + 4)
            clear(3)
            clear(4)
            pool.wait_ge(tp_ready, JOBS["pool_v"] + 4)
            pool.dma_start(T2[:], tokens(x[0])).then_inc(res_landed, 16)
            pool.wait_ge(combined, 4)
            clear(5)
            pool.dma_start(tokens(resid[0]), T2[:]).then_inc(res_stored, 16)
            pool.wait_ge(pv_ready, DSA_HEADS)
            pool.wait_ge(res_stored, 16)
            pool.dma_start(T0[:], tokens(resid[0])).then_inc(res_landed, 16)
            pool.wait_ge(o_done, DSA_HEADS)
            pool.wait_ge(row_stored, 16)
            widen(final_g.rearrange("(a n) -> a n", a=1), final_w)
            pool.wait_ge(x_ready, SPLITS["attn"] + 4)
            pool.wait_ge(wide_landed, 16)
            widen(gate_row)
            pool.wait_ge(res_done, 1)
            pool.dma_start(tokens(resid[1]), T2[:]).then_inc(res_stored, 16)
            pool.wait_ge(x_ready, SPLITS["moba"] + 2)
            pool.wait_ge(wide_landed, 32)
            widen(norm_mix_post_2)
            pool.wait_ge(pv_ready, DSA_HEADS + M_HEADS + MOBA_HEADS)
            pool.wait_ge(res_stored, 32)
            pool.dma_start(T3[:], tokens(resid[1])).then_inc(res_landed, 16)
            pool.wait_ge(res_done, 2)
            widen(norm_ffn_post_2)

        @block.scalar
        def _(act):
            step = Chain(act, act_step)

            def hi(B, o, cols=NBLK):
                lap = B + o // CPB
                act.wait_ge(landed[o % RAW], lap * 16 + 16)
                if not (isinstance(B, int) and B == 0 and o < SPL):
                    act.wait_ge(w_used, lap * CPB + (o % CPB + 1 - SPL))
                nc.scalar.copy(w_hi[:, o % SPL, :, 0:cols], raw[:, o % RAW, :, 0:cols]).then_inc(hi_ready, 1)

            def evac(dst, A, done, func=ACT.Copy, scale=None):
                act.wait_ge(w_used, done)
                if scale is not None:
                    for t in range(NT):
                        ins = nc.scalar.activation(dst[:, t, :], ps[:, bass.ds((A % 2) * 2 + t, 1), :]
                                                   .rearrange("p a n -> p (a n)"), func, scale=scale[:, t:t + 1])
                    ins.then_inc(acc_free, 1)
                    return
                nc.scalar.activation(dst, ps[:, bass.ds((A % 2) * 2, 2), :], func).then_inc(acc_free, 1)

            def narrow(name, cols, job, hooks=None):
                B0, A0, _ = PHASES[name]
                blk(B0, hooks, cols=cols)
                act.wait_ge(tp_ready, job)
                act.wait_ge(w_used, B0 * CPB + CPB)
                nc.scalar.copy(stage[0:cols, 0, 0:S], ps[0:cols, A0 % 2 * 2, 0:S]).then_inc(acc_free, 1)

            def split(n, s, X, g, src):
                act.wait_ge(tp_evac, n + 1)
                nc.scalar.copy(X[0][:, bass.ds(g * 4, 4), :], src).then_inc(xh_ready, 1)

            def blk(B, hooks=None, last=False, cols=NBLK):
                if hooks and AHEAD - 1 in hooks:
                    hooks[AHEAD - 1]()
                for o in range(AHEAD, CPB if last else CPB + AHEAD):
                    hi(B, o, cols if o < CPB else NBLK)
                    if hooks and o in hooks:
                        hooks[o]()

            def phase(name, each, job=None, at=6, first=None):
                B0, A0, n = PHASES[name]
                blk(B0, first)
                each(0, B0, A0)
                if n > 1:
                    with act.Fori(1, n) as b:
                        blk(b + B0, {at: lambda: job(b - 1)} if job else None)
                        each(b, b + B0, b + A0)

            def splits(name, X):
                return lambda b: split(b + JOBS[name], b + SPLITS[name], X, b, tmp[:])

            def root(i, n):
                act.wait_ge(ms_ready, i + 1)
                nc.scalar.activation(rs[:, 0:n], t8[:, 0:n], ACT.Sqrt).then_inc(root_ready, 1)

            def square(k, src, dst, junk):
                nc.scalar.activation(junk, src, ACT.Square, accum_out=dst).then_inc(sq_part, 1)
                act.wait_ge(sq_part, k + 1)

            def squares(k, b, junk, *srcs):
                for i, src in enumerate(srcs):
                    for t in range(NT):
                        square(k + (i * NT + t), src[:, t, :], ms_part[:, i, t, bass.ds(b, 1)], junk)

            def quarter(src, b):
                return src[:, :, bass.ds(b * NBLK, NBLK)]

            junk_a, junk_b = (X[1][:, 0:2, :].rearrange("p f t -> p (f t)") for X in (XA, XB))

            def feed(name, X, scale=None, shift=None):
                def group(g):
                    buf = (tmp[:], stage_f)[g % 2]
                    if shift is not None:
                        n = JOBS[name] + g
                        act.wait_ge(tp_ready, n + 1)
                        if name == "norm0" or g == 0:
                            act.wait_ge(scl_ready, min(g + 1, 2) if name == "norm0" else 3)
                        if g >= 2:
                            act.wait_ge(x_ready, SPLITS[name] + g - 1)
                        p0 = job_bank(n)
                        for f in range(4):
                            ins = nc.scalar.activation(
                                buf[:, f, :], ps[:, p0 + f // 2, f % 2 * S:f % 2 * S + S], ACT.Identity,
                                bias=shift[:, 4 * g + f:4 * g + f + 1], scale=scale[:, 4 * g + f:4 * g + f + 1])
                        ins.then_inc(tp_evac, 1)
                    split(JOBS[name] + g, SPLITS[name] + g, X, g, buf)

                def start():
                    for g in range(2):
                        group(g)
                        if name == "norm0":
                            hi(0, g + 1)

                return {2: start, 3: lambda: group(2), 5: lambda: group(3)}

            def load_table(i, func):
                nc.scalar.activation(small[:, 10, i:i + 1], ones[:, 0:1], func)

            act.wait_ge(vec_done, 1)
            nc.scalar.activation(csil[:], C_, ACT.Silu).then_inc(csil_ready, 1)
            act.wait_ge(sin_in, 1)
            nc.scalar.activation(rot[:], rot[:], ACT.Sin).then_inc(rot_ready, 1)

            act.wait_ge(x_landed, 16)
            for t in range(NT):
                square(t, T0[:, t, :], ms[:, t:t + 1], xb_lo[:, 0:8, :].rearrange("p f t -> p (f t)"))
            root(0, NT)
            hi(0, 0)

            def pool_v(b, B, A):
                act.wait_ge(tp_ready, b + JOBS["pool_v"])
                act.wait_ge(x_ready, SPLITS["norm0"] + 4)
                evac(stage[:], A, B * CPB + CPB)

            pool_job = splits("pool_v", XB)
            phase("pool_v", pool_v, pool_job, first=feed("norm0", XA, scl[:, 0, :], vec3[:, 0:16]))
            phase("pool_gate", lambda b, B, A: evac(T1[:, :, bass.ds(b * NBLK, NBLK)], A, B * CPB + CPB, ACT.Silu),
                  first={6: lambda: pool_job(3)})
            act.wait_ge(mod_sum, 4)
            nc.scalar.copy(wide[:].rearrange("p (b n) -> p b n", b=4), ps[:, 4:8, :]).then_inc(sum_taken, 1)

            B0, A0, _ = PHASES["group"]
            jg, sg = JOBS["group"], SPLITS["group"]
            for o in range(AHEAD, CPB + AHEAD):
                hi(B0, o)
                if o in (4, 6, 8, 10):
                    g = (o - 4) // 2
                    act.wait_ge(tp_ready, jg + g)
                    evac(stage[:], A0 + g, B0 * CPB + 2 * g + 2)
                if o in (7, 9):
                    split(jg + (o - 7) // 2, sg + (o - 7) // 2, XA, (o - 7) // 2, tmp[:])

            def to_residual(name, job):
                def each(b, B, A):
                    act.wait_ge(tp_ready, job)
                    if COMBINED[name] or not isinstance(b, int):
                        act.wait_ge(combined, b + COMBINED[name])
                    evac(stage[:], A, B * CPB + CPB)
                return each

            load_table(1, ACT.Sqrt)

            def pool_squares(b):
                act.wait_ge(combined, b + 1)
                squares(b * NT + SQ["norm1"], b, junk_b, quarter(T2, b))

            phase("pool_out", to_residual("pool_out", JOBS["group"] + 4), pool_squares, at=4,
                  first={2: lambda: split(jg + 2, sg + 2, XA, 2, tmp[:]), 6: lambda: split(jg + 3, sg + 3, XA, 3, tmp[:])})
            pool_squares(3)
            root(1, NT)

            def to_stage(name, norm=None, scale=None):
                def each(b, B, A):
                    act.wait_ge(tp_ready, b + JOBS[name])
                    if norm:
                        act.wait_ge(x_ready, SPLITS[norm] + 4)
                    evac(stage[:], A, B * CPB + CPB, scale=scale)
                return each

            phase("idx_q", to_stage("idx_q", "norm1"), first=feed("norm1", XB, scl[:, 1, :], vec3[:, 16:32]))
            narrow("idx_kw", 80, JOBS["idx_kw"])

            def index_relu(b):
                act.wait_ge(staged, b + STAGED["qk"])
                for i in range(2):
                    act.wait_ge(sc_ready, b * 2 + (i + 1))
                    nc.scalar.activation(probs[:, i, :], ps[:, 6 + i, 0:CAUS], ACT.Relu).then_inc(relu_ready, 1)

            to_qk = to_stage("qk")
            B0, A0, n = PHASES["qk"]
            with act.Fori(0, n) as b:
                blk(b + B0, {8: lambda: index_relu(b)})
                to_qk(b, b + B0, b + A0)
            act.wait_ge(res_stored, 16)
            phase("v", lambda b, B, A: evac(T2[:, :, bass.ds(b * NBLK, NBLK)], A, B * CPB + CPB))
            act.wait_ge(mod_sum, 7)
            nc.scalar.copy(wide[0:1, :].rearrange("p (b n) -> p b n", b=4), ps[0:1, 4:8, :]).then_inc(row_ready, 1)
            act.wait_ge(row_ready, 1)
            act.dma_start(gate_row, wide[0:1, :]).then_inc(row_stored, 16)
            phase("gate", lambda b, B, A: evac(T3[:, :, bass.ds(b * NBLK, NBLK)], A, B * CPB + CPB, ACT.Silu))
            load_table(4, ACT.Exp)
            act.wait_ge(picked, 1)

            def copy_probs(h, i):
                act.wait_ge(pt_ready, h + 1)
                if i >= 2 or h >= DSA_HEADS:
                    act.wait_ge(pv_ready, h - 1)
                nc.scalar.copy(probs_t[:, i % 2, :], ps[:, 6 + i % 2, 0:CAUS]).then_inc(pt_copied, 1)

            def attention(h0, e0, heads, name, g0):
                for i in range(heads + 3):
                    if i < heads:
                        act.wait_ge(masked, h0 + i + 1)
                        for t, (a, z) in enumerate(((0, P), (P, CAUS))):
                            last = nc.scalar.activation(
                                probs[:, i % 2, a:z], probs[:, i % 2, a:z], ACT.Exp, bias=nmx[:, i % 2, t:t + 1],
                                scale=HD ** -0.5, accum_out=den[:, i % 4, t:t + 1])
                        act.drain()
                        act.sem_inc(exp_ready, 1)
                    if 1 <= i <= heads:
                        copy_probs(h0 + i - 1, i - 1)
                    if i >= 6 and i % 4 == 2 and i < heads:
                        n = (i - 6) // 4
                        split(JOBS[name] + n, SPLITS[name] + n, XA, g0 + n, x_tmp)

            attention(0, 0, DSA_HEADS, "attn", 0)

            def attn_out(b, B, A):
                act.wait_ge(tp_ready, b + JOBS["norm2"])
                evac(stage[:], A, B * CPB + CPB)

            norm2_split = splits("norm2", XB)

            def attn_job(b):
                act.wait_ge(staged, b + (STAGED["norm2"] + 1))
                squares(b * (2 * NT) + SQ["norm2"], b, T1[:, 0, 0:NBLK], quarter(T0, b), stage)
                norm2_split(b)

            phase("attn_out", attn_out, attn_job,
                  first={6: lambda: split(JOBS["attn"] + 3, SPLITS["attn"] + 3, XA, 3, x_tmp)})

            def last_attn_squares():
                act.wait_ge(staged, STAGED["norm2"] + 4)
                squares(3 * (2 * NT) + SQ["norm2"], 3, T1[:, 0, 0:NBLK], quarter(T0, 3), stage)

            def conv_silu(b):
                act.wait_ge(conv_in, b + 1)
                nc.scalar.activation(feat(0)[:, bass.ds(b * 4, 4), :], tmp[:], ACT.Silu).then_inc(conv_done, 1)

            phase("m_qk", to_stage("m_qk", scale=r_mix), conv_silu, at=9,
                  first={3: last_attn_squares, 4: lambda: root(2, NT), 5: lambda: root(3, NT),
                         6: lambda: norm2_split(3), 10: lambda: act.wait_ge(xn_ready, 3)})

            narrow("m_if", 8, JOBS["m_qk"] + 4, {9: lambda: conv_silu(3)})

            def forget_exp():
                act.wait_ge(g_in, 1)
                nc.scalar.activation(gate_u, gate_u, ACT.Exp).then_inc(g_act, 1)

            def forget_log():
                act.wait_ge(g_in, 2)
                nc.scalar.activation(gate_f, gate_w, ACT.Ln).then_inc(g_act, 1)

            def decays():
                act.wait_ge(g_dve, 1)
                for h in range(M_HEADS):
                    for t, (a, z) in enumerate(((0, P), (P, CAUS))):
                        nc.scalar.activation(m_dec[:, h, a:z], m_dec[:, h, a:z], ACT.Exp, bias=m_nmax[:, t, h:h + 1])
                nc.scalar.activation(m_floor, m_floor, ACT.Exp, scale=-1.0).then_inc(g_act, 1)

            B0, A0, n = PHASES["m_v"]
            act.wait_ge(res_done, 1)
            for b, hooks in enumerate(({3: forget_exp, 4: forget_log}, {9: decays})):
                blk(B0 + b, hooks)
                evac(m_v[:, :, b * NBLK:(b + 1) * NBLK], A0 + b, (B0 + b) * CPB + CPB, scale=r_mix)
            phase("m_o", lambda b, B, A: evac(m_o[:, :, bass.ds(b * NBLK, NBLK)], A, B * CPB + CPB, ACT.Sigmoid, r_mix))
            for i in range(M_HEADS + 2):
                if 1 <= i <= M_HEADS:
                    copy_probs(DSA_HEADS + i - 1, i - 1)
                if i >= 2:
                    act.wait_ge(o_done, DSA_HEADS + i - 1)
                    for t in range(NT):
                        square(SQ["mlstm"] + (i - 2) * NT + t, m_num[:, i - 2, t, :],
                               ms[:, t * M_HEADS + i - 2:t * M_HEADS + i - 1], T[:, 3, (i - 2) * S:(i - 1) * S])
            root(4, NT * M_HEADS)

            def mlstm_split(n):
                return lambda: split(JOBS["mlstm"] + n, SPLITS["mlstm"] + n, XA, n, x_tmp)

            phase("a_qk", to_stage("a_qk", scale=r_mix), first={4: mlstm_split(0), 6: mlstm_split(1)})
            phase("a_v", lambda b, B, A: evac(a_v[:, :, bass.ds(b * NBLK, NBLK)], A, B * CPB + CPB, scale=r_mix))
            attention(DSA_HEADS + M_HEADS, DSA_HEADS, MOBA_HEADS, "moba", 2)
            n = JOBS["moba"] + 1
            phase("g_m", lambda b, B, A: evac(T0[:, :, bass.ds(b * NBLK, NBLK)], A, B * CPB + CPB, ACT.Sigmoid, r_mix),
                  first={6: lambda: split(n, SPLITS["moba"] + 1, XA, 3, x_tmp)})
            phase("g_a", lambda b, B, A: evac(T1[:, :, bass.ds(b * NBLK, NBLK)], A, B * CPB + CPB, ACT.Sigmoid, r_mix))

            B0, A0, n = PHASES["branch"]

            def branch(b, first=False):
                B, A = b + B0, b * 2 + A0
                for o in range(AHEAD, CPB + AHEAD):
                    hi(B, o)
                    if o == 6:
                        if not first:
                            split(b + (JOBS["branch"] - 1), b + (SPLITS["branch"] - 1), XB, b - 1, tmp[:])
                        act.wait_ge(tp_ready, b + JOBS["branch"])
                        evac(stage[:], A, B * CPB + 4)
                act.wait_ge(x_ready, b + SPLITS["branch"])
                evac(tmp_t, A + 1, B * CPB + 8)

            branch(0, first=True)
            with act.Fori(1, n) as b:
                branch(b)

            load_table(2, ACT.Sqrt)

            def mix_out(b, B, A):
                evac(T2[:, :, bass.ds(b * NBLK, NBLK)], A, B * CPB + CPB)
                act.wait_ge(acc_free, A + 1)
                squares(b * NT + SQ["mix_out"], b, junk_a, quarter(T2, b))

            phase("mix_out", mix_out,
                  first={6: lambda: split(JOBS["branch"] + 3, SPLITS["branch"] + 3, XB, 3, tmp[:])})
            root(5, NT)
            for i in range(2 * NT):
                act.wait_ge(sum_ready, i + 1)
                t, c0 = i % 2, i // 2 * (D // 2)
                square(SQ["norm3"] + i, T3[:, t, c0:c0 + D // 2], ms_part[:, 1, t, i // 2:i // 2 + 1],
                       xa_lo[:, 0:4, :].rearrange("p f t -> p (f t)"))

            J, X0, C0 = JOBS["ffn"], SPLITS["ffn"], COMBINED["ffn"]

            def up(e, half, B, A, after=None):
                for h in range(2):
                    def mid():
                        split(e * 2 + (J + h - 1), e * 2 + (X0 + h - 1), XB, (2 * half + h - 1) % 4, tmp[:])
                    blk(B + h, {6: mid} if h == 1 or after == "up" else
                        {**feed("norm3", XA), 7: lambda: root(6, NT)} if after == "norm" else None)
                    act.wait_ge(tp_ready, e * 2 + (J + h))
                    if after == "norm":
                        act.wait_ge(x_ready, X0)
                        act.wait_ge(xn_ready, 4)
                    elif after is None:
                        act.wait_ge(combined, e * 4 + (C0 - 4))
                    evac(stage[:], A + h, (B + h) * CPB + CPB, ACT.Relu, r_ffn)

            def last_squares(q):
                act.wait_ge(combined, C0 + 4 * (N_FFN - 1) + q + 1)
                squares(SQ["ffn"] + NT * q, q, junk_a, quarter(T1, q))

            def dn(e, half, B, A, last=False):
                def take(q):
                    act.wait_ge(tp_ready, (J + 2 * N_FFN) if last else e * 2 + (J + 4))
                    act.wait_ge(combined, e * 4 + (C0 + q))
                    evac(stage[:], A + q, B * CPB + 4 * (q + 1))
                    if last and q:
                        last_squares(q - 1)

                def mid():
                    if not last:
                        split(e * 2 + (J + 3), e * 2 + (X0 + 3), XB, 2 * (1 - half) + 1, tmp[:])
                    take(0)

                blk(B, {6: mid, 10: lambda: take(1)})
                blk(B + 1, {6: lambda: take(2), 10: lambda: take(3)}, last=last)
                if last:
                    take(3)

            up(0, 0, FB, FA, after="norm")
            up(1, 1, FB + 2, FA + 2, after="up")
            dn(0, 0, FB + 4, FA + 4)
            with act.Fori(0, 3) as i:
                up(i * 2 + 2, 0, i * 8 + (FB + 6), i * 12 + (FA + 8))
                dn(i * 2 + 1, 1, i * 8 + (FB + 8), i * 12 + (FA + 10))
                up(i * 2 + 3, 1, i * 8 + (FB + 10), i * 12 + (FA + 14))
                dn(i * 2 + 2, 0, i * 8 + (FB + 12), i * 12 + (FA + 16))
            load_table(3, ACT.Sqrt)
            dn(7, 1, FB + 30, FA + 44, last=True)
            last_squares(3)
            root(7, NT)

        @block.vector
        def _(dve):
            step = Chain(dve, dve_step)
            tt, ts, stt = nc.vector.tensor_tensor, nc.vector.tensor_scalar, nc.vector.scalar_tensor_tensor

            def lo(B, o, cols=NBLK):
                dve.wait_ge(hi_ready, (B + o // CPB) * CPB + (o % CPB + 1))
                part = slice(0, cols)
                tt(w_lo[:, o % SPL, :, part], raw[:, o % RAW, :, part], w_hi[:, o % SPL, :, part].bitcast(F32),
                   ALU.subtract).then_inc(lo_ready, 1)

            def blk(B, hooks=None, last=False, cols=NBLK, ride=None, b=None, ride_to=CPB + AHEAD):
                if hooks and AHEAD - 1 in hooks:
                    hooks[AHEAD - 1]()
                for o in range(AHEAD, CPB if last else CPB + AHEAD):
                    lo(B, o, cols if o < CPB else NBLK)
                    if ride and o < ride_to:
                        rider(ride, b, o)
                    if hooks and o in hooks:
                        hooks[o]()

            def phase(name, each=None, out=None, low=None, per=0, first=None):
                B0, A0, n = PHASES[name]
                u = RIDERS.get(name)
                if u and name != "pool_v":
                    for o in range(AHEAD):
                        rider(u, 0, o)
                blk(B0, first, ride=u, b=0)
                if each:
                    each(0, A0)
                if n > 1:
                    def hooks(b):
                        return {5: lambda: out(b - 1), 6: lambda: low(b - 1)} if out else None

                    with step.loop(1, n - 1 if u else n, per) as b:
                        blk(b + B0, hooks(b), ride=u, b=b)
                        if each:
                            each(b, b + A0)
                    if u:
                        blk(n - 1 + B0, hooks(n - 1), ride=u, b=n - 1, ride_to=CPB)
                        if each:
                            each(n - 1, n - 1 + A0)

            def leave(n, dst, scale=None, shift=None, bank=None):
                dve.wait_ge(tp_ready, n + 1)
                p0 = job_bank(n) if bank is None else bank
                src = ps[:, p0:p0 + 2, :].rearrange("p b (f t) -> p (b f) t", t=S)
                if scale is None:
                    nc.vector.tensor_copy(dst, src).then_inc(tp_evac, 1)
                elif shift is None:
                    tt(dst, src, scale.unsqueeze(2).to_broadcast([P, 4, S]), ALU.mult).then_inc(tp_evac, 1)
                else:
                    step(tt(dst, src, scale.unsqueeze(2).to_broadcast([P, 4, S]), ALU.mult))
                    tt(dst, dst, shift.unsqueeze(2).to_broadcast([P, 4, S]), ALU.add).then_inc(tp_evac, 1)

            def low_part(s, X, g, src):
                dve.wait_ge(xh_ready, s + 1)
                tt(X[1][:, bass.ds(g * 4, 4), :], src, X[0][:, bass.ds(g * 4, 4), :].bitcast(F32), ALU.subtract
                   ).then_inc(x_ready, 1)
                dve.wait_ge(x_ready, s + 1)

            def outs(name, X, scale=None):
                def out(b):
                    leave(b + JOBS[name], tmp[:], None if scale is None else scale[:, bass.ds(b * 4, 4)])
                return out, lambda b: low_part(b + SPLITS[name], X, b, tmp[:])

            def newton(i, y, m, n):
                q = small[:, 9, 0:n]
                dve.wait_ge(root_ready, i + 1)
                step(nc.vector.reciprocal(y, rs[:, 0:n]))
                step(tt(q, y, y, ALU.mult))
                step(tt(q, q, m, ALU.mult))
                step(ts(q, q, -0.5, 1.5, ALU.mult, ALU.add))
                step(tt(y, y, q, ALU.mult))

            def rstd(i, n, width, squares):
                dve.wait_ge(sq_part, squares)
                ts(t8[:, 0:n], ms[:, 0:n], 1.0 / width, EPS, ALU.mult, ALU.add).then_inc(ms_ready, 1)
                newton(i, rs[:, 0:n], t8[:, 0:n], n)

            def sum_parts(dst, k, n=4):
                part = ms_part[:, k]
                if n == 4:
                    step(tt(part[:, :, 0:2], part[:, :, 0:2], part[:, :, 2:4], ALU.add))
                step(tt(dst, part[:, :, 0], part[:, :, 1], ALU.add))

            def to_diag(r):
                for t in range(NT):
                    step(ts(rs_diag[:, t, :], ident, r[:, t:t + 1], None, ALU.mult))
                dve.sem_inc(xn_ready, 1)

            def feed(name, X, scale=None):
                bufs = (tmp[:], stage_f)

                def out(g):
                    if scale is not None:
                        leave(JOBS[name] + g, bufs[g % 2], scale[:, 4 * g:4 * g + 4])

                def low(g):
                    low_part(SPLITS[name] + g, X, g, bufs[g % 2])

                def start():
                    out(0)
                    out(1)
                    low(0)
                    low(1)

                def group(g):
                    out(g)
                    low(g)

                return {2: start, 3: lambda: group(2), 5: lambda: group(3)}

            def rotate(src, heads, half, at):
                v = src.rearrange("p t (h d) -> p t h d", h=heads)
                n = NT * heads * half
                ta, tb = (tmp[:].rearrange("p f t -> p (f t)")[:, k * 512:k * 512 + n]
                          .rearrange("p (t h d) -> p t h d", t=NT, h=heads) for k in range(2))
                x1, x2 = v[:, :, :, 0:half], v[:, :, :, half:2 * half]
                cosb, sinb = (rot[:, k, :, at:at + half].unsqueeze(2).to_broadcast([P, NT, heads, half])
                              for k in range(2))
                step(tt(ta, x1, cosb, ALU.mult))
                step(tt(tb, x2, sinb, ALU.mult))
                step(tt(ta, ta, tb, ALU.subtract))
                step(tt(tb, x1, sinb, ALU.mult))
                step(tt(x2, x2, cosb, ALU.mult))
                step(tt(x2, x2, tb, ALU.add))
                step(nc.vector.tensor_copy(x1, ta))

            dve.wait_ge(in_landed, 16 * 5)
            step(nc.vector.tensor_copy(posf[:], posi[:]))
            cos, sin = rot[:, 0], rot[:, 1]
            ang, turns = (tmp[:].rearrange("p f t -> p (f t)")[:, k * 512:k * 512 + NT * 88]
                          .rearrange("p (t f) -> p t f", t=NT) for k in range(2))
            for t in range(NT):
                step(ts(ang[:, t, 0:24], freqs[:, 0:24], posf[:, 0, t:t + 1], None, ALU.mult))
                step(ts(ang[:, t, 24:88], freqs[:, 24:88], posf[:, 1, t:t + 1], None, ALU.mult))
            for dst, turn in ((cos, 0.25), (sin, 0.0)):
                step(ts(turns, ang, 1.0 / (2 * np.pi), turn, ALU.mult, ALU.add))
                step(ts(turns, turns, MAGIC, None, ALU.add))
                step(ts(turns, turns, MAGIC, None, ALU.subtract))
                step(stt(dst, turns, -TWO_PI[0], ang, ALU.mult, ALU.add))
                for part in TWO_PI[1:]:
                    step(stt(dst, turns, -part, dst, ALU.mult, ALU.add))
                step(ts(dst, dst, 2 * np.pi * turn, PI_CLAMP, ALU.add, ALU.min))
                step(ts(dst, dst, -PI_CLAMP, None, ALU.max))
            dve.sem_inc(sin_in, 1)

            dve.wait_ge(vec_tp, 1)
            step(nc.vector.tensor_copy(vec1[:, 0:120], ps[:, 4, 0:120]))
            step(nc.vector.tensor_copy(vec2[:, 0:64], ps[:, 5, 0:64]))
            dve.sem_inc(vec_done, 1)

            dve.wait_ge(csil_ready, 1)
            for u in range(2):
                dve.wait_ge(bias_landed, 16 * u + 16)
                for k in range(KC):
                    dve.wait_ge(mod_landed[k % 4], 16 * (4 * u + k // 4 + 1))
                    stt(mod_acc[u], mod_raw[:, k % 4, :], csil[:, k:k + 1], mod_acc[u], ALU.mult, ALU.add
                        ).then_inc(mod_used, 1)
                    dve.wait_ge(mod_used, u * KC + k + 1)
                if u == 0:
                    rstd(0, NT, D, NT)
                    to_diag(rs)

            def rider(u, b, o):
                if o == 0 and isinstance(b, int):
                    dve.wait_ge(bias_landed, 16 * u + 16)
                c0 = b * CPB + (o % CPB + o // CPB * CPB)
                at = o % 2 * 1024
                lap = b * 2 + (2 * KC // 16 * 4 * (u - 2) + o // 4 + 1)
                dve.wait_ge(ride_landed[o % 4], lap * 16)
                acc = mod_acc[u][:, at:at + 1024]
                stt(acc, ride_raw[:, o % 4, :], csil[:, bass.ds(b * 4 + o // 2, 1)], acc, ALU.mult, ALU.add
                    ).then_inc(mod_used, 1)
                dve.wait_ge(mod_used, c0 + (RIDE[u] + 1))

            def shift_scale(i, sums, shift_bank, scale_bank, part=slice(0, KC)):
                dve.wait_ge(mod_sum, sums)
                shift, scale = ps[:, shift_bank, 0:KC], ps[:, scale_bank, KC:2 * KC]
                step(nc.vector.tensor_copy(vec3[:, 16 * i:16 * i + 16][:, part], shift[:, part]))
                step(stt(scl[:, i, part], scale[:, part], 1.0, (G0, G1)[i][:, part], ALU.add, ALU.mult))
                dve.sem_inc(scl_ready, 1)

            shift_scale(0, 2, 0, 1, slice(0, 4))
            lo(0, 0)
            shift_scale(0, 3, 0, 2, slice(4, KC))

            hooks = feed("norm0", XA)
            first_low = hooks[2]

            def first_riders():
                first_low()
                lo(0, 1)
                lo(0, 2)
                for o in range(AHEAD):
                    rider(2, 0, o)

            out, low = outs("pool_v", XB)
            phase("pool_v", None, out, low, first={**hooks, 2: first_riders})
            phase("pool_gate", first={5: lambda: out(3), 6: lambda: low(3)})
            B0, A0, _ = PHASES["group"]
            gout, glow = outs("group", XA, PSC)
            for o in range(AHEAD, CPB + AHEAD):
                lo(B0, o)
                if o in (4, 6, 8, 10):
                    g = (o - 4) // 2
                    dve.wait_ge(acc_free, A0 + g + 1)
                    tt(stage[:], stage[:], T1[:, :, NBLK * g:NBLK * g + NBLK], ALU.mult).then_inc(staged, 1)
                if o in (7, 9):
                    gout((o - 7) // 2)
                if o in (8, 10):
                    glow((o - 8) // 2)

            def group_rest():
                gout(2)
                glow(2)

            def add_residual(k, dst):
                def each(b, A):
                    dve.wait_ge(acc_free, A + 1)
                    if k == 1:
                        dve.wait_ge(sum_taken, 1)
                    else:
                        dve.wait_ge(wide_landed, 32)
                    dve.wait_ge(res_landed, 16 * k)
                    cols = bass.ds(b * NBLK, NBLK)
                    step(tt(stage[:], stage[:], wide[:, cols].unsqueeze(1).to_broadcast([P, NT, NBLK]), ALU.mult))
                    ins = tt(dst[:, :, cols], dst[:, :, cols], stage[:], ALU.add)
                    if k == 1:
                        ins.then_inc(combined, 1)
                    else:
                        step(ins)
                        tt(stage[:], T0[:, :, cols], final_w[:, cols].unsqueeze(1).to_broadcast([P, NT, NBLK]),
                           ALU.mult).then_inc(staged, 1)
                return each

            phase("pool_out", add_residual(1, T2), per=1,
                  first={2: group_rest, 5: lambda: gout(3), 6: lambda: glow(3)})

            dve.wait_ge(sq_part, SQ["norm1"] + 8)
            sum_parts(ms[:, 0:NT], 0)
            rstd(1, NT, D, SQ["norm1"] + 8)
            to_diag(rs)
            shift_scale(1, 6, 6, 6)

            def index_q(b, A):
                dve.wait_ge(acc_free, A + 1)
                rotate(stage[:], 8, FRQI, FRQ1)
                dve.sem_inc(staged, 1)

            def qi_out(b):
                leave(b + JOBS["idx_q"], qi_t[:, bass.ds(b * 4, 4), :])

            dve.wait_ge(rot_ready, 1)
            phase("idx_q", index_q, qi_out, lambda b: None, per=7, first=feed("norm1", XB))
            blk(PHASES["idx_kw"][0], {5: lambda: qi_out(1)}, cols=80)

            def kw_out():
                n = JOBS["idx_kw"]
                dve.wait_ge(tp_ready, n + 1)
                src = ps[:, 4, 0:2 * P].rearrange("p (t n) -> p t n", t=NT)
                step(nc.vector.tensor_copy(stage[:, :, 0:80], src[:, :, 0:80]))
                dve.sem_inc(tp_evac, 1)
                rotate(stage[:, :, 0:64], 1, FRQI, FRQ1)
                step(ts(idx_w[:], stage[:, :, 64:80], IDX_HEADS ** -0.5 * 64 ** -0.5, None, ALU.mult))
                nc.vector.tensor_copy(stage[:, :, 64:128], stage[:, :, 0:64]).then_inc(staged, 1)
                step(nc.vector.tensor_copy(score, tri))

            def ki_out():
                n = JOBS["idx_kw"] + 1
                dve.wait_ge(tp_ready, n + 1)
                nc.vector.tensor_copy(ki_t, ps[:, 6, 0:S]).then_inc(tp_evac, 1)

            def start_scores():
                kw_out()
                qi_out_now(0)

            def qi_out_now(b):
                if not isinstance(b, int):
                    dve.wait_ge(sc_ready, b * 2)
                nc.vector.tensor_copy(qi_now, qi_t[:, bass.ds(b, 1), :].rearrange("p a t -> p (a t)")
                                      ).then_inc(qi_ready, 1)

            def index_scores(b):
                for i in range(2):
                    dve.wait_ge(relu_ready, b * 2 + (i + 1))
                    for t, (a, z) in enumerate(((0, P), (P, CAUS))):
                        step(stt(score[:, a:z], probs[:, i, a:z], idx_w[:, t, bass.ds(b * 2 + i, 1)], score[:, a:z],
                                 ALU.mult, ALU.add))

            def carry():
                nc.vector.tensor_copy(small[:, 10, 0:1], posf[:, 0, 0:1])

            def query_key(b, A):
                dve.wait_ge(acc_free, A + 1)
                rotate(stage[:], 4, FRQ1, 0)
                dve.sem_inc(staged, 1)

            def qk_out(b):
                leave(b + JOBS["qk"], qk_t[:, bass.ds(b * 4, 4), :])

            B0, A0, n = PHASES["qk"]
            blk(B0, {3: start_scores, 6: ki_out, 9: lambda: index_scores(0)})
            query_key(0, A0)
            with step.loop(1, n, 11) as b:
                blk(b + B0, {3: lambda: qi_out_now(b), 5: lambda: qk_out(b - 1), 9: lambda: index_scores(b)})
                query_key(b, b + A0)

            def top_k(b, A):
                for t, (a, z) in enumerate(((0, P), (P, CAUS))):
                    carry()
                    step(nc.vector.max(best[:, t, :], score[:, a:z]))
                    carry()
                    step(nc.vector.match_replace(score[:, a:z], best[:, t, :], score[:, a:z], TAKEN))

            phase("v", top_k, per=4, first={5: lambda: qk_out(7)})
            phase("gate", top_k, per=4)
            step(ts(score, score, 0.5 * (TAKEN + FAR), UNPICKED, ALU.is_gt, ALU.mult))
            step(tt(pick[:], score, tri, ALU.add))
            dve.sem_inc(picked, 1)

            def attention(h0, e0, heads, name, g0, mask, gate):
                for i in range(heads + 2):
                    if i < heads:
                        h, b = h0 + i, i % 2
                        dve.wait_ge(lg_ready, h + 1)
                        if i >= 2:
                            dve.wait_ge(pt_ready, h - 1)
                        for t, (a, z) in enumerate(((0, P), (P, CAUS))):
                            step(nc.vector.tensor_tensor_reduce(
                                out=probs[:, b, a:z], in0=ps[:, 4 + b, a:z], in1=mask[:, a:z], scale=1.0,
                                scalar=FAR, op0=ALU.add, op1=ALU.max, accum_out=mx[:, b, t:t + 1]))
                        ts(nmx[:, b, :], mx[:, b, :], -(HD ** -0.5), None, ALU.mult).then_inc(masked, 1)
                    if i >= 6 and i % 4 == 2 and i < heads:
                        n = (i - 6) // 4
                        leave(JOBS[name] + n, x_tmp, bank=2)
                    if i >= 6 and i % 4 == 3 and i < heads:
                        low_part(SPLITS[name] + (i - 7) // 4, XA, g0 + (i - 7) // 4, x_tmp)
                    if 2 <= i < heads + 2:
                        j = i - 2
                        b = j % 2
                        dve.wait_ge(exp_ready, e0 + j + 1)
                        if name == "attn" and j == 0:
                            dve.wait_ge(acc_free, PHASES["gate"][1] + 4)
                        step(nc.vector.reciprocal(rden[:, b, :], den[:, j % 4, :]))
                        dve.wait_ge(pv_ready, h0 + j + 1)
                        for t in range(NT):
                            dst, src = stage[:, t, j % 4 * HD:j % 4 * HD + HD], ps[:, b, t * HD:t * HD + HD]
                            if gate is None:
                                step(ts(dst, src, rden[:, b, t:t + 1], None, ALU.mult))
                            else:
                                step(stt(dst, src, rden[:, b, t:t + 1], gate[:, t, j * HD:j * HD + HD],
                                         ALU.mult, ALU.mult))
                        dve.sem_inc(o_done, 1)
                        if j % 4 == 3:
                            dve.sem_inc(staged, 1)

            def rest(name, n, g, bank):
                return {5: lambda: leave(JOBS[name] + n, x_tmp, bank=bank),
                        6: lambda: low_part(SPLITS[name] + n, XA, g, x_tmp)}

            dve.wait_ge(row_stored, 16)
            attention(0, 0, DSA_HEADS, "attn", 0, pick[:], T3)
            norm_out, norm_low = outs("norm2", XB, MIXP)
            phase("attn_out", add_residual(2, T0), norm_out, norm_low, per=2, first=rest("attn", 3, 3, 4))

            def output_rstd():
                dve.wait_ge(sq_part, SQ["norm2"] + 16)
                sum_parts(ms[:, 0:NT], 0)
                sum_parts(ms[:, 2:4], 1)
                rstd(2, NT, D, SQ["norm2"] + 16)
                m2 = t8[:, 0:2]
                step(nc.vector.tensor_copy(r_out, rs[:, 0:NT]))
                step(tt(m2, r_out, r_out, ALU.mult))
                step(tt(m2, m2, ms[:, 2:4], ALU.mult))
                ts(m2, m2, 1.0 / D, EPS, ALU.mult, ALU.add).then_inc(ms_ready, 1)

            def mix_rstd():
                newton(3, r_mix, t8[:, 0:2], NT)
                step(tt(r_mix, r_mix, r_out, ALU.mult))
                dve.sem_inc(xn_ready, 1)
                norm_out(3)

            def first_output(t):
                step(stt(T2[:, t, :], T0[:, t, :], r_out[:, t:t + 1], final_w, ALU.mult, ALU.mult))
                if t:
                    dve.sem_inc(res_done, 1)

            def conv(b, f):
                if f == 0:
                    dve.wait_ge(tp_ready, b + (JOBS["m_qk"] + 1))
                p0 = job_bank(b + JOBS["m_qk"])
                u = ps[:, p0 + f // 2, f % 2 * S:f % 2 * S + S]
                col = b * 4 + f
                w = [vec2[:, bass.ds(col + 16 * k, 1)] for k in range(4)]
                step(ts(tmp[:, f, :], u, w[3], CVB[:, bass.ds(col, 1)], ALU.mult, ALU.add))
                for k in range(3):
                    lag = 3 - k
                    step(stt(tmp[:, f, lag:S], u[:, 0:S - lag], w[k], tmp[:, f, lag:S], ALU.mult, ALU.add))
                if f == 3:
                    dve.sem_inc(tp_evac, 1)
                    dve.sem_inc(conv_in, 1)

            B0, A0, n = PHASES["m_qk"]
            blk(B0, {4: output_rstd, 5: mix_rstd, 6: lambda: norm_low(3), 7: lambda: first_output(0),
                     8: lambda: first_output(1)})
            with step.loop(1, n, 16) as b:
                blk(b + B0, {5 + f: (lambda f=f: conv(b - 1, f)) for f in range(4)})
            blk(PHASES["m_if"][0], {5 + f: (lambda f=f: conv(3, f)) for f in range(4)}, cols=8)

            def log_gates():
                dve.wait_ge(tp_ready, JOBS["m_if"] + 1)
                src = ps[:, 6, 0:16].rearrange("p (t n) -> p t n", t=NT)
                for k, dst in ((0, gate_i), (1, gate_f)):
                    step(tt(dst, src[:, :, 4 * k:4 * k + 4], r_mix.unsqueeze(2).to_broadcast([P, NT, 4]), ALU.mult))
                    step(tt(dst, dst, ifb[:, 4 * k:4 * k + 4].unsqueeze(1)
                            .to_broadcast([P, NT, 4]), ALU.add))
                dve.sem_inc(tp_evac, 1)
                step(ts(gate_u, gate_f, -1.0, None, ALU.mult))
                step(tt(gate_u, gate_u, gate_f, ALU.min))
                step(ts(m_e, gate_f, 0.0, None, ALU.min))
                dve.sem_inc(g_in, 1)

            def forget_one():
                dve.wait_ge(g_act, 1)
                step(ts(gate_w, gate_u, 1.0, None, ALU.add))
                dve.sem_inc(g_in, 1)
                step(ts(cum_f, gate_w, -1.0, 1e-30, ALU.add, ALU.max))
                step(nc.vector.reciprocal(cum_f, cum_f))
                step(tt(cum_f, cum_f, gate_u, ALU.mult))

            def forget_log():
                dve.wait_ge(g_act, 2)
                step(tt(gate_f, gate_f, cum_f, ALU.mult))
                step(tt(gate_f, m_e, gate_f, ALU.subtract))
                dve.sem_inc(g_in, 1)

            def diagonals():
                dve.wait_ge(g_mm, 1)
                step(nc.vector.tensor_copy(cum_f, ps[:, 6, 0:8].rearrange("p (t h) -> p t h", t=NT)))
                step(tt(m_e, gate_i, cum_f, ALU.subtract))
                dve.wait_ge(conv_done, 4)
                for t in range(NT):
                    for h in range(M_HEADS):
                        step(ts(m_diag[:, t, h, :], ident, m_e[:, t, h:h + 1], None, ALU.mult))
                dve.sem_inc(g_in, 1)

            def exponents():
                dve.wait_ge(g_mm, 2)
                dve.wait_ge(res_stored, 32)
                for h in range(M_HEADS):
                    for t, (a, z) in enumerate(((0, P), (P, CAUS))):
                        at = h % 2 * S
                        step(nc.vector.tensor_tensor_reduce(
                            out=m_dec[:, h, a:z], in0=ps[:, 4 + h // 2, at:at + z - a], in1=tri[:, a:z], scale=1.0,
                            scalar=0.0, op0=ALU.add, op1=ALU.max, accum_out=m_max[:, t, h:h + 1]))
                step(ts(m_nmax, m_max, -1.0, None, ALU.mult))
                step(tt(m_floor, m_max, cum_f, ALU.add))
                dve.sem_inc(g_dve, 1)

            B0, A0, n = PHASES["m_v"]
            blk(B0, {3: log_gates, 4: forget_one, 5: forget_log, 8: diagonals})
            blk(B0 + 1, {8: exponents})
            phase("m_o")
            dve.wait_ge(g_act, 3)
            for i in range(M_HEADS + 2):
                if i < M_HEADS:
                    dve.wait_ge(lg_ready, DSA_HEADS + i + 1)
                    if i >= 2:
                        dve.wait_ge(pt_ready, DSA_HEADS + i - 1)
                    for t, (a, z) in enumerate(((0, P), (P, CAUS))):
                        step(nc.vector.tensor_tensor_reduce(
                            out=probs[:, i % 2, a:z], in0=ps[:, 4 + i % 2, a:z], in1=m_dec[:, i, a:z], scale=S ** -0.5,
                            scalar=0.0, op0=ALU.mult, op1=ALU.add, accum_out=den[:, i % 2, t:t + 1]))
                    dve.sem_inc(masked, 1)
                if i >= 2:
                    j = i - 2
                    dve.wait_ge(pv_ready, DSA_HEADS + j + 1)
                    for t in range(NT):
                        step(ts(m_num[:, j, t, :], ps[:, j % 2, t * S:t * S + S], rden[:, j % 2, t:t + 1], None,
                                ALU.mult))
                    dve.sem_inc(o_done, 1)
                if i < M_HEADS:
                    step(ts(rden[:, i % 2, :], den[:, i % 2, :], -1.0, None, ALU.mult))
                    step(tt(rden[:, i % 2, :], rden[:, i % 2, :], den[:, i % 2, :], ALU.max))
                    step(tt(rden[:, i % 2, :], rden[:, i % 2, :], m_floor[:, :, i], ALU.max))
                    step(nc.vector.reciprocal(rden[:, i % 2, :], rden[:, i % 2, :]))
            rstd(4, NT * M_HEADS, S, SQ["mlstm"] + 8)

            def mlstm_stage(n):
                if n:
                    dve.wait_ge(tp_ready, JOBS["mlstm"] + n)
                for t in range(NT):
                    for h in range(2):
                        j = 2 * n + h
                        step(stt(stage[:, t, h * S:h * S + S], m_num[:, j, t, :],
                                 rs[:, t * M_HEADS + j:t * M_HEADS + j + 1], m_o[:, t, j * S:j * S + S],
                                 ALU.mult, ALU.mult))
                dve.sem_inc(staged, 1)

            def mlstm_out(n):
                leave(JOBS["mlstm"] + n, x_tmp, MLN[:, 4 * n:4 * n + 4], bank=6)

            def mlstm_low(n):
                low_part(SPLITS["mlstm"] + n, XA, n, x_tmp)

            def mlstm_mid():
                mlstm_out(0)
                mlstm_stage(1)
                mlstm_low(0)

            def mlstm_last():
                mlstm_out(1)
                mlstm_low(1)

            def rotary_full(b, A):
                dve.wait_ge(acc_free, A + 1)
                rotate(stage[:], 4, FRQ2, FRQ1 + FRQI)
                dve.sem_inc(staged, 1)

            def aqk_out(b):
                leave(b + JOBS["a_qk"], feat(2)[:, bass.ds(b * 4, 4), :])

            phase("a_qk", rotary_full, aqk_out, lambda b: None, per=7,
                  first={2: lambda: mlstm_stage(0), 4: mlstm_mid, 6: mlstm_last})
            phase("a_v", first={5: lambda: aqk_out(3)})
            attention(DSA_HEADS + M_HEADS, DSA_HEADS, MOBA_HEADS, "moba", 2, tri, None)
            phase("g_m", first=rest("moba", 1, 3, 4))
            phase("g_a")

            B0, A0, n = PHASES["branch"]
            out, low = outs("branch", XB)

            def branch(b, first=False):
                B, A = b + B0, b * 2 + A0
                cols = bass.ds(b * NBLK, NBLK)
                for o in range(AHEAD, CPB + AHEAD):
                    lo(B, o)
                    if o == 5 and not first:
                        out(b - 1)
                    if o == 6:
                        if not first:
                            low(b - 1)
                        dve.wait_ge(acc_free, A + 1)
                        step(tt(stage[:], stage[:], T0[:, :, cols], ALU.mult))
                dve.wait_ge(acc_free, A + 2)
                step(tt(tmp_t, tmp_t, T1[:, :, cols], ALU.mult))
                tt(stage[:], stage[:], tmp_t, ALU.add).then_inc(staged, 1)

            branch(0, first=True)
            with step.loop(1, n, 2) as b:
                branch(b)

            def mix_scaled(b, A):
                dve.wait_ge(acc_free, A + 1)
                dve.wait_ge(wide_landed, 48)
                cols = bass.ds(b * NBLK, NBLK)
                step(tt(T1[:, :, cols], T2[:, :, cols], wide[:, cols].unsqueeze(1).to_broadcast([P, NT, NBLK]),
                        ALU.mult))

            phase("mix_out", mix_scaled, per=1, first={5: lambda: out(3), 6: lambda: low(3)})
            dve.sem_inc(res_done, 1)
            dve.wait_ge(sq_part, SQ["mix_out"] + 8)
            sum_parts(ms[:, 0:NT], 0)
            rstd(5, NT, D, SQ["mix_out"] + 8)
            dve.wait_ge(res_landed, 48)

            def add_scaled(src, done):
                for i in range(2 * NT):
                    t, c0 = i % 2, i // 2 * (D // 2)
                    dst = T3[:, t, c0:c0 + D // 2]
                    stt(dst, src[:, t, c0:c0 + D // 2], rs[:, t:t + 1], dst, ALU.mult, ALU.add).then_inc(done, 1)

            add_scaled(T1, sum_ready)

            def ffn_rstd():
                dve.wait_ge(sq_part, SQ["norm3"] + 4)
                sum_parts(ms[:, 0:NT], 1, 2)
                rstd(6, NT, D, SQ["norm3"] + 4)
                step(nc.vector.tensor_copy(r_ffn, rs[:, 0:NT]))
                dve.sem_inc(xn_ready, 1)

            J, X0, C0, S0 = JOBS["ffn"], SPLITS["ffn"], COMBINED["ffn"], STAGED["ffn"]

            def up(e, half, B, A, after=None):
                for h in range(2):
                    hooks = None
                    if h == 1 or after == "up":
                        j, g = e * 2 + (h - 1), (2 * half + h - 1) % 4
                        hooks = {5: lambda: leave(j + J, tmp[:]), 6: lambda: low_part(j + X0, XB, g, tmp[:])}
                    elif after == "norm":
                        hooks = {**feed("norm3", XA, FFNP), 7: ffn_rstd, 8: lambda: step(nc.vector.memset(T1[:], 0.0))}
                    blk(B + h, hooks)
                    dve.wait_ge(acc_free, A + (h + 1))
                    tt(stage[:], stage[:], stage[:], ALU.mult).then_inc(staged, 1)

            def dn(e, half, B, A, last=False):
                def add(q):
                    dve.wait_ge(acc_free, A + (q + 1))
                    cols = slice(q * NBLK, q * NBLK + NBLK)
                    y = T1[:, :, cols]
                    tt(y, y, stage[:], ALU.add).then_inc(combined, 1)
                    if last:
                        dve.wait_ge(combined, C0 + 4 * (N_FFN - 1) + q + 1)
                        dve.wait_ge(wide_landed, 64)
                        step(tt(T2[:, :, cols], y, wide[:, cols].unsqueeze(1).to_broadcast([P, NT, NBLK]), ALU.mult))

                def mid():
                    if not last:
                        low_part(e * 2 + (X0 + 3), XB, 2 * (1 - half) + 1, tmp[:])
                    add(0)

                blk(B, {5: (lambda: None) if last else (lambda: leave(e * 2 + (J + 3), tmp[:])),
                        6: mid, 10: lambda: add(1)})
                blk(B + 1, {6: lambda: add(2), 10: lambda: add(3)}, last=last)
                if last:
                    add(3)

            up(0, 0, FB, FA, after="norm")
            up(1, 1, FB + 2, FA + 2, after="up")
            dn(0, 0, FB + 4, FA + 4)
            with step.loop(0, 3, 0) as i:
                up(i * 2 + 2, 0, i * 8 + (FB + 6), i * 12 + (FA + 8))
                dn(i * 2 + 1, 1, i * 8 + (FB + 8), i * 12 + (FA + 10))
                up(i * 2 + 3, 1, i * 8 + (FB + 10), i * 12 + (FA + 14))
                dn(i * 2 + 2, 0, i * 8 + (FB + 12), i * 12 + (FA + 16))
            dn(7, 1, FB + 30, FA + 44, last=True)

            dve.wait_ge(sq_part, SQ["ffn"] + 8)
            sum_parts(ms[:, 0:NT], 0)
            rstd(7, NT, D, SQ["ffn"] + 8)
            add_scaled(T2, out_done)

        @block.tensor
        def _(pe):
            mm = nc.tensor.matmul

            def chunk(B, j, X, k0, A, first, last):
                pe.wait_ge(lo_ready, B * CPB + (j + 1))
                bank = (A % 2) * 2
                for k in range(KPC):
                    for t in range(NT):
                        x_hi, x_lo = (v[:, k0 + k, t * P:(t + 1) * P] for v in X)
                        h, l = (w[:, j % SPL, k, :] for w in (w_hi, w_lo))
                        dst = ps[:, bank + t, :]
                        mm(dst, x_hi, h, start=first and k == 0, stop=False)
                        mm(dst, x_hi, l, start=False, stop=False)
                        ins = mm(dst, x_lo, h, start=False, stop=last and k == KPC - 1)
                ins.then_inc(w_used, 1)

            def narrow(name, X, cols, hooks):
                B, A, _ = PHASES[name]
                pe.wait_ge(acc_free, A - 1)
                dst = ps[0:cols, A % 2 * 2, 0:S]
                for j in range(CPB):
                    pe.wait_ge(lo_ready, B * CPB + (j + 1))
                    for k in range(KPC):
                        x_hi, x_lo = (v[:, KPC * j + k, :] for v in X)
                        h, l = (w[:, j % SPL, k, 0:cols] for w in (w_hi, w_lo))
                        mm(dst, h, x_hi, start=j == 0 and k == 0, stop=False)
                        mm(dst, l, x_hi, start=False, stop=False)
                        ins = mm(dst, h, x_lo, start=False, stop=j == CPB - 1 and k == KPC - 1)
                    ins.then_inc(w_used, 1)
                    if j in hooks:
                        hooks[j]()

            def turn_back(name, cols, dst, width):
                pe.wait_ge(acc_free, PHASES[name][1] + 1)
                pe.wait_ge(tp_evac, JOBS[name])
                for t in range(NT):
                    ins = nc.tensor.transpose(dst[:, t * width:t * width + cols], stage[0:cols, 0, t * P:(t + 1) * P],
                                              ident[0:cols, 0:cols])
                ins.then_inc(tp_ready, 1)

            def blk(B, A, X, free, hooks=None, ready=None):
                if hooks and -1 in hooks:
                    hooks[-1]()
                if free:
                    pe.wait_ge(acc_free, A - 1)
                for j in range(CPB):
                    if ready is not None and j % 2 == 0:
                        pe.wait_ge(x_ready, ready + j // 2 + 1)
                    chunk(B, j, X, KPC * j, A, j == 0, j == CPB - 1)
                    if hooks and j in hooks:
                        hooks[j]()

            def phase(name, X, job=None, first=None, ready=None):
                B0, A0, n = PHASES[name]
                blk(B0, A0, X, A0 >= 2, first, ready)
                if n > 1:
                    if A0 < 2:
                        blk(1 + B0, 1 + A0, X, False, {3: lambda: job(0)} if job else None)
                    with pe.Fori(2 if A0 < 2 else 1, n) as b:
                        blk(b + B0, b + A0, X, True, {3: lambda: job(b - 1)} if job else None)

            def job(n, src, ready, value, bank=None):
                pe.wait_ge(ready, value)
                if bank is not None or not isinstance(n, int):
                    pe.wait_ge(tp_evac, n)
                elif n >= 2:
                    pe.wait_ge(tp_evac, n - 1)
                p0 = job_bank(n) if bank is None else bank
                for f in range(4):
                    for t in range(NT):
                        at = f % 2 * S + t * P
                        dst, part = ps[:, p0 + f // 2, at:at + P], src[:, t, f * P:(f + 1) * P]
                        if ready is xn_ready:
                            ins = mm(dst, part, rs_diag[:, t, :], start=True, stop=True)
                        else:
                            ins = nc.tensor.transpose(dst, part, ident)
                ins.then_inc(tp_ready, 1)

            def stage_job(name):
                return lambda b: job(b + JOBS[name], stage, staged, b + (STAGED[name] + 1))

            def norm_job(name, i, src, g):
                src = src[:, :, g * NBLK:(g + 1) * NBLK]
                if name == "norm3":
                    job(JOBS[name] + g, src, sum_ready, g // 2 * 2 + 2)
                else:
                    job(JOBS[name] + g, src, xn_ready, i + 1)

            def feed(name, i, src):
                def start():
                    norm_job(name, i, src, 0)
                    norm_job(name, i, src, 1)

                return {-1: start, 1: lambda: norm_job(name, i, src, 2), 3: lambda: norm_job(name, i, src, 3)}

            pe.wait_ge(vec_landed, 16 * 12)
            pe.wait_ge(in_landed, 16 * 5)
            nc.tensor.transpose(ps[:, 4, 0:120], stage[0:120, 0, 0:P], ident[0:120, 0:120])
            nc.tensor.transpose(ps[:, 5, 0:64], stage[0:64, 1, 0:P], ident[0:64, 0:64]).then_inc(vec_tp, 1)

            def total(u, banks, col):
                pe.wait_ge(mod_used, RIDE[u] + 2 * KC if u >= 2 else KC * (u + 1))
                for f in range(KC):
                    ins = mm(ps[:, banks[f >= 4], col + f:col + f + 1], mod_acc[u][:, f * P:(f + 1) * P], ones[:, 0:1],
                             start=True, stop=True)
                    if u == 1 and f == 3:
                        ins.then_inc(mod_sum, 1)
                ins.then_inc(mod_sum, 1)

            def total_gate(u, rows):
                pe.wait_ge(mod_used, RIDE[u] + 2 * KC)
                for q in range(4):
                    ins = mm(ps[0:rows, 4 + q, :], ones[:, 0:rows], mod_acc[u][:, q * NBLK:(q + 1) * NBLK],
                             start=True, stop=True)
                ins.then_inc(mod_sum, 1)

            total(0, (0, 0), 0)
            hooks = feed("norm0", 0, T0)
            pe.wait_ge(vec_done, 1)
            hooks.pop(-1)()
            total(1, (1, 2), KC)

            def pool(b):
                n = b + JOBS["pool_v"]
                pe.wait_ge(acc_free, b + (PHASES["pool_v"][1] + 1))
                pe.wait_ge(tp_evac, n)
                p0 = job_bank(n)
                for f in range(4):
                    for u in range(NT):
                        ins = mm(ps[:, p0 + f // 2, f % 2 * S:f % 2 * S + S],
                                 stage[:, u, f * P:(f + 1) * P], amat[:, bass.ds(b, 1), u, :].rearrange("p a t -> p (a t)"),
                                 start=u == 0, stop=u == NT - 1)
                ins.then_inc(tp_ready, 1)

            pe.wait_ge(amat_landed, 16)
            phase("pool_v", XA, pool, first=hooks, ready=SPLITS["norm0"])
            phase("pool_gate", XA, first={3: lambda: pool(3)})
            pe.wait_ge(tp_evac, JOBS["pool_v"] + 4)
            total_gate(2, P)
            B0, A0, _ = PHASES["group"]
            pe.wait_ge(x_ready, SPLITS["pool_v"] + 4)
            group_job = stage_job("group")
            for j in range(CPB):
                if j % 2 == 0:
                    pe.wait_ge(acc_free, A0 + j // 2 - 1)
                chunk(B0, j, XB, KPC * j, A0 + j // 2, j % 2 == 0, j % 2 == 1)
                if j == 5:
                    pe.wait_ge(sum_taken, 1)
                if j in (5, 7):
                    group_job((j - 5) // 2)
            phase("pool_out", XA, first={-1: lambda: group_job(2), 3: lambda: group_job(3)}, ready=SPLITS["group"])

            pe.wait_ge(tp_evac, JOBS["group"] + 4)
            total(3, (6, 6), 0)
            total(4, (6, 6), KC)
            norm_job("norm1", 1, T2, 0)
            pe.wait_ge(scl_ready, 3)
            norm_job("norm1", 1, T2, 1)
            hooks = feed("norm1", 1, T2)
            hooks.pop(-1)
            idx_q_job, qk_job = stage_job("idx_q"), stage_job("qk")
            phase("idx_q", XB, idx_q_job, first=hooks, ready=SPLITS["norm1"])
            narrow("idx_kw", XB, 80, {3: lambda: idx_q_job(1)})

            def ki_job():
                pe.wait_ge(staged, STAGED["idx_kw"] + 1)
                pe.wait_ge(tp_evac, JOBS["idx_kw"])
                for t in range(NT):
                    ins = nc.tensor.transpose(ps[:, 6, t * P:(t + 1) * P], stage[:, t, 0:P], ident)
                ins.then_inc(tp_ready, 1)

            def index_scores(b):
                pe.wait_ge(qi_ready, b + 1)
                if not isinstance(b, int):
                    pe.wait_ge(relu_ready, b * 2)
                for i in range(2):
                    rows = slice(i * 64, i * 64 + 64)
                    for t, (a, z) in enumerate(((0, P), (P, CAUS))):
                        ins = mm(ps[:, 6 + i, a:z], qi_now[rows, t * P:(t + 1) * P], ki_t[rows, 0:z - a],
                                 start=True, stop=True)
                    ins.then_inc(sc_ready, 1)

            def first_scores():
                pe.wait_ge(tp_evac, JOBS["idx_kw"] + 2)
                index_scores(0)

            B0, A0, n = PHASES["qk"]
            blk(B0, A0, XB, True, {0: lambda: turn_back("idx_kw", 80, ps[:, 4], P), 4: ki_job, 6: first_scores})
            with pe.Fori(1, n) as b:
                blk(b + B0, b + A0, XB, True, {3: lambda: qk_job(b - 1), 5: lambda: index_scores(b)})
            phase("v", XB, first={3: lambda: qk_job(7)})
            pe.wait_ge(tp_evac, JOBS["qk"] + 8)
            pe.wait_ge(relu_ready, IDX_HEADS)
            total_gate(5, 1)
            phase("gate", XB)

            def attention(h0, e0, heads, name, q, k, v, ready, value, free, rows_of=1, width=HD):
                for i in range(heads + 3):
                    if i < heads:
                        h = h0 + i
                        if i >= 2:
                            pe.wait_ge(masked, h - 1)
                        for t, (a, z) in enumerate(((0, P), (P, CAUS))):
                            for r in range(rows_of):
                                ins = mm(ps[:, 4 + i % 2, a:z], q(i, r)[:, t * P:(t + 1) * P], k(i, r)[:, 0:z - a],
                                         start=r == 0, stop=r == rows_of - 1)
                        ins.then_inc(lg_ready, 1)
                    if 1 <= i <= heads:
                        h, b = h0 + i - 1, (i - 1) % 2
                        pe.wait_ge(ready, value + i)
                        if i >= 3:
                            pe.wait_ge(pt_copied, h - 1)
                        for dst, src in ((0, 0), (P, P), (2 * P, 2 * P)):
                            ins = nc.tensor.transpose(ps[:, 6 + b, dst:dst + P], probs[:, b, src:src + P], ident)
                        ins.then_inc(pt_ready, 1)
                    if name and i >= 6 and i % 4 == 2 and i < heads:
                        n = (i - 6) // 4
                        job(JOBS[name] + n, stage, staged, STAGED[name] + n + 1, bank=2)
                    if 2 <= i < heads + 2:
                        h, b = h0 + i - 2, (i - 2) % 2
                        pe.wait_ge(pt_copied, h + 1)
                        if i == 2:
                            pe.wait_ge(acc_free, free)
                        if i >= 4:
                            pe.wait_ge(o_done, h - 1)
                        mm(ps[:, b, 0:width], probs_t[:, b, 0:P], v(i - 2, 0), start=True, stop=True)
                        mm(ps[:, b, width:2 * width], probs_t[:, b, P:2 * P], v(i - 2, 0), start=True, stop=False)
                        mm(ps[:, b, width:2 * width], probs_t[:, b, 2 * P:CAUS], v(i - 2, 1), start=False, stop=True
                           ).then_inc(pv_ready, 1)

            pe.wait_ge(row_ready, 1)
            attention(0, 0, DSA_HEADS, "attn", lambda i, r: qk_t[:, i, :], lambda i, r: qk_t[:, DSA_HEADS + i, :],
                      lambda i, u: T2[:, u, i * HD:(i + 1) * HD], exp_ready, 0, PHASES["gate"][1] + 4)

            def rest(name, n):
                return {3: lambda: job(JOBS[name] + n, stage, staged, STAGED[name] + n + 1, bank=4)}

            pe.wait_ge(o_done, DSA_HEADS)
            norm2_job = stage_job("norm2")
            phase("attn_out", XA, norm2_job, first=rest("attn", 3), ready=SPLITS["attn"])

            a0 = PHASES["m_qk"][1]

            def m_qk_job(b):
                job(b + JOBS["m_qk"], stage, acc_free, b + (a0 + 1))

            phase("m_qk", XB, m_qk_job, first={3: lambda: norm2_job(3)}, ready=SPLITS["norm2"])
            narrow("m_if", XB, 8, {3: lambda: m_qk_job(3)})

            def cumulate():
                pe.wait_ge(g_in, 3)
                mm(ps[:, 6, 0:4], cum, gate_f[:, 0, :], start=True, stop=True)
                mm(ps[:, 6, 4:8], cum, gate_f[:, 1, :], start=True, stop=False)
                mm(ps[:, 6, 4:8], ones, gate_f[:, 0, :], start=False, stop=True).then_inc(g_mm, 1)

            def spread():
                pe.wait_ge(g_in, 4)
                for h in range(M_HEADS):
                    for t in range(NT):
                        at = h % 2 * S + t * P
                        ins = mm(ps[:, 4 + h // 2, at:at + P], ones, m_diag[:, t, h, :], start=True, stop=True)
                ins.then_inc(g_mm, 1)

            B0, A0, _ = PHASES["m_v"]
            blk(B0, A0, XB, True, {0: lambda: turn_back("m_if", 8, ps[:, 6], 8), 3: cumulate})
            blk(B0 + 1, A0 + 1, XB, True, {3: spread})
            phase("m_o", XB)
            pe.wait_ge(g_dve, 1)
            mq = feat(0)
            attention(DSA_HEADS, 0, M_HEADS, None, lambda i, r: mq[:, 2 * i + r, :], lambda i, r: mq[:, 8 + 2 * i + r, :],
                      lambda i, u: m_v[:, u, i * S:(i + 1) * S], masked, DSA_HEADS, PHASES["m_o"][1] + 2,
                      rows_of=2, width=S)

            def mlstm_job(n):
                return lambda: job(JOBS["mlstm"] + n, stage, staged, STAGED["mlstm"] + n + 1, bank=6)

            pe.wait_ge(o_done, DSA_HEADS + M_HEADS)
            aqk_job = stage_job("a_qk")
            phase("a_qk", XB, aqk_job, first={1: mlstm_job(0), 3: mlstm_job(1)})
            phase("a_v", XB, first={3: lambda: aqk_job(3)})
            pe.wait_ge(tp_evac, JOBS["a_qk"] + 4)
            aq = feat(2)
            attention(DSA_HEADS + M_HEADS, DSA_HEADS, MOBA_HEADS, "moba", lambda i, r: aq[:, i, :],
                      lambda i, r: aq[:, MOBA_HEADS + i, :], lambda i, u: a_v[:, u, i * HD:(i + 1) * HD],
                      exp_ready, DSA_HEADS, PHASES["a_v"][1] + 2)
            pe.wait_ge(o_done, DSA_HEADS + M_HEADS + MOBA_HEADS)
            phase("g_m", XB, first=rest("moba", 1))
            phase("g_a", XB)

            pe.wait_ge(x_ready, SPLITS["moba"] + 2)
            B0, A0, n = PHASES["branch"]
            branch_job = stage_job("branch")

            def branch(b, first=False):
                for half in range(2):
                    A = b * 2 + (A0 + half)
                    pe.wait_ge(acc_free, A - 1)
                    for j in range(4):
                        chunk(b + B0, 4 * half + j, XA, 8 * half + KPC * j, A, j == 0, j == 3)
                    if half == 0 and not first:
                        branch_job(b - 1)

            branch(0, first=True)
            with pe.Fori(1, n) as b:
                branch(b)
            phase("mix_out", XB, first={3: lambda: branch_job(3)}, ready=SPLITS["branch"])

            ffn_job = stage_job("ffn")
            X0 = SPLITS["ffn"]

            def up(e, B, A, after=None):
                for h in range(2):
                    if after == "norm" and h == 0:
                        blk(B, A, XA, True, feed("norm3", 3, T3), ready=SPLITS["norm3"])
                    else:
                        blk(B + h, A + h, XA, True,
                            {3: lambda: ffn_job(e * 2 + (h - 1))} if h == 1 or after == "up" else None)

            def dn(e, half, B, A, last=False):
                pe.wait_ge(x_ready, e * 2 + (X0 + 2))
                for q in range(4):
                    pe.wait_ge(acc_free, A + (q - 1))
                    for j in range(4):
                        chunk(B + q // 2, 4 * (q % 2) + j, XB, 8 * half + KPC * j, A + q, j == 0, j == 3)
                    if q == 0 and not last:
                        ffn_job(e * 2 + 3)

            up(0, FB, FA, after="norm")
            up(1, FB + 2, FA + 2, after="up")
            dn(0, 0, FB + 4, FA + 4)
            with pe.Fori(0, 3) as i:
                up(i * 2 + 2, i * 8 + (FB + 6), i * 12 + (FA + 8))
                dn(i * 2 + 1, 1, i * 8 + (FB + 8), i * 12 + (FA + 10))
                up(i * 2 + 3, i * 8 + (FB + 10), i * 12 + (FA + 14))
                dn(i * 2 + 2, 0, i * 8 + (FB + 12), i * 12 + (FA + 16))
            dn(7, 1, FB + 30, FA + 44, last=True)


_INS = [
    "x", "c", "positions", "norm_g", "mod_w", "mod_b", "pool_w_in", "pool_w_grp", "pool_scale", "pool_w_out",
    "attn_w_in", "attn_w_out", "final_g", "positions_2", "norm_mix_pre_2", "w_in_2", "conv_w_2", "conv_b_2",
    "i_bias_2", "f_bias_2", "mlstm_norm_2", "w_branch_m_2", "w_branch_a_2", "w_out_2", "norm_mix_post_2",
    "norm_ffn_pre_2", "w_up_2", "w_down_2", "norm_ffn_post_2",
]


def shape_constants():
    far = np.float32(FAR)
    con = np.zeros((P, C_ALL), np.float32)
    con[:, C_ID:C_ID + P] = np.eye(P)
    key, query = np.arange(P)[None, :], np.arange(P)[:, None]
    triangle = np.where(key <= query, np.float32(0), far)
    con[:, C_TRI:C_TRI + P] = triangle
    con[:, C_TRI + 2 * P:C_TRI + 3 * P] = triangle
    con[:, C_CUM:C_CUM + P] = (query <= key)
    con[:, C_ONE:C_ONE + P] = 1.0
    col = C_FRQ
    for theta, width, half in ((500000.0, 32, FRQ1), (500000.0, 16, FRQI), (10000.0, 128, FRQ2)):
        con[:, col:col + half] = theta ** (-np.arange(half) * 2.0 / width)
        col += half
    win = np.zeros((len(WINDOWS), S, S), np.float64)
    for g, w in enumerate(WINDOWS):
        for t in range(S):
            lo = max(t + 1 - w, 0)
            win[g, lo:t + 1, t] = 1.0 / (t + 1 - lo)
            win[g, t, t] -= 1.0
    win = win.astype(np.float32).reshape(len(WINDOWS), NT, P, S).transpose(2, 0, 1, 3)
    return con, np.ascontiguousarray(win)


def kernel(**inputs):
    import concourse.bacc as bacc
    from concourse.bass_utils import run_bass_kernel_spmd

    nc = bacc.Bacc("TRN2", target_bir_lowering=False, num_devices=1, dynamic_dma_scratch_size=1024)
    arrays, args = {}, {}
    for name in _INS:
        a = np.ascontiguousarray(inputs[name])
        arrays[f"in_{name}"] = a
        args[name] = nc.dram_tensor(f"in_{name}", a.shape, mybir.dt.from_np(a.dtype), kind="ExternalInput").ap()
    for name, a in zip(("consts", "windows"), shape_constants()):
        arrays[f"in_{name}"] = a
        args[name] = nc.dram_tensor(f"in_{name}", a.shape, F32, kind="ExternalInput").ap()
    args["gate_row"] = nc.dram_tensor("gate_row", (1, D), F32).ap()
    args["resid"] = nc.dram_tensor("resid", (2, S, D), F32).ap()
    args["out"] = nc.dram_tensor("out", (1, S, D), F32, kind="ExternalOutput").ap()
    build(nc, **args)
    r = run_bass_kernel_spmd(nc, [arrays], core_ids=[0])
    return r.results[0]["out"]
```
